# Optimizing a Trainium2 kernel written in Bass

```python
import math
import jax, jax.numpy as jnp
from jax import lax
import numpy as np

D_MODEL = 1024
BATCH = 1
SEQ = 512
DEPTH = 1

D_CONV = 512
CONV_K = 3
N_HEADS = 8
HEAD_DIM = 64
D_ATTN = N_HEADS * HEAD_DIM
N_IDX_HEADS = 8
IDX_DIM = 64
TOPK_MAX = 256
Q_BLOCK = 128
N_BUCKETS = 32
MAX_EXACT = 16
MAX_DISTANCE = 128
D_FF = -(-8 * D_MODEL // (3 * 256)) * 256
EPS = 1e-6

PROJ_SIZES = (
    D_CONV, D_CONV, D_CONV,
    D_ATTN, HEAD_DIM, HEAD_DIM,
    N_IDX_HEADS * IDX_DIM, IDX_DIM,
    N_IDX_HEADS,
    D_MODEL, D_MODEL,
)
N_PROJ = int(sum(PROJ_SIZES))
PROJ_SPLITS = [int(v) for v in np.cumsum(PROJ_SIZES)[:-1]]


def rms_norm(x, g):
    xf = x.astype(jnp.float32)
    y = xf * lax.rsqrt(jnp.mean(xf * xf, axis=-1, keepdims=True) + EPS)
    return (y * g.astype(jnp.float32)).astype(x.dtype)

def rel_bucket(dist):
    n = jnp.maximum(dist, 0)
    large = MAX_EXACT + (jnp.log(jnp.maximum(n, 1).astype(jnp.float32) / MAX_EXACT)
                         / math.log(MAX_DISTANCE / MAX_EXACT)
                         * (N_BUCKETS - MAX_EXACT)).astype(jnp.int32)
    large = jnp.minimum(large, N_BUCKETS - 1)
    return jnp.where(n < MAX_EXACT, n, large)

def short_conv_mixer(gate_b, gate_c, x_a, conv_w):
    u = gate_c * x_a
    rhs = conv_w[:, None, :].astype(u.dtype)
    y = lax.conv_general_dilated(u, rhs, window_strides=(1,), padding=[(CONV_K - 1, 0)],
                                 dimension_numbers=("NWC", "WIO", "NWC"),
                                 feature_group_count=D_CONV)
    return gate_b * y

def dsa_attention(q, k, v, iq, ik, iw, rel_bias):
    bsz, seq_len = q.shape[0], q.shape[1]
    k_top = min(TOPK_MAX, seq_len // 4)
    n_blk = seq_len // Q_BLOCK
    iw = iw * (N_IDX_HEADS ** -0.5 * IDX_DIM ** -0.5)
    s_pos = jnp.arange(seq_len, dtype=jnp.int32)
    t_blocks = s_pos.reshape(n_blk, Q_BLOCK)

    def to_blocks(a):
        return jnp.moveaxis(a.reshape(bsz, n_blk, Q_BLOCK, *a.shape[2:]), 1, 0)

    gather = jax.vmap(lambda arr, ind: arr[ind])

    def block_fn(args):
        q_b, iq_b, iw_b, t_b = args
        dots = jnp.einsum("bthd,bsd->bths", iq_b, ik)
        score = jnp.einsum("bth,bths->bts", iw_b, jax.nn.relu(dots)).astype(jnp.float32)
        causal = s_pos[None, :] <= t_b[:, None]
        score = jnp.where(causal[None], score, -jnp.inf)
        _, idx = lax.top_k(score, k_top)
        valid = idx <= t_b[None, :, None]
        k_sel = gather(k, idx)
        v_sel = gather(v, idx)
        logits = jnp.einsum("bthd,btkd->bhtk", q_b, k_sel).astype(jnp.float32) * (HEAD_DIM ** -0.5)
        bias = rel_bias[rel_bucket(t_b[None, :, None] - idx)]
        logits = logits + jnp.moveaxis(bias, -1, 1).astype(jnp.float32)
        logits = jnp.where(valid[:, None], logits, -jnp.inf)
        p = jax.nn.softmax(logits, axis=-1).astype(v.dtype)
        o = jnp.einsum("bhtk,btkd->bthd", p, v_sel)
        return o.reshape(bsz, Q_BLOCK, D_ATTN)

    out = lax.map(block_fn, (to_blocks(q), to_blocks(iq), to_blocks(iw), t_blocks))
    return jnp.moveaxis(out, 0, 1).reshape(bsz, seq_len, D_ATTN)

def first_inputs(seed: int = 0) -> dict:
    key = jax.random.key(seed)
    ks = jax.random.split(key, 16)
    f32 = jnp.float32
    nrm = lambda k, shape, scale: jax.random.normal(k, shape, f32) * scale
    return {
        "x": nrm(ks[0], (BATCH, SEQ, D_MODEL), 1.0),
        "g_mix": 1.0 + nrm(ks[1], (DEPTH, D_MODEL), 0.02),
        "w_in": nrm(ks[2], (DEPTH, D_MODEL, N_PROJ), D_MODEL ** -0.5),
        "b_gate": nrm(ks[3], (DEPTH, 2 * D_MODEL), 0.02),
        "conv_w": nrm(ks[4], (DEPTH, CONV_K, D_CONV), CONV_K ** -0.5),
        "w_branch_a": nrm(ks[5], (DEPTH, D_CONV, D_MODEL), D_CONV ** -0.5),
        "w_branch_b": nrm(ks[6], (DEPTH, D_ATTN, D_MODEL), D_ATTN ** -0.5),
        "w_out": nrm(ks[7], (DEPTH, D_MODEL, D_MODEL), D_MODEL ** -0.5),
        "rel_bias": nrm(ks[8], (N_BUCKETS, N_HEADS), 0.5),
        "g_ffn": 1.0 + nrm(ks[9], (DEPTH, D_MODEL), 0.02),
        "w_ffn_gate": nrm(ks[10], (DEPTH, D_MODEL, D_FF), D_MODEL ** -0.5),
        "w_ffn_up": nrm(ks[11], (DEPTH, D_MODEL, D_FF), D_MODEL ** -0.5),
        "w_ffn_down": nrm(ks[12], (DEPTH, D_FF, D_MODEL), D_FF ** -0.5),
        "g_final": 1.0 + nrm(ks[13], (D_MODEL,), 0.02),
    }

def first_block(x, g_mix, w_in, b_gate, conv_w, w_branch_a, w_branch_b, w_out, rel_bias,
              g_ffn, w_ffn_gate, w_ffn_up, w_ffn_down, g_final):
    bsz, seq_len, _ = x.shape
    for layer in range(DEPTH):
        h = rms_norm(x, g_mix[layer])
        proj = h @ w_in[layer]
        (c_b, c_c, c_x, q, k, v, iq, ik, iw, g_a, g_b) = jnp.split(proj, PROJ_SPLITS, axis=-1)
        y_a = short_conv_mixer(c_b, c_c, c_x, conv_w[layer]) @ w_branch_a[layer]
        attn = dsa_attention(q.reshape(bsz, seq_len, N_HEADS, HEAD_DIM), k, v,
                             iq.reshape(bsz, seq_len, N_IDX_HEADS, IDX_DIM), ik, iw, rel_bias)
        y_b = attn @ w_branch_b[layer]
        gates = jax.nn.sigmoid(jnp.concatenate([g_a, g_b], axis=-1) + b_gate[layer])
        merged = gates[..., :D_MODEL] * y_a + gates[..., D_MODEL:] * y_b
        x = x + merged @ w_out[layer]
        h2 = rms_norm(x, g_ffn[layer])
        x = x + (jax.nn.silu(h2 @ w_ffn_gate[layer]) * (h2 @ w_ffn_up[layer])) @ w_ffn_down[layer]
    return rms_norm(x, g_final)


QK_NOPE_DIM = 64
QK_ROPE_DIM = 32
V_HEAD_DIM = 64
Q_LORA_RANK = 384
KV_LORA_RANK = 256
ROPE_BASE = 10000.0
QK_DIM = QK_NOPE_DIM + QK_ROPE_DIM
ATTN_WIDTH = N_HEADS * V_HEAD_DIM
CONV_CHANNELS = 512
CONV_KERNEL = 31
N_GROUPS = 4
EXPERTS_PER_GROUP = 8
TOP_K_IN_GROUP = 2
D_EXPERT = 128
SPLIT_POINTS = tuple(int(v) for v in np.cumsum([Q_LORA_RANK, KV_LORA_RANK, QK_ROPE_DIM, 2 * CONV_CHANNELS]))
IN_COLS = Q_LORA_RANK + KV_LORA_RANK + QK_ROPE_DIM + 2 * CONV_CHANNELS + 2 * D_MODEL


def rmsnorm(x, g):
    xf = x.astype(jnp.float32)
    y = xf * lax.rsqrt(jnp.mean(xf * xf, axis=-1, keepdims=True) + EPS)
    return (y * g.astype(jnp.float32)).astype(x.dtype)

def layernorm(x, g, b):
    xf = x.astype(jnp.float32)
    mu = jnp.mean(xf, axis=-1, keepdims=True)
    var = jnp.mean(jnp.square(xf - mu), axis=-1, keepdims=True)
    y = (xf - mu) * lax.rsqrt(var + EPS)
    return (y * g.astype(jnp.float32) + b.astype(jnp.float32)).astype(x.dtype)

def rope_tables(positions):
    inv_freq = ROPE_BASE ** (-jnp.arange(0, QK_ROPE_DIM, 2, dtype=jnp.float32) / QK_ROPE_DIM)
    ang = positions.astype(jnp.float32)[..., None] * inv_freq
    return jnp.cos(ang), jnp.sin(ang)

def apply_rope(x, cos, sin):
    xf = x.astype(jnp.float32)
    x1, x2 = jnp.split(xf, 2, axis=-1)
    return jnp.concatenate([x1 * cos - x2 * sin, x2 * cos + x1 * sin], axis=-1).astype(x.dtype)

def causal_block_attention(q, k, v, positions):
    B, H, S, _ = q.shape
    nb = S // Q_BLOCK
    scale = QK_DIM ** -0.5
    qb = q.reshape(B, H, nb, Q_BLOCK, QK_DIM).transpose(2, 0, 1, 3, 4)
    pb = positions.reshape(B, nb, Q_BLOCK).transpose(1, 0, 2)
    neg = jnp.finfo(jnp.float32).min

    def one_block(args):
        q_blk, p_blk = args
        s = jnp.einsum('bhqd,bhkd->bhqk', q_blk, k, preferred_element_type=jnp.float32) * scale
        mask = positions[:, None, None, :] <= p_blk[:, None, :, None]
        p = jax.nn.softmax(jnp.where(mask, s, neg), axis=-1)
        return jnp.einsum('bhqk,bhkd->bhqd', p.astype(v.dtype), v)

    out = lax.map(one_block, (qb, pb))
    return out.transpose(1, 0, 3, 2, 4).reshape(B, S, H * V_HEAD_DIM)

def causal_depthwise_conv(u, w, b):
    y = lax.conv_general_dilated(
        u, w[:, None, :].astype(u.dtype), window_strides=(1,),
        padding=[(CONV_KERNEL - 1, 0)], dimension_numbers=('NWC', 'WIO', 'NWC'),
        feature_group_count=u.shape[-1])
    return y + b

def hierarchical_moe(h, rg_w, rg_b, re_w, re_b, e_gate, e_up, e_down):
    B, S, D = h.shape
    t = h.reshape(-1, D)
    g_prob = jax.nn.softmax((t @ rg_w + rg_b).astype(jnp.float32), axis=-1)
    g_val, g_idx = lax.top_k(g_prob, 1)
    e_logits = (t @ re_w + re_b).astype(jnp.float32).reshape(-1, N_GROUPS, EXPERTS_PER_GROUP)
    e_sel = jnp.take_along_axis(e_logits, g_idx[:, :, None], axis=1)[:, 0]
    e_val, e_idx = lax.top_k(jax.nn.softmax(e_sel, axis=-1), TOP_K_IN_GROUP)
    e_val = e_val / jnp.sum(e_val, axis=-1, keepdims=True)
    w_group = jnp.sum(jax.nn.one_hot(e_idx, EXPERTS_PER_GROUP, dtype=jnp.float32) * e_val[..., None], axis=1)
    combine = (jax.nn.one_hot(g_idx[:, 0], N_GROUPS, dtype=jnp.float32)[:, :, None]
               * (g_val * w_group)[:, None, :]).astype(h.dtype)
    out = jnp.zeros_like(t)
    for gi in range(N_GROUPS):
        a = jnp.einsum('td,edf->tef', t, e_gate[gi])
        u = jnp.einsum('td,edf->tef', t, e_up[gi])
        hid = jax.nn.silu(a) * u * combine[:, gi, :, None]
        out = out + jnp.einsum('tef,efd->td', hid, e_down[gi])
    return out.reshape(B, S, D)

def second_inputs(seed: int = 0) -> dict:
    key = jax.random.key(seed)
    ks = iter(jax.random.split(key, 32))
    L, D = DEPTH, D_MODEL

    def nrm(shape, scale):
        return jax.random.normal(next(ks), shape, jnp.float32) * scale

    x = nrm((BATCH, SEQ, D), 1.0)
    c = nrm((BATCH, D), 1.0)
    offsets = jax.random.randint(next(ks), (BATCH, 1), 0, 1024, dtype=jnp.int32)
    positions = offsets + jnp.arange(SEQ, dtype=jnp.int32)[None, :]
    G, E, F = N_GROUPS, EXPERTS_PER_GROUP, D_EXPERT
    return {
        "x": x, "c": c, "positions": positions,
        "ada_w": nrm((L, D, 6 * D), 0.5 * D ** -0.5),
        "ada_b": nrm((L, 6 * D), 0.02),
        "norm1_g": 1.0 + nrm((L, D), 0.02),
        "norm2_g": 1.0 + nrm((L, D), 0.02),
        "w_in": nrm((L, D, IN_COLS), D ** -0.5),
        "q_norm_g": 1.0 + nrm((L, Q_LORA_RANK), 0.02),
        "w_uq": nrm((L, Q_LORA_RANK, N_HEADS * QK_DIM), Q_LORA_RANK ** -0.5),
        "kv_norm_g": 1.0 + nrm((L, KV_LORA_RANK), 0.02),
        "w_ukv": nrm((L, KV_LORA_RANK, N_HEADS * (QK_NOPE_DIM + V_HEAD_DIM)), KV_LORA_RANK ** -0.5),
        "w_o_attn": nrm((L, ATTN_WIDTH, D), ATTN_WIDTH ** -0.5),
        "conv_w": nrm((L, CONV_KERNEL, CONV_CHANNELS), CONV_KERNEL ** -0.5),
        "conv_b": nrm((L, CONV_CHANNELS), 0.02),
        "conv_ln_g": 1.0 + nrm((L, CONV_CHANNELS), 0.02),
        "conv_ln_b": nrm((L, CONV_CHANNELS), 0.02),
        "w_conv_out": nrm((L, CONV_CHANNELS, D), CONV_CHANNELS ** -0.5),
        "w_out": nrm((L, D, D), D ** -0.5),
        "router_group_w": nrm((L, D, G), D ** -0.5),
        "router_group_b": nrm((L, G), 0.01),
        "router_expert_w": nrm((L, D, G * E), D ** -0.5),
        "router_expert_b": nrm((L, G * E), 0.01),
        "expert_w_gate": nrm((L, G, E, D, F), D ** -0.5),
        "expert_w_up": nrm((L, G, E, D, F), D ** -0.5),
        "expert_w_down": nrm((L, G, E, F, D), F ** -0.5),
        "final_norm_g": 1.0 + nrm((D,), 0.02),
    }

def second_block(x, c, positions, ada_w, ada_b, norm1_g, norm2_g, w_in, q_norm_g, w_uq,
              kv_norm_g, w_ukv, w_o_attn, conv_w, conv_b, conv_ln_g, conv_ln_b,
              w_conv_out, w_out, router_group_w, router_group_b, router_expert_w,
              router_expert_b, expert_w_gate, expert_w_up, expert_w_down, final_norm_g):
    B, S, D = x.shape
    cos, sin = rope_tables(positions)
    c_act = jax.nn.silu(c)
    for l in range(DEPTH):
        ada = c_act @ ada_w[l] + ada_b[l]
        sh1, sc1, gt1, sh2, sc2, gt2 = [a[:, None, :] for a in jnp.split(ada, 6, axis=-1)]

        h = rmsnorm(x, norm1_g[l]) * (1.0 + sc1) + sh1
        z = h @ w_in[l]
        q_lat, kv_lat, k_rope, conv_in, gate_logits = jnp.split(z, SPLIT_POINTS, axis=-1)

        q = (rmsnorm(q_lat, q_norm_g[l]) @ w_uq[l]).reshape(B, S, N_HEADS, QK_DIM)
        q_nope, q_pe = jnp.split(q, [QK_NOPE_DIM], axis=-1)
        q_pe = apply_rope(q_pe, cos[:, :, None, :], sin[:, :, None, :])
        kv = (rmsnorm(kv_lat, kv_norm_g[l]) @ w_ukv[l]).reshape(B, S, N_HEADS, QK_NOPE_DIM + V_HEAD_DIM)
        k_nope, v = jnp.split(kv, [QK_NOPE_DIM], axis=-1)
        k_pe = jnp.broadcast_to(apply_rope(k_rope, cos, sin)[:, :, None, :], (B, S, N_HEADS, QK_ROPE_DIM))
        qh = jnp.concatenate([q_nope, q_pe], axis=-1).transpose(0, 2, 1, 3)
        kh = jnp.concatenate([k_nope, k_pe], axis=-1).transpose(0, 2, 1, 3)
        attn = causal_block_attention(qh, kh, v.transpose(0, 2, 1, 3), positions)
        y_attn = attn @ w_o_attn[l]

        glu_a, glu_b = jnp.split(conv_in, 2, axis=-1)
        u = glu_a * jax.nn.sigmoid(glu_b)
        u = causal_depthwise_conv(u, conv_w[l], conv_b[l])
        u = jax.nn.silu(layernorm(u, conv_ln_g[l], conv_ln_b[l]))
        y_conv = u @ w_conv_out[l]

        g_attn, g_conv = jnp.split(jax.nn.sigmoid(gate_logits), 2, axis=-1)
        y = (g_attn * y_attn + g_conv * y_conv) @ w_out[l]
        x = x + gt1 * y

        h = rmsnorm(x, norm2_g[l]) * (1.0 + sc2) + sh2
        x = x + gt2 * hierarchical_moe(h, router_group_w[l], router_group_b[l], router_expert_w[l],
                                       router_expert_b[l], expert_w_gate[l], expert_w_up[l],
                                       expert_w_down[l])
    return rmsnorm(x, final_norm_g)


def setup_inputs(seed=0):
    out = dict(first_inputs(seed))
    for name, value in second_inputs(seed + 1).items():
        if name != "x":
            out[name + "_2"] = value
    return out


def reference(
    x, g_mix, w_in, b_gate, conv_w, w_branch_a, w_branch_b, w_out, rel_bias, g_ffn, w_ffn_gate,
    w_ffn_up, w_ffn_down, g_final, c_2, positions_2, ada_w_2, ada_b_2, norm1_g_2, norm2_g_2,
    w_in_2, q_norm_g_2, w_uq_2, kv_norm_g_2, w_ukv_2, w_o_attn_2, conv_w_2, conv_b_2,
    conv_ln_g_2, conv_ln_b_2, w_conv_out_2, w_out_2, router_group_w_2, router_group_b_2,
    router_expert_w_2, router_expert_b_2, expert_w_gate_2, expert_w_up_2, expert_w_down_2,
    final_norm_g_2,
):
    x = first_block(
        x, g_mix, w_in, b_gate, conv_w, w_branch_a, w_branch_b, w_out, rel_bias, g_ffn,
        w_ffn_gate, w_ffn_up, w_ffn_down, g_final,
    )
    return second_block(
        x, c_2, positions_2, ada_w_2, ada_b_2, norm1_g_2, norm2_g_2, w_in_2, q_norm_g_2, w_uq_2,
        kv_norm_g_2, w_ukv_2, w_o_attn_2, conv_w_2, conv_b_2, conv_ln_g_2, conv_ln_b_2,
        w_conv_out_2, w_out_2, router_group_w_2, router_group_b_2, router_expert_w_2,
        router_expert_b_2, expert_w_gate_2, expert_w_up_2, expert_w_down_2, final_norm_g_2,
    )


_drawn_inputs = setup_inputs


def setup_inputs(seed=0):
    import zlib

    import numpy as np

    out = dict(_drawn_inputs(seed))
    spreads = {}
    factors = {'b_gate': 8.0,
     'g_ffn': 3.578,
     'ada_b_2': 3.328,
     'norm1_g_2': 8.0,
     'norm2_g_2': 5.184,
     'q_norm_g_2': 8.0,
     'kv_norm_g_2': 8.0,
     'conv_b_2': 8.0,
     'conv_ln_g_2': 8.0,
     'conv_ln_b_2': 8.0,
     'router_group_b_2': 8.0,
     'router_expert_b_2': 7.902,
     'final_norm_g_2': 2.764}
    for name, (base, spread) in spreads.items():
        noise = np.random.default_rng([zlib.crc32(name.encode()), seed]).standard_normal(out[name].shape)
        drawn = base * np.exp(spread * noise) if base else spread * noise
        out[name] = __import__('jax').numpy.asarray(drawn.astype(out[name].dtype))
    for name, factor in factors.items():
        out[name] = (out[name] * factor).astype(out[name].dtype)
    return out
```

```python
from contextlib import ExitStack

import numpy as np

import concourse.bass as bass
from concourse import mybir

F32 = mybir.dt.float32
F32R = mybir.dt.float32r
I32 = mybir.dt.int32
ALU = mybir.AluOpType
ACT = mybir.ActivationFunctionType
AX = mybir.AxisListType

P = 128
D = 1024
SEQ = 512
NB = SEQ // P
DC = D // P
H = 8
HD = 64
K_TOP = min(256, SEQ // 4)
D_FF = 2816
FC = D_FF // P
FH = FC // 2
EPS = 1e-6
N_BUCKETS, MAX_EXACT, MAX_DISTANCE = 32, 16, 128
Q_RANK, KV_RANK, ROPE = 384, 256, 32
QC, KC = Q_RANK // P, KV_RANK // P
QK_DIM = HD + ROPE
TAPS = 31
CC = 512 // P
G, E = 4, 8
NEG = -1e30
FILL = -3.0e38
TAKEN = -3.3e38
SLAB = 2048
W = 2
GELEM = 640

SLABS = (
    [("kv_ikw", DC, 256)] + [("iq", DC, 256)] * 2 + [("q", DC, 256)] * 2
    + [("conv_c", DC, 256)] * 2 + [("conv_x", DC, 256)] * 2 + [("conv_b", DC, 256)] * 2
    + [("branch_a", CC, 512)] * 2 + [("gate_a", DC, 256)] * 4 + [("gate_b", DC, 256)] * 4
    + [("branch_b", CC, 512)] * 2 + [("w_out", DC, 256)] * 4
    + ([("ffn_up", DC, 256)] * FH + [("ffn_down", FH, 128)] * DC) * 2
    + [("latents", DC, 256)] * 3 + [("glu_b", DC, 256)] * 2 + [("glu_a", DC, 256)] * 2
    + [("w_uq", QC, 384)] * 2 + [("w_ukv", KC, 1024)] + [("gate_conv", DC, 256)] * 4
    + [("o_attn", CC, 256), ("gate_attn", DC, 256)] * 4 + [("conv_out", CC, 512)] * 2
    + [("w_out_2", DC, 256)] * 4 + ([("moe_up", DC, 256)] * E + [("moe_down", E, 256)] * 4) * G
)
FIRST = {}
for _n, (_name, _, _) in enumerate(SLABS):
    FIRST.setdefault(_name, _n)
NS = len(SLABS)
ADA_SLABS = 6 * D // 256
FFN2 = FIRST["ffn_up"] + FH + DC

TILE, JOB = {}, {}


def _number(table, names):
    n = 0
    for name, count in names:
        table[name] = n
        n += count


_number(TILE, [
    ("kv_ikw", 2), ("iq", 4), ("q", 4), ("conv_c", 4), ("conv_x", 4), ("conv_b", 4), ("branch_a", 8),
    ("gate_a", 8), ("gate_b", 8), ("attn_1", 2 * NB), ("branch_b", 8), ("w_out", 8),
    ("ffn_up_0", 2 * FH), ("ffn_down_0", DC), ("ffn_up_1", 2 * FH), ("ffn_down_1", DC),
    ("latents", 6), ("glu_b", 4), ("glu_a", 4), ("w_uq", 6), ("w_ukv", 8), ("gate_conv", 8),
    ("attn_2", 2 * NB), ("o_and_gate", 16), ("conv_out", 8), ("w_out_2", 8), ("moe", 24 * G)])
_number(JOB, [
    ("norm_1", 1), ("strip", 2), ("v_rows", 1), ("iw_rows", 1), ("dots", (NB - 1) * H), ("bias", H),
    ("attn_1", 2 * NB * H), ("norm_2", 1), ("norm_x", 1), ("norm_3", 1), ("norm_q", 1), ("norm_kv", 1),
    ("attn_2", 2 * NB * H), ("ln_mean", 1), ("ln_var", 1), ("norm_4", 1), ("router", 1),
    ("combine", 1), ("norm_out", 1)])
SPLIT = {}
_number(SPLIT, [
    ("h1", DC), ("conv_1", CC), ("merged_1", DC), ("h2", DC), ("ffn_0", FH), ("ffn_1", FH),
    ("h3", DC), ("q_lat", QC), ("kv_lat", KC), ("conv_2", CC), ("merged_2", DC),
    ("h4", DC), ("moe", G * E)])
GATE = {}
_number(GATE, [("dots", (NB - 1) * H), ("gate_a", 8), ("ffn_0", FH), ("ffn_1", FH), ("gate_attn", 8), ("moe", G * E)])

COLUMNS = {}
_number(COLUMNS, [
    ("g_mix", DC), ("b_gate", 2 * DC), ("conv_w", 3 * CC), ("g_ffn", DC), ("g_final", DC), ("c", DC),
    ("ada_b", 6 * DC), ("norm1_g", DC), ("norm2_g", DC), ("q_norm_g", QC), ("kv_norm_g", KC),
    ("conv_w_2", TAPS * CC), ("conv_b", CC), ("conv_ln_g", CC), ("conv_ln_b", CC), ("final_norm_g", DC),
    ("end", 0)])
CONST = {}
_number(CONST, [("ident", P), ("flip", P), ("ones", P), ("after", P), ("ramp", E), ("inv_freq", 1),
                ("rope_sign", 1), ("end", 0)])


def attn_jobs(r, kind):
    if kind == "logits":
        return r if r < 2 else 2 * r - 1
    return 2 * r + 2 if r < NB * H - 2 else r + NB * H


SQUARE = {}
_number(SQUARE, [("norm_1", DC), ("norm_2", DC), ("norm_x", DC), ("norm_3", DC), ("norm_q", QC), ("norm_kv", KC),
                 ("ln_var", CC), ("norm_4", DC), ("norm_out", DC)])
TILES_OF = {"kv_ikw": 2, "branch_a": 4, "branch_b": 4, "conv_out": 4, "ffn_down": 1, "w_uq": 3, "w_ukv": 8}
TILE_END = []
_t = 0
for _n, (_name, _, _) in enumerate(SLABS):
    if _n in (FIRST["branch_b"], FIRST["o_attn"]):
        _t += 2 * NB
    _t += TILES_OF.get(_name, 2)
    TILE_END.append(_t)


def build(nc, a, out):
    ctx = ExitStack()
    with ctx:
        def sem(name):
            return ctx.enter_context(nc.semaphore(name))

        def sbuf(name, shape, dt=F32, stack=ctx):
            return stack.enter_context(nc.sbuf_tensor(name, shape, dt))

        raw = sbuf("raw", [P, W, SLAB])
        whi = sbuf("whi", [P, W, SLAB], F32R)
        wlo = sbuf("wlo", [P, W, SLAB], F32R)
        x = sbuf("x", [P, DC, SEQ])
        tmp = sbuf("tmp", [P, 2, SEQ])
        square = sbuf("square", [P, 2, SEQ])
        rstd = sbuf("rstd", [P, SEQ])
        gate = sbuf("gate", [P, 2, SEQ])
        cst = sbuf("cst", [P, CONST["end"]])
        col = sbuf("col", [P, COLUMNS["end"]])
        c_act = sbuf("c_act", [P, DC])
        ada = sbuf("ada", [P, 6 * DC])
        mod = sbuf("mod", [P, 2, DC])
        h_hi = sbuf("h_hi", [P, DC, SEQ], F32R)
        h_lo = sbuf("h_lo", [P, DC, SEQ], F32R)
        stats = sbuf("stats", [P, 160])
        sums = stats[:, 0:NB * H].rearrange("p (b h) -> p b h", h=H)
        inv_sums = stats[:, 32:32 + NB * H].rearrange("p (b h) -> p b h", h=H)
        neg_max = stats[:, 64:66]
        top8 = stats[:, 72:80]
        iw_rows = stats[:, 80:80 + NB * H].rearrange("p (b h) -> p b h", h=H)
        pos_col = stats[:, 112:112 + NB]
        pos_col_raw = stats[:, 120:120 + NB].bitcast(I32)

        def overlay(*views):
            made, size = {}, 0
            for view in views:
                with ExitStack() as s:
                    n = 0
                    for name, shape, dt in view:
                        made[name] = sbuf(name, shape, dt, s)
                        n += 4 * int(np.prod(shape[1:])) + 32
                    size = max(size, n)
            return made, size

        memory = {}

        def place(name, *views):
            made, size = overlay(*views)
            memory.update(made)
            ctx.enter_context(nc.sbuf_tensor(name, [P, size // 4], F32))

        place("place_a",
              [("onehot", [N_BUCKETS, GELEM], F32), ("rel", [N_BUCKETS, H], F32), ("strip", [H, GELEM], F32)],
              [("conv_in", [P, CC, SEQ + 2], F32), ("conv_mid", [P, 2, SEQ], F32)],
              [("strip_t", [P, H, SEQ], F32)],
              [("ada_raw", [P, 2, SLAB], F32)],
              [("rope", [P, 5, SEQ], F32)],
              [("gate_conv", [P, DC, SEQ], F32)])
        stages = []

        def stage(*views):
            stages.append(overlay(*views))
            memory.update(stages[-1][0])

        base_1 = ExitStack()
        made, size = overlay([("iq_t", [P, CC, SEQ], F32), ("score", [P, 1152], F32), ("work", [P, 1152], F32)],
                             [("bias", [P, H, SEQ], F32)])
        memory.update(made)
        base_1.enter_context(nc.sbuf_tensor("place_1", [P, size // 4], F32))
        stage([("ik_t", [P, SEQ], F32), ("q_t", [P, CC, SEQ], F32), ("k_t", [P, SEQ], F32), ("v_t", [P, SEQ], F32),
               ("v_rows_1", [P, NB, HD], F32), ("mask_1", [P, 1280], F32), ("y1", [P, DC, SEQ], F32),
               ("prob_t1", [P, 2, SEQ], F32), ("a_hi1", [P, CC, SEQ], F32R), ("a_lo1", [P, CC, SEQ], F32R)])
        base_1.close()
        stage([("f_hi", [P, FH, SEQ], F32R), ("f_lo", [P, FH, SEQ], F32R)])
        base_3 = ExitStack()
        memory["q_h"] = sbuf("q_h", [P, H, SEQ], F32, base_3)
        made, size = overlay([("k_h", [P, H, SEQ], F32)],
                             [("c_hi", [P, CC, SEQ], F32R), ("c_lo", [P, CC, SEQ], F32R)])
        memory.update(made)
        base_3.enter_context(nc.sbuf_tensor("place_3", [P, size // 4], F32))
        made, size = overlay([("l_hi", [P, QC + KC, SEQ], F32R), ("l_lo", [P, QC + KC, SEQ], F32R)],
                             [("o_hi", [P, CC, SEQ], F32R), ("o_lo", [P, CC, SEQ], F32R),
                              ("prob_t2", [P, 2, SEQ], F32)])
        memory.update(made)
        base_3.enter_context(nc.sbuf_tensor("place_3b", [P, size // 4], F32))
        stage([("v_rows_2", [P, NB, H * HD], F32), ("pos_row", [P, SEQ], F32),
               ("u", [P, CC + 1, SEQ + TAPS - 1], F32)])
        base_3.close()
        stage([("e_hi", [P, E, SEQ], F32R), ("e_lo", [P, E, SEQ], F32R), ("comb", [P, 2, SEQ], F32),
               ("comb_t", [G * E, SEQ], F32), ("router_w", [P, DC, G + G * E], F32),
               ("router_b", [P, G + G * E], F32), ("rt", [P, 14, NB, G * E], F32)])
        m = memory
        iq_t, score, work, bias = m["iq_t"], m["score"], m["work"], m["bias"]
        ik_t, q_t, k_t, v_t, v_rows_1 = m["ik_t"], m["q_t"], m["k_t"], m["v_t"], m["v_rows_1"]
        mask_1, y1, prob_t1, a_hi1, a_lo1 = m["mask_1"], m["y1"], m["prob_t1"], m["a_hi1"], m["a_lo1"]
        conv_in, conv_mid, strip_t = m["conv_in"], m["conv_mid"], m["strip_t"]
        ada_raw, gate_conv, f_hi, f_lo = m["ada_raw"], m["gate_conv"], m["f_hi"], m["f_lo"]
        q_h, k_h, c_hi, c_lo = m["q_h"], m["k_h"], m["c_hi"], m["c_lo"]
        l_hi, l_lo, o_hi, o_lo, prob_t2 = m["l_hi"], m["l_lo"], m["o_hi"], m["o_lo"], m["prob_t2"]
        v_rows_2, pos_row, u = m["v_rows_2"], m["pos_row"], m["u"]
        e_hi, e_lo, comb, comb_t = m["e_hi"], m["e_lo"], m["comb"], m["comb_t"]
        router_w, router_b, rt = m["router_w"], m["router_b"], m["rt"]
        rope_cos, rope_sin, pos_raw, turn, angle = (m["rope"][:, n, :] for n in range(5))

        bank = [ctx.enter_context(nc.psum_tensor(f"bank{b}", [P, 512], F32)) for b in range(8)]
        strip_dram = nc.dram_tensor("strip_dram", [H, GELEM], F32)
        comb_dram = nc.dram_tensor("comb_dram", [G * E, SEQ], F32)

        def const(name, width=1):
            return cst[:, CONST[name]:CONST[name] + width]

        def column(name, n=0, width=1):
            return col[:, COLUMNS[name] + n:COLUMNS[name] + n + width]

        ident, flip, ones = const("ident", P), const("flip", P), const("ones", P)

        cst_loaded, col_loaded, rel_loaded = sem("cst_loaded"), sem("col_loaded"), sem("rel_loaded")
        x_loaded = [sem(f"x_loaded{n}") for n in range(2)]
        x_again = [sem(f"x_again{n}") for n in range(2)]
        slab_full = [sem(f"slab_full{w}") for w in range(W)]
        hi_done, lo_done = sem("hi_done"), sem("lo_done")
        tile_done = sem("tile_done")
        bank_free = [sem(f"bank_free{b}") for b in range(8)]
        ada_full = [sem(f"ada_full{w}") for w in range(2)]
        ada_done, ada_taken = sem("ada_done"), sem("ada_taken")
        c_ready = sem("c_ready")
        squared, summed = sem("squared"), sem("summed")
        var_ready, rstd_ready = sem("var_ready"), sem("rstd_ready")
        split_done = sem("split_done")
        strip_sum, strip_stored, strip_turned = sem("strip_sum"), sem("strip_stored"), sem("strip_turned")
        bias_sum = sem("bias_sum")
        turned = sem("turned")
        dots_done, dots_used = sem("dots_done"), sem("dots_used")
        gate_used = sem("gate_used")
        logits_done, probs_ready, probs_turned, pv_done = (
            sem("logits_done"), sem("probs_ready"), sem("probs_turned"), sem("pv_done"))
        pos_loaded, angles_ready, rope_ready = sem("pos_loaded"), sem("angles_ready"), sem("rope_ready")
        heads_ready = sem("heads_ready")
        pads_ready = sem("pads_ready")
        conv_done, mean_done, scaled, silu_done = (
            sem("conv_done"), sem("mean_done"), sem("scaled"), sem("silu_done"))
        router_loaded, h4_ready, routed, shift_ready, exp_ready = (
            sem("router_loaded"), sem("h4_ready"), sem("routed"), sem("shift_ready"), sem("exp_ready"))
        router_done, weights_ready, weights_turned, comb_stored = (
            sem("router_done"), sem("weights_ready"), sem("weights_turned"), sem("comb_stored"))
        comb_full, comb_used = [sem(f"comb_full{w}") for w in range(2)], sem("comb_used")
        out_ready, stored = sem("out_ready"), sem("stored")
        step = sem("step")

        def width(n):
            return SLABS[n][1] * SLABS[n][2]

        def parts(n):
            kc, c = SLABS[n][1:]
            return [t[:, n % W, 0:kc * c].rearrange("p (k c) -> p k c", c=c) for t in (whi, wlo)]

        def runs(eng, n0, count, body, size=2):
            whole = count // size
            if whole >= 2:
                with eng.Fori(0, whole) as i:
                    for k in range(size):
                        body(n0 + k, i, size)
            else:
                whole = 0
            for n in range(n0 + whole * size, n0 + count):
                body(n, 0, 0)

        def tile_is_done(eng, t, i=0, per=0):
            eng.wait_ge(tile_done, t + 1 + i * per)

        def tile_is_taken(eng, t, i=0, per=0):
            eng.wait_ge(bank_free[t % 4], t // 4 + 1 + i * (per // 4))

        def job_is_taken(eng, j):
            eng.wait_ge(bank_free[4 + j % 4], j // 4 + 1)

        def head_is_multiplied(eng, base_t, first, r):
            if r % H == H - 1:
                tile_is_done(eng, base_t + 2 * (r // H))
            else:
                eng.wait_ge(pv_done, first * (H - 1) // H + (H - 1) * (r // H) + r % H + 1)

        block = ctx.enter_context(nc.Block())

        @block.sync
        def _(sp):
            def load_slab(n, i=0, per=0):
                if n >= W:
                    sp.wait_ge(lo_done, n - W + 1 + i * per)
                sp.dma_start(raw[:, n % W, 0:width(n)], a["wpack"][n + i * per][:, 0:width(n)]) \
                    .then_inc(slab_full[n % W], 16)

            def load_ada(s, i=0, per=0):
                if s >= 2:
                    sp.wait_ge(ada_done, s - 1 + i * per)
                sp.dma_start(ada_raw[:, s % 2, :], a["ada_pack"][s + i * per]).then_inc(ada_full[s % 2], 16)

            x_dram = a["x_t"].rearrange("(c p) t -> p c t", p=P)
            out_dram = out.rearrange("(c p) t -> p c t", p=P)
            sp.dma_start(x[:, 0:DC // 2, :], x_dram[:, 0:DC // 2, :]).then_inc(x_loaded[0], 16)
            sp.dma_start(cst[:], a["const"]).then_inc(cst_loaded, 16)
            sp.dma_start(x[:, DC // 2:, :], x_dram[:, DC // 2:, :]).then_inc(x_loaded[1], 16)
            sp.dma_start(col[:], a["columns"]).then_inc(col_loaded, 16)
            load_slab(0)
            load_slab(1)
            sp.dma_start(m["onehot"][:], a["onehot"]).then_inc(rel_loaded, 16)
            sp.dma_start(m["rel"][:], a["rel_bias"]).then_inc(rel_loaded, 16)
            for j in range(2):
                job_is_taken(sp, JOB["strip"] + j)
            sp.dma_start(strip_dram.ap(), m["strip"][:]).then_inc(strip_stored, 16)
            first_a = FIRST["branch_a"]
            runs(sp, 2, first_a - 2, load_slab)
            sp.wait_ge(strip_stored, 16)
            sp.wait_ge(split_done, SPLIT["conv_1"] + CC)
            sp.dma_start(strip_t[:], bass.AP(tensor=strip_dram, offset=0, ap=[[1, P], [GELEM, H], [1, SEQ]])) \
                .then_inc(strip_turned, 16)
            runs(sp, first_a, FIRST["w_out"] - first_a, load_slab)
            for half in range(2):
                for c in range(half * DC // 2, (half + 1) * DC // 2):
                    tile_is_taken(sp, TILE["branch_b"] + c)
                cs = slice(half * DC // 2, (half + 1) * DC // 2)
                sp.dma_start(x[:, cs, :], x_dram[:, cs, :]).then_inc(x_again[half], 16)
                load_slab(FIRST["w_out"] + 2 * half)
                load_slab(FIRST["w_out"] + 2 * half + 1)

            for half in range(2):
                n0, s0 = FIRST["ffn_up"] + half * (FH + DC), half * FH

                def up(n, i=0, per=0, n0=n0, s0=s0):
                    load_slab(n, i, per)
                    load_ada(s0 + n - n0, i, per)

                if half == 0:
                    sp.wait_ge(bias_sum, H)
                up(n0)
                up(n0 + 1)
                runs(sp, n0 + 2, FH - 2, up)
                if half == 0:
                    runs(sp, n0 + FH, DC, load_slab)
            down = FFN2 + FH
            for n in range(down, down + DC):
                load_slab(n)
                if n < down + ADA_SLABS - FC:
                    load_ada(FC + n - down)
            load_slab(FIRST["latents"])
            load_slab(FIRST["latents"] + 1)
            sp.wait_ge(ada_done, ADA_SLABS)
            sp.dma_start(pos_raw.bitcast(I32), a["positions_2"].to_broadcast([P, SEQ])).then_inc(pos_loaded, 16)
            sp.dma_start(pos_col_raw, a["positions_2"].rearrange("o (b p) -> p (o b)", p=P),
                         allow_slow_non_contiguous=True).then_inc(pos_loaded, 16)
            for n in range(FIRST["latents"] + 2, FIRST["moe_up"]):
                load_slab(n)
            tile_is_done(sp, TILE["conv_out"] + DC - 1)
            sp.dma_start(router_w[:], a["router_w"]).then_inc(router_loaded, 16)
            sp.dma_start(router_b[:], a["router_b"].to_broadcast([P, G + G * E])).then_inc(router_loaded, 16)
            n0 = FIRST["moe_up"]
            load_slab(n0)
            load_slab(n0 + 1)
            job_is_taken(sp, JOB["combine"])
            sp.dma_start(comb_dram.ap(), comb_t[:]).then_inc(comb_stored, 16)
            sp.wait_ge(comb_stored, 16)

            def moe_group(i, first):
                for e in range(E):
                    if not (first and e < 2):
                        load_slab(n0 + e, i, E + 4)
                        sp.wait_ge(comb_used, e - 1 + i * E)
                    row = comb_dram.ap()[e:e + 1, :] if first else comb_dram.ap()[bass.ds(e + i * E, 1), :]
                    sp.dma_start(comb[:, e % 2, :], row.to_broadcast([P, SEQ])).then_inc(comb_full[e % 2], 16)
                for d in range(4):
                    load_slab(n0 + E + d, i, E + 4)

            moe_group(0, True)
            with sp.Fori(1, G) as i:
                moe_group(i, False)
            for c in range(DC):
                sp.wait_ge(out_ready, c + 1)
                sp.dma_start(out_dram[:, c, :], x[:, c, :]).then_inc(stored, 16)
            sp.wait_ge(stored, 16 * DC)

        @block.gpsimd
        def _(pool):
            def low_part(n, i=0, per=0):
                pool.wait_ge(hi_done, n + 1 + i * per)
                pool.tensor_tensor(wlo[:, n % W, 0:width(n)], raw[:, n % W, 0:width(n)],
                                   whi[:, n % W, 0:width(n)].bitcast(F32), ALU.subtract).then_inc(lo_done, 1)

            n = 0
            while n < NS:
                count = 1
                while n + count < NS and width(n + count) == width(n):
                    count += 1
                runs(pool, n, count, low_part)
                n += count

        @block.scalar
        def _(act):
            def high_part(n, i=0, per=0, tiles=0):
                act.wait_ge(slab_full[n % W], 16 * (n // W + 1) + i * (per // W * 16))
                if n >= W:
                    act.wait_ge(tile_done, TILE_END[n - W] + i * tiles)
                act.copy(whi[:, n % W, 0:width(n)], raw[:, n % W, 0:width(n)]).then_inc(hi_done, 1)

            def root(k):
                act.wait_ge(var_ready, k + 1)
                act.activation(rstd[:], rstd[:], ACT.Sqrt).then_inc(rstd_ready, 1)

            def take(out_ap, t, func, bias=0.0, i=0, per=0):
                tile_is_done(act, t, i, per)
                act.activation(out_ap, bank[t % 4][:], func, bias=bias).then_inc(bank_free[t % 4], 1)

            def attention(base_j, base_t, prob_t, first, full):
                for r in range(NB * H + 1):
                    if r < NB * H:
                        blk, h = r // H, r % H
                        w = SEQ if full else P * (blk + 1)
                        job_is_taken(act, base_j + attn_jobs(r, "logits"))
                        act.activation(square[:, r % 2, 0:w], square[:, r % 2, 0:w], ACT.Exp,
                                       bias=neg_max[:, r % 2:r % 2 + 1], scale=-1.0,
                                       accum_out=sums[:, blk, h:h + 1]).then_inc(probs_ready, 1)
                    if r >= 1:
                        s = r - 1
                        w = SEQ if full else P * (s // H + 1)
                        act.wait_ge(probs_turned, first + s + 1)
                        if s >= 2:
                            head_is_multiplied(act, base_t, first, s - 2)
                        j = base_j + attn_jobs(s, "turn")
                        act.copy(prob_t[:, s % 2, 0:w], bank[4 + j % 4][:, 0:w]).then_inc(bank_free[4 + j % 4], 1)

            def after(n, i=0, per=0, tiles=0):
                name, k = SLABS[n][0], n - FIRST[SLABS[n][0]]
                if name == "iq" and k == 1:
                    for d in range((NB - 1) * H):
                        w, j = P * (d // H + 2), JOB["dots"] + d
                        act.wait_ge(dots_done, d + 1)
                        if d >= 2:
                            act.wait_ge(dots_used, d - 1)
                        act.activation(gate[:, d % 2, 0:w], bank[4 + j % 4][:, 0:w], ACT.Relu) \
                            .then_inc(bank_free[4 + j % 4], 1)
                elif name == "gate_a":
                    for c in (2 * k, 2 * k + 1):
                        if c >= 2:
                            act.wait_ge(gate_used, c - 1)
                        else:
                            act.wait_ge(dots_used, (NB - 1) * H)
                        take(gate[:, c % 2, :], TILE["gate_a"] + c, ACT.Sigmoid, column("b_gate", c))
                elif name == "gate_b":
                    for c in (2 * k, 2 * k + 1):
                        take(x[:, c, :], TILE["gate_b"] + c, ACT.Sigmoid, column("b_gate", DC + c))
                    if k == 3:
                        attention(JOB["attn_1"], TILE["attn_1"], prob_t1, 0, False)
                elif name == "w_out" and k == 3:
                    root(1)
                    act.activation(c_act[:], column("c", 0, DC), ACT.Silu).then_inc(c_ready, 1)
                elif name == "ffn_up":
                    n0 = n - k if k < FH else FFN2
                    t = TILE["ffn_up_0" if k < FH else "ffn_up_1"] + 2 * (n - n0)
                    if n - n0 >= 2:
                        tile_is_taken(act, t - 3, i, tiles)
                    elif k < FH:
                        act.wait_ge(gate_used, DC)
                    else:
                        tile_is_taken(act, TILE["ffn_up_0"] + 2 * (FH - 1 - (n - n0 + FH - 1) % 2) + 1)
                    take(gate[:, (n - n0) % 2, :], t, ACT.Silu, i=i, per=tiles)
                elif n == FFN2 + FH + DC - 1:
                    root(2)
                    root(3)
                    act.wait_ge(angles_ready, 1)
                    act.activation(rope_sin, angle, ACT.Sin).then_inc(rope_ready, 1)
                    act.activation(rope_cos, turn, ACT.Sin).then_inc(rope_ready, 1)
                elif name == "latents" and k == 2:
                    root(4)
                    root(5)
                elif name == "glu_b":
                    act.wait_ge(pads_ready, 1)
                    for c in (2 * k, 2 * k + 1):
                        take(u[:, c + 1, TAPS - 1:], TILE["glu_b"] + c, ACT.Sigmoid)
                elif name == "gate_conv":
                    if k == 0:
                        act.wait_ge(heads_ready, 3)
                    for c in (2 * k, 2 * k + 1):
                        take(gate_conv[:, c, :], TILE["gate_conv"] + c, ACT.Sigmoid)
                    if k == 3:
                        attention(JOB["attn_2"], TILE["attn_2"], prob_t2, NB * H, True)
                elif name == "gate_attn":
                    k //= 2
                    for c in (2 * k, 2 * k + 1):
                        t = TILE["o_and_gate"] + 4 * k + c % 2
                        if k:
                            tile_is_taken(act, t - 4)
                        else:
                            act.wait_ge(probs_ready, 2 * NB * H)
                            tile_is_taken(act, TILE["attn_2"] + 2 * NB - 1)
                        take(gate[:, c % 2, :], t + 2, ACT.Sigmoid)
                    if k == 1:
                        root(6)
                        for c in range(CC):
                            act.wait_ge(scaled, c + 1)
                            act.activation(u[:, c, TAPS - 1:], u[:, c, TAPS - 1:], ACT.Silu,
                                           bias=column("conv_ln_b", c), scale=column("conv_ln_g", c)) \
                                .then_inc(silu_done, 1)
                elif name == "w_out_2" and k == 3:
                    root(7)
                    for v, n_v in ((0, G), (1, E)):
                        act.wait_ge(shift_ready, v + 1)
                        act.activation(rt[:, v, :, 0:n_v], rt[:, v, :, 0:n_v], ACT.Exp).then_inc(exp_ready, 1)
                elif name == "moe_up":
                    e = k
                    t = TILE["moe"] + 2 * e
                    tile_is_taken(act, t - 3 if e >= 2 else t - 3 - 8, i, tiles)
                    take(gate[:, e % 2, :], t, ACT.Silu, i=i, per=tiles)

            high_part(0)
            high_part(1)
            act.wait_ge(col_loaded, 16)
            root(0)
            up, moe = FIRST["ffn_up"], FIRST["moe_up"]
            for n in range(W, up + W):
                high_part(n)
                after(n - W)
            for n0 in (up, FFN2):
                for k in (0, 1):
                    high_part(n0 + W + k)
                    after(n0 + k)
                with act.Fori(0, (FH - 1 - W - 2) // 2) as i:
                    for k in (2, 3):
                        high_part(n0 + W + k, i, 2, 4)
                        after(n0 + k, i, 2, 4)
                for k in range(2 + (FH - 1 - W - 2) // 2 * 2, FH + DC):
                    high_part(n0 + W + k)
                    after(n0 + k)
            for n in range(FIRST["latents"], moe):
                high_part(n + W)
                after(n)

            def moe_group(i, per, tiles, count):
                for k in range(E + 4):
                    if k < count:
                        high_part(moe + W + k, i, per, tiles)
                    if k < E:
                        after(moe + k, i, per, tiles)

            with act.Fori(0, G - 1) as i:
                moe_group(i, E + 4, 24, E + 4)
            moe_group(G - 1, E + 4, 24, E + 4 - W)
            root(8)

        @block.tensor
        def _(pe):
            def tile_bank(t, i=0, per=0):
                if t >= 4:
                    pe.wait_ge(bank_free[t % 4], t // 4 + i * (per // 4))
                return bank[t % 4]

            def job_bank(j):
                if j >= 4:
                    pe.wait_ge(bank_free[4 + j % 4], j // 4)
                return bank[4 + j % 4]

            def product(t, n, c0, rhs, i=0, per=0, tiles=0, ready=None):
                ps = tile_bank(t, i, tiles)
                hi, lo = parts(n)
                kc = SLABS[n][1]
                for k in range(kc):
                    if ready is not None:
                        pe.wait_ge(split_done, ready + k + 1 + i * per)
                    x_hi, x_lo = rhs(k)
                    wh, wl = hi[:, k, c0:c0 + P], lo[:, k, c0:c0 + P]
                    pe.matmul(ps[:], wh, x_hi, start=(k == 0), stop=False)
                    pe.matmul(ps[:], wl, x_hi, start=False, stop=False)
                    mm = pe.matmul(ps[:], wh, x_lo, start=False, stop=(k == kc - 1))
                mm.then_inc(tile_done, 1)

            def slab(n, i=0, per=0):
                pe.wait_ge(lo_done, n + 1 + i * per)

            def chunks(hi, lo):
                return lambda k: (hi[:, k, :], lo[:, k, :])

            h = chunks(h_hi, h_lo)

            def dense(name, t_name, rhs, ready=None, after_slab=None):
                n0 = FIRST[name]
                count = sum(s[0] == name for s in SLABS)
                per_slab = SLABS[n0][2] // P
                for k in range(count):
                    slab(n0 + k)
                    for q in range(per_slab):
                        product(TILE[t_name] + k * per_slab + q, n0 + k, q * P, rhs,
                                ready=ready if k == 0 and q == 0 else None)
                    if after_slab:
                        after_slab(k)

            def sum_square(name, c, count):
                s = SQUARE[name] + c
                b = job_bank(JOB[name]) if c == 0 else bank[4 + JOB[name] % 4]
                pe.wait_ge(squared, s + 1)
                pe.matmul(b[:], ones, square[:, s % 2, :], start=(c == 0), stop=(c == count - 1)).then_inc(summed, 1)

            def sums_behind(name, per_slab, slabs):
                def after_slab(k):
                    for c in range(max(0, (k - 1) * per_slab), k * per_slab):
                        sum_square(name, c, per_slab * slabs)
                    if k == slabs - 1:
                        for c in range(k * per_slab, (k + 1) * per_slab):
                            sum_square(name, c, per_slab * slabs)
                return after_slab

            def attention(base_j, base_t, prob_t, first, full, q, k, v):
                def w(r):
                    return SEQ if full else P * (r // H + 1)

                def logits(r):
                    b = job_bank(base_j + attn_jobs(r, "logits"))
                    pe.matmul(b[:, 0:w(r)], q(r % H, r // H), k(r % H, w(r)), start=True, stop=True) \
                        .then_inc(logits_done, 1)

                def turn_probs(r):
                    pe.wait_ge(probs_ready, first + r + 1)
                    b = job_bank(base_j + attn_jobs(r, "turn"))
                    for s in range(w(r) // P):
                        mm = pe.transpose(b[:, s * P:(s + 1) * P], square[:, r % 2, s * P:(s + 1) * P], ident)
                    mm.then_inc(probs_turned, 1)

                def values(r):
                    hh, t = r % H, base_t + 2 * (r // H)
                    b = tile_bank(t) if hh == 0 else bank[t % 4]
                    job_is_taken(pe, base_j + attn_jobs(r, "turn"))
                    ns = w(r) // P
                    for s in range(ns):
                        mm = pe.matmul(b[:, hh * HD:(hh + 1) * HD], prob_t[:, r % 2, s * P:(s + 1) * P], v(hh, s),
                                       start=(s == 0), stop=(s == ns - 1))
                    mm.then_inc(tile_done if hh == H - 1 else pv_done, 1)

                def turn_rows(blk):
                    t = base_t + 2 * blk + 1
                    tile_is_taken(pe, t - 1)
                    b = tile_bank(t)
                    for c in range(CC):
                        mm = pe.transpose(b[:, c * P:(c + 1) * P], tmp[:, blk % 2, c * P:(c + 1) * P], ident)
                    mm.then_inc(tile_done, 1)

                logits(0)
                logits(1)
                for r in range(NB * H):
                    turn_probs(r)
                    if r + 2 < NB * H:
                        logits(r + 2)
                    if r >= 1:
                        values(r - 1)
                    if r % H == 4 and r > H:
                        turn_rows(r // H - 1)
                values(NB * H - 1)
                turn_rows(NB - 1)

            def half_rows(hh):
                return slice(HD * (hh % 2), HD * (hh % 2 + 1))

            pe.wait_ge(cst_loaded, 16)
            for c in range(DC):
                sum_square("norm_1", c, DC)
            pe.wait_ge(rel_loaded, 32)
            for j, (d0, d1) in enumerate(((0, SEQ), (SEQ, GELEM))):
                pe.matmul(job_bank(JOB["strip"] + j)[0:H, 0:d1 - d0], m["rel"][:], m["onehot"][:, d0:d1],
                          start=True, stop=True).then_inc(strip_sum, 1)
            dense("kv_ikw", "kv_ikw", h, ready=SPLIT["h1"])
            dense("iq", "iq", h)
            tile_is_taken(pe, TILE["kv_ikw"])
            b = job_bank(JOB["v_rows"])
            for s in range(NB):
                mm = pe.transpose(b[:, s * HD:(s + 1) * HD], v_t[HD:P, s * P:(s + 1) * P], ident[HD:P, HD:P])
            mm.then_inc(turned, 1)
            tile_is_taken(pe, TILE["kv_ikw"] + 1)
            b = job_bank(JOB["iw_rows"])
            for s in range(NB):
                mm = pe.transpose(b[:, s * H:(s + 1) * H], square[HD:HD + H, 0, s * P:(s + 1) * P],
                                  ident[HD:HD + H, HD:HD + H])
            mm.then_inc(turned, 1)
            for d in range((NB - 1) * H):
                blk, hh = d // H + 1, d % H
                if d < H and hh % 2 == 0:
                    tile_is_taken(pe, TILE["iq"] + hh // 2)
                w = P * (blk + 1)
                pe.matmul(job_bank(JOB["dots"] + d)[:, 0:w], iq_t[half_rows(hh), hh // 2, blk * P:(blk + 1) * P],
                          ik_t[half_rows(hh), 0:w], start=True, stop=True).then_inc(dots_done, 1)
            for name in ("q", "conv_c", "conv_x", "conv_b"):
                dense(name, name, h)
            dense("branch_a", "branch_a", chunks(a_hi1, a_lo1), ready=SPLIT["conv_1"])
            dense("gate_a", "gate_a", h)
            pe.wait_ge(strip_turned, 16)
            for hh in range(H):
                pe.matmul(job_bank(JOB["bias"] + hh)[:], flip, strip_t[:, hh, :], start=True, stop=True) \
                    .then_inc(bias_sum, 1)
            dense("gate_b", "gate_b", h)
            for c in range(CC):
                tile_is_taken(pe, TILE["q"] + c)
            attention(JOB["attn_1"], TILE["attn_1"], prob_t1, 0, False,
                      lambda hh, blk: q_t[half_rows(hh), hh // 2, blk * P:(blk + 1) * P],
                      lambda hh, w: k_t[half_rows(hh), 0:w],
                      lambda hh, s: v_rows_1[:, s, :])
            for blk in range(NB):
                tile_is_taken(pe, TILE["attn_1"] + 2 * blk + 1)
            dense("branch_b", "branch_b", chunks(a_hi1, a_lo1))
            dense("w_out", "w_out", h, ready=SPLIT["merged_1"], after_slab=sums_behind("norm_2", 2, 4))

            def modulation(s, i=0, per=0):
                pe.wait_ge(ada_full[s % 2], 16 * (s // 2 + 1) + i * (per // 2 * 16))
                if s >= 2:
                    pe.wait_ge(ada_taken, s - 1 + i * per)
                w_ada = ada_raw[:, s % 2, :].rearrange("p (k c) -> p k c", c=256)
                for q in range(2):
                    for k in range(DC):
                        mm = pe.matmul(bank[6 + s % 2][:, q:q + 1], w_ada[:, k, q * P:(q + 1) * P],
                                       c_act[:, k:k + 1], start=(k == 0), stop=(k == DC - 1))
                mm.then_inc(ada_done, 1)

            pe.wait_ge(c_ready, 1)
            for b in (2, 3):
                pe.wait_ge(bank_free[4 + b], len(range(b, JOB["norm_x"], 4)))
            for half in range(2):
                n0, t0, s0 = (FIRST["ffn_up"], FFN2)[half], TILE[f"ffn_up_{half}"], half * FH

                def up(n, i=0, per=0, n0=n0, t0=t0, s0=s0, half=half):
                    slab(n, i, per)
                    for q in range(2):
                        product(t0 + 2 * (n - n0) + q, n, q * P, h, i, per, 2 * per,
                                ready=SPLIT["h2"] if n == n0 and half == 0 and q == 0 and not per else None)
                    modulation(s0 + n - n0, i, per)

                up(n0)
                up(n0 + 1)
                runs(pe, n0 + 2, FH - 2, up)
                down, t0 = n0 + FH, TILE[f"ffn_down_{half}"]
                for k in range(FH):
                    pe.wait_ge(split_done, SPLIT[f"ffn_{half}"] + k + 1)

                def down_slab(n, i=0, per=0, down=down, t0=t0):
                    slab(n, i, per)
                    product(t0 + n - down, n, 0, chunks(f_hi, f_lo), i, per, per)

                if half == 0:
                    runs(pe, down, DC, down_slab, 4)
                else:
                    for c in range(DC):
                        down_slab(down + c)
                        if c < ADA_SLABS - FC:
                            modulation(FC + c)
                        if c == ADA_SLABS - FC:
                            pe.wait_ge(ada_taken, ADA_SLABS)
                        if c > ADA_SLABS - FC:
                            for cc in ([c - 1] if c > ADA_SLABS - FC + 1 else range(c)):
                                sum_square("norm_x", cc, DC)
                    sum_square("norm_x", DC - 1, DC)

            for c in range(DC):
                sum_square("norm_3", c, DC)
            n0 = FIRST["latents"]
            for k in range(3):
                slab(n0 + k)
                for q in range(2):
                    product(TILE["latents"] + 2 * k + q, n0 + k, q * P, h,
                            ready=SPLIT["h3"] if k == 0 and q == 0 else None)
            for c in range(QC):
                sum_square("norm_q", c, QC)
            for c in range(KC):
                sum_square("norm_kv", c, KC)
            dense("glu_b", "glu_b", h)
            dense("glu_a", "glu_a", h)
            dense("w_uq", "w_uq", chunks(l_hi, l_lo), ready=SPLIT["q_lat"])
            n = FIRST["w_ukv"]
            slab(n)
            lat = lambda k: (l_hi[:, QC + k, :], l_lo[:, QC + k, :])
            for q in range(4):
                product(TILE["w_ukv"] + q, n, q * P, lat, ready=SPLIT["kv_lat"] if q == 0 else None)
            for blk in range(NB):
                t = TILE["w_ukv"] + 4 + blk
                ps = tile_bank(t)
                hi, lo = parts(n)
                for k in range(KC):
                    x_hi = l_hi[:, QC + k, blk * P:(blk + 1) * P]
                    x_lo = l_lo[:, QC + k, blk * P:(blk + 1) * P]
                    pe.matmul(ps[:], x_hi, hi[:, k, 512:], start=(k == 0), stop=False)
                    pe.matmul(ps[:], x_hi, lo[:, k, 512:], start=False, stop=False)
                    mm = pe.matmul(ps[:], x_lo, hi[:, k, 512:], start=False, stop=(k == KC - 1))
                mm.then_inc(tile_done, 1)
            dense("gate_conv", "gate_conv", h)
            pe.wait_ge(heads_ready, 3)
            for t in (4, 5, 6, 7):
                tile_is_taken(pe, TILE["w_ukv"] + t)
            attention(JOB["attn_2"], TILE["attn_2"], prob_t2, NB * H, True,
                      lambda hh, blk: q_h[0:QK_DIM, hh, blk * P:(blk + 1) * P],
                      lambda hh, w: k_h[0:QK_DIM, hh, 0:w],
                      lambda hh, s: v_rows_2[:, s, hh * HD:(hh + 1) * HD])
            for blk in range(NB):
                tile_is_taken(pe, TILE["attn_2"] + 2 * blk + 1)
            for k in range(4):
                n = FIRST["o_attn"] + 2 * k
                t = TILE["o_and_gate"] + 4 * k
                slab(n)
                for q in range(2):
                    product(t + q, n, q * P, chunks(o_hi, o_lo))
                slab(n + 1)
                for q in range(2):
                    product(t + 2 + q, n + 1, q * P, h)
                if k == 0:
                    b = job_bank(JOB["ln_mean"])
                    for c in range(CC):
                        pe.wait_ge(conv_done, c + 1)
                        mm = pe.matmul(b[:], ones, u[:, c, TAPS - 1:], start=(c == 0), stop=(c == CC - 1))
                    mm.then_inc(mean_done, 1)
                if k == 1:
                    for c in range(CC):
                        sum_square("ln_var", c, CC)
            dense("conv_out", "conv_out", chunks(c_hi, c_lo), ready=SPLIT["conv_2"])
            dense("w_out_2", "w_out_2", h, ready=SPLIT["merged_2"], after_slab=sums_behind("norm_4", 2, 4))
            pe.wait_ge(router_loaded, 32)
            b = job_bank(JOB["router"])
            for k in range(DC):
                pe.wait_ge(h4_ready, k + 1)
                for blk in range(NB):
                    mm = pe.matmul(b[:, blk * 36:(blk + 1) * 36], tmp[:, k % 2, blk * P:(blk + 1) * P],
                                   router_w[:, k, :], start=(k == 0 and blk == 0), stop=(k == DC - 1),
                                   skip_group_check=True)
                mm.then_inc(routed, 1)
            n0 = FIRST["moe_up"]

            def moe_group(i, first):
                per, tiles = (0, 0) if first else (E + 4, 24)
                for e in range(E):
                    slab(n0 + e, i, per)
                    for q in range(2):
                        product(TILE["moe"] + 2 * e + q, n0 + e, q * P, h, i, 0, tiles,
                                ready=SPLIT["h4"] if first and e == 0 and q == 0 else None)
                    if first and e == 0:
                        pe.wait_ge(weights_ready, 1)
                        b = job_bank(JOB["combine"])
                        for blk in range(NB):
                            mm = pe.transpose(b[0:G * E, blk * P:(blk + 1) * P],
                                              rt[:, 2, blk, :], ident)
                        mm.then_inc(weights_turned, 1)
                for d in range(4):
                    n = n0 + E + d
                    slab(n, i, per)
                    for q in range(2):
                        product(TILE["moe"] + 2 * (E + d) + q, n, q * P, chunks(e_hi, e_lo), i,
                                E if not first else 0, tiles,
                                ready=SPLIT["moe"] if d == 0 and q == 0 else None)

            moe_group(0, True)
            with pe.Fori(1, G) as i:
                moe_group(i, False)
            for c in range(DC):
                sum_square("norm_out", c, DC)

        @block.vector
        def _(dve):
            class Steps:
                n, i, per = 0, 0, 0

            def link(ins):
                Steps.n += 1
                ins.then_inc(step, 1)
                dve.wait_ge(step, Steps.n + Steps.i * Steps.per)

            def loop_runs(n0, count, body, size, steps):
                whole = count // size
                base = Steps.n
                with dve.Fori(0, whole) as i:
                    Steps.i, Steps.per = i, size * steps
                    for k in range(size):
                        body(n0 + k, i, size)
                assert Steps.n - base == size * steps
                Steps.n, Steps.i, Steps.per = base + whole * size * steps, 0, 0
                for n in range(n0 + whole * size, n0 + count):
                    body(n, 0, 0)

            def take(ins, t, i=0, per=0):
                ins.then_inc(bank_free[t % 4], 1)
                tile_is_taken(dve, t, i, per)

            def take_job(ins, j):
                ins.then_inc(bank_free[4 + j % 4], 1)
                job_is_taken(dve, j)

            def split(src, hi, lo):
                link(dve.tensor_copy(hi, src))
                dve.tensor_tensor(lo, src, hi.bitcast(F32), ALU.subtract).then_inc(split_done, 1)

            def squares(name, c, src):
                s = SQUARE[name] + c
                if s >= 2:
                    dve.wait_ge(summed, s - 1)
                dve.tensor_tensor(square[:, s % 2, :], src, src, ALU.mult).then_inc(squared, 1)

            norms = []

            def variance(name, count):
                dve.wait_ge(summed, SQUARE[name] + count)
                j = JOB[name]
                take_job(dve.tensor_scalar(rstd[:], bank[4 + j % 4][:], 1.0 / (count * P), EPS, ALU.mult, ALU.add), j)
                dve.reciprocal(rstd[:], rstd[:]).then_inc(var_ready, 1)
                norms.append(name)
                dve.wait_ge(rstd_ready, len(norms))

            def normalize(src, gain, out_ap):
                return dve.scalar_tensor_tensor(out_ap, src, gain, rstd[:], ALU.mult, ALU.mult)

            def tile(t, i=0, per=0):
                tile_is_done(dve, t, i, per)
                return bank[t % 4]

            def attention_logits(r, base_j, first, full):
                blk, hh = r // H, r % H
                w = SEQ if full else P * (blk + 1)
                j = base_j + attn_jobs(r, "logits")
                b = bank[4 + j % 4]
                dve.wait_ge(logits_done, first + r + 1)
                if r >= 2:
                    dve.wait_ge(probs_turned, first + r - 1)
                p = square[:, r % 2, 0:w]
                if full:
                    dve.tensor_tensor_reduce(p, b[:, 0:w], gate[:, blk % 2, :], -float(QK_DIM) ** -0.5, 3e38,
                                             ALU.add, ALU.min, neg_max[:, r % 2:r % 2 + 1]) \
                        .then_inc(bank_free[4 + j % 4], 1)
                else:
                    off = P * blk * (blk + 1) // 2
                    link(dve.tensor_tensor(p, b[:, 0:w], bias[:, hh, SEQ - w:], ALU.add))
                    dve.tensor_tensor_reduce(p, p, mask_1[:, off:off + w], -1.0, 3e38,
                                             ALU.add, ALU.min, neg_max[:, r % 2:r % 2 + 1]) \
                        .then_inc(bank_free[4 + j % 4], 1)

            def attention_rows(blk, base_t, first):
                dve.wait_ge(probs_ready, first + H * (blk + 1))
                link(dve.reciprocal(inv_sums[:, blk, :], sums[:, blk, :]))
                t = base_t + 2 * blk
                take(dve.tensor_tensor(tmp[:, blk % 2, :].rearrange("p (h d) -> p h d", d=HD),
                                       tile(t)[:].rearrange("p (h d) -> p h d", d=HD),
                                       inv_sums[:, blk, :].unsqueeze(2).to_broadcast([P, H, HD]), ALU.mult), t)

            def attention_split(blk, base_t, hi, lo):
                t = base_t + 2 * blk + 1
                b = tile(t)[:].rearrange("p (c t) -> p c t", t=P)
                cols = slice(blk * P, (blk + 1) * P)
                link(dve.tensor_copy(hi[:, :, cols], b))
                take(dve.tensor_tensor(lo[:, :, cols], b, hi[:, :, cols].bitcast(F32), ALU.subtract), t)

            def attention(base_j, base_t, first, full, hi, lo, before=None, between=None):
                for r in range(NB * H):
                    if before and r % H == 0:
                        before(r // H)
                    attention_logits(r, base_j, first, full)
                    if r % H == 2 and r > H:
                        attention_rows(r // H - 1, base_t, first)
                    if r % H == 6 and r > H:
                        attention_split(r // H - 1, base_t, hi, lo)
                    if between:
                        between()
                attention_rows(NB - 1, base_t, first)
                attention_split(NB - 1, base_t, hi, lo)

            for c in range(DC):
                if c % (DC // 2) == 0:
                    dve.wait_ge(x_loaded[c // (DC // 2)], 16)
                squares("norm_1", c, x[:, c, :])
            dve.wait_ge(col_loaded, 16)
            variance("norm_1", DC)
            for c in range(DC):
                link(normalize(x[:, c, :], column("g_mix", c), tmp[:, c % 2, :]))
                split(tmp[:, c % 2, :], h_hi[:, c, :], h_lo[:, c, :])
            dve.wait_ge(strip_sum, 2)
            for j, (d0, d1) in enumerate(((0, SEQ), (SEQ, GELEM))):
                jj = JOB["strip"] + j
                take_job(dve.tensor_copy(m["strip"][:, d0:d1], bank[4 + jj % 4][0:H, 0:d1 - d0]), jj)
            t = TILE["kv_ikw"]
            b = tile(t)
            dve.tensor_copy(k_t[0:HD, :], b[0:HD, :])
            dve.tensor_copy(k_t[HD:P, :], b[0:HD, :])
            take(dve.tensor_copy(v_t[HD:P, :], b[HD:P, :]), t)
            b = tile(t + 1)
            dve.tensor_copy(ik_t[0:HD, :], b[0:HD, :])
            dve.tensor_copy(ik_t[HD:P, :], b[0:HD, :])
            take(dve.tensor_scalar(square[HD:HD + H, 0, :], b[HD:HD + H, :], H ** -0.5 * HD ** -0.5, None, ALU.mult), t + 1)
            for c in range(CC):
                t = TILE["iq"] + c
                take(dve.tensor_copy(iq_t[:, c, :], tile(t)[:]), t)
            for n, (dst, name) in enumerate(((v_rows_1[:], "v_rows"), (iw_rows, "iw_rows"))):
                j = JOB[name]
                dve.wait_ge(turned, n + 1)
                w = dst.shape[2] * NB
                take_job(dve.tensor_copy(dst, bank[4 + j % 4][:, 0:w].rearrange("p (b d) -> p b d", b=NB)), j)
            score_at = {blk: (P * (blk * (blk + 1) // 2 - 1), P * (blk + 1)) for blk in range(1, NB)}
            for d in range((NB - 1) * H):
                blk, hh = d // H + 1, d % H
                off, w = score_at[blk]
                sc = score[:, off:off + w]
                job_is_taken(dve, JOB["dots"] + d)
                iw = iw_rows[:, blk, hh:hh + 1]
                if hh == 0:
                    dve.tensor_scalar(sc, gate[:, d % 2, 0:w], iw, None, ALU.mult).then_inc(dots_used, 1)
                else:
                    dve.scalar_tensor_tensor(sc, gate[:, d % 2, 0:w], iw, sc, ALU.mult, ALU.add).then_inc(dots_used, 1)
                dve.wait_ge(dots_used, d + 1)
                if hh == H - 1:
                    link(dve.scalar_tensor_tensor(sc[:, w - P:w], const("after", P), FILL, sc[:, w - P:w],
                                                  ALU.mult, ALU.add))
            link(dve.tensor_scalar(mask_1[:, 0:P], const("after", P), NEG, None, ALU.mult))

            def top_k():
                for blk in range(1, NB):
                    off, w = score_at[blk]
                    src, dst = score[:, off:off + w], work[:, off:off + w]
                    for n in range(K_TOP // 8):
                        link(dve.max(top8, src if n == 0 else dst))
                        link(dve.match_replace(dst, top8, src if n == 0 else dst, TAKEN))
                        yield
                    mk = mask_1[:, off + P:off + P + w]
                    link(dve.tensor_tensor(mk, dst, src, ALU.is_equal))
                    link(dve.tensor_scalar(mk, mk, NEG, None, ALU.mult))
                    yield

            def advance(work_left, n):
                for _ in range(n):
                    next(work_left, None)

            selection = top_k()
            for c in range(CC):
                t = TILE["q"] + c
                take(dve.tensor_scalar(q_t[:, c, :], tile(t)[:], HD ** -0.5, None, ALU.mult), t)
                advance(selection, 3)
            dve.wait_ge(strip_stored, 16)
            link(dve.memset(conv_in[:, :, 0:2], 0.0))
            for c in range(CC):
                t = TILE["conv_c"] + c
                take(dve.tensor_copy(conv_in[:, c, 2:], tile(t)[:]), t)
                advance(selection, 4)
            for c in range(CC):
                t = TILE["conv_x"] + c
                take(dve.tensor_tensor(conv_in[:, c, 2:], conv_in[:, c, 2:], tile(t)[:], ALU.mult), t)
                advance(selection, 4)
            for c in range(CC):
                mid = conv_mid[:, c % 2, :]
                for tap in range(3):
                    src, w_tap = conv_in[:, c, tap:tap + SEQ], column("conv_w", tap * CC + c)
                    link(dve.tensor_scalar(mid, src, w_tap, None, ALU.mult) if tap == 0 else
                         dve.scalar_tensor_tensor(mid, src, w_tap, mid, ALU.mult, ALU.add))
                t = TILE["conv_b"] + c
                take(dve.tensor_tensor(tmp[:, c % 2, :], mid, tile(t)[:], ALU.mult), t)
                split(tmp[:, c % 2, :], a_hi1[:, c, :], a_lo1[:, c, :])
                advance(selection, 1)
            for c in range(DC):
                t = TILE["branch_a"] + c
                take(dve.tensor_copy(y1[:, c, :], tile(t)[:]), t)
            advance(selection, 100)
            for c in range(DC):
                tile_is_taken(dve, TILE["gate_a"] + c)
                dve.tensor_tensor(y1[:, c, :], y1[:, c, :], gate[:, c % 2, :], ALU.mult).then_inc(gate_used, 1)
            for hh in range(H):
                j = JOB["bias"] + hh
                dve.wait_ge(bias_sum, hh + 1)
                take_job(dve.tensor_copy(bias[:, hh, :], bank[4 + j % 4][:]), j)
            attention(JOB["attn_1"], TILE["attn_1"], 0, False, a_hi1, a_lo1)
            dve.wait_ge(gate_used, DC)
            for c in range(DC):
                t = TILE["branch_b"] + c
                tile_is_taken(dve, TILE["gate_b"] + c)
                take(dve.tensor_tensor(tmp[:, c % 2, :], x[:, c, :], tile(t)[:], ALU.mult), t)
                link(dve.tensor_tensor(tmp[:, c % 2, :], tmp[:, c % 2, :], y1[:, c, :], ALU.add))
                split(tmp[:, c % 2, :], h_hi[:, c, :], h_lo[:, c, :])
            for c in range(DC):
                t = TILE["w_out"] + c
                if c % (DC // 2) == 0:
                    dve.wait_ge(x_again[c // (DC // 2)], 16)
                take(dve.tensor_tensor(x[:, c, :], x[:, c, :], tile(t)[:], ALU.add), t)
                squares("norm_2", c, x[:, c, :])
            variance("norm_2", DC)
            for c in range(DC):
                link(normalize(x[:, c, :], column("g_ffn", c), tmp[:, c % 2, :]))
                split(tmp[:, c % 2, :], h_hi[:, c, :], h_lo[:, c, :])

            def modulation(s, i=0, per=0):
                dve.wait_ge(ada_done, s + 1 + i * per)
                cols = bass.ds(2 * s + i * 2 * per, 2)
                bias_cols = bass.ds(COLUMNS["ada_b"] + 2 * s + i * 2 * per, 2)
                dve.tensor_tensor(ada[:, cols], bank[6 + s % 2][:, 0:2], col[:, bias_cols], ALU.add) \
                    .then_inc(ada_taken, 1)

            for half in range(2):
                n0, t0, s0 = (FIRST["ffn_up"], FFN2)[half], TILE[f"ffn_up_{half}"], half * FH

                def up(n, i=0, per=0, n0=n0, t0=t0, s0=s0):
                    k, t = n - n0, t0 + 2 * (n - n0)
                    tile_is_taken(dve, t, i, 2 * per)
                    take(dve.tensor_tensor(tmp[:, k % 2, :], gate[:, k % 2, :], tile(t + 1, i, 2 * per)[:], ALU.mult),
                         t + 1, i, 2 * per)
                    chunk = bass.ds(k + i * per, 1)
                    split(tmp[:, k % 2, :], f_hi[:, chunk, :].rearrange("p a t -> p (a t)"),
                          f_lo[:, chunk, :].rearrange("p a t -> p (a t)"))
                    modulation(s0 + k, i, per)

                loop_runs(n0, FH, up, 2, 1)
                down, t0 = n0 + FH, TILE[f"ffn_down_{half}"]

                def add_down(n, i=0, per=0, down=down, t0=t0):
                    t, chunk = t0 + n - down, bass.ds(n - down + i * per, 1)
                    xc = x[:, chunk, :].rearrange("p a t -> p (a t)")
                    take(dve.tensor_tensor(xc, xc, tile(t, i, per)[:], ALU.add), t, i, per)

                if half == 0:
                    loop_runs(down, DC, add_down, 4, 0)
                else:
                    for c in range(DC):
                        add_down(down + c)
                        squares("norm_x", c, x[:, c, :])
                        if c < ADA_SLABS - FC:
                            modulation(FC + c)
            dve.wait_ge(ada_taken, ADA_SLABS)
            for n, (at, gain) in enumerate(((DC, "norm1_g"), (4 * DC, "norm2_g"))):
                link(dve.tensor_scalar(mod[:, n, :], ada[:, at:at + DC], 1.0, None, ALU.add))
                link(dve.tensor_tensor(mod[:, n, :], mod[:, n, :], column(gain, 0, DC), ALU.mult))
            variance("norm_x", DC)

            for c in range(DC):
                link(normalize(x[:, c, :], column("g_final", c), x[:, c, :]))
                squares("norm_3", c, x[:, c, :])
            variance("norm_3", DC)
            for c in range(DC):
                link(normalize(x[:, c, :], mod[:, 0, c:c + 1], tmp[:, c % 2, :]))
                link(dve.tensor_scalar(tmp[:, c % 2, :], tmp[:, c % 2, :], ada[:, c:c + 1], None, ALU.add))
                split(tmp[:, c % 2, :], h_hi[:, c, :], h_lo[:, c, :])
            dve.wait_ge(pos_loaded, 32)
            link(dve.tensor_copy(pos_row[:], pos_raw.bitcast(I32)))
            link(dve.tensor_copy(pos_col, pos_col_raw))
            link(dve.tensor_scalar(angle, pos_row[:], const("inv_freq"), None, ALU.mult))
            link(dve.tensor_scalar(turn, angle, 1.0 / (2.0 * np.pi), 12582912.0, ALU.mult, ALU.add))
            link(dve.tensor_scalar(turn, turn, -12582912.0, None, ALU.add))
            for part in (6.28125, 0.0019359588623046875, 2.0 * np.pi - 6.28125 - 0.0019359588623046875):
                link(dve.scalar_tensor_tensor(angle, turn, -part, angle, ALU.mult, ALU.add))
            link(dve.tensor_scalar(turn, angle, np.pi / 2, None, ALU.add))
            link(dve.tensor_scalar(pos_raw, turn, np.pi, -2.0 * np.pi, ALU.is_gt, ALU.mult))
            link(dve.tensor_tensor(turn, turn, pos_raw, ALU.add))
            link(dve.tensor_scalar(turn, turn, 3.1415925, -3.1415925, ALU.min, ALU.max))
            dve.tensor_scalar(angle, angle, 3.1415925, -3.1415925, ALU.min, ALU.max).then_inc(angles_ready, 1)
            for c in range(QC + KC):
                t = TILE["latents"] + c
                take(dve.tensor_copy(q_h[:, c, :], tile(t)[:]), t)
                squares("norm_q" if c < QC else "norm_kv", c if c < QC else c - QC, q_h[:, c, :])
            dve.wait_ge(rope_ready, 2)
            link(dve.tensor_scalar(rope_sin, rope_sin, const("rope_sign"), None, ALU.mult))

            def rotate(t, rows):
                take(dve.tensor_copy(turn[0:rows, :], tile(t)[0:rows, :]), t)
                link(dve.stream_shuffle(angle[0:rows, :], turn[0:rows, :],
                                        [(r + ROPE // 2) % ROPE for r in range(ROPE)]))
                link(dve.tensor_tensor(turn[0:rows, :], turn[0:rows, :], rope_cos[0:rows, :], ALU.mult))
                link(dve.tensor_tensor(angle[0:rows, :], angle[0:rows, :], rope_sin[0:rows, :], ALU.mult))

            rotate(TILE["latents"] + QC + KC, ROPE)
            link(dve.tensor_tensor(k_h[HD:QK_DIM, 0, :], turn[0:ROPE, :], angle[0:ROPE, :], ALU.add))
            dve.tensor_copy(k_h[HD:QK_DIM, 1:, :], k_h[HD:QK_DIM, 0:1, :].to_broadcast([ROPE, H - 1, SEQ])) \
                .then_inc(heads_ready, 1)
            for name, c0, count in (("q", 0, QC), ("kv", QC, KC)):
                variance("norm_" + name, count)
                for c in range(count):
                    link(normalize(q_h[:, c0 + c, :], column(name + "_norm_g", c), tmp[:, c % 2, :]))
                    split(tmp[:, c % 2, :], l_hi[:, c0 + c, :], l_lo[:, c0 + c, :])
            dve.memset(u[:, :, 0:TAPS - 1], 0.0).then_inc(pads_ready, 1)
            dve.wait_ge(pads_ready, 1)
            for c in range(CC):
                t = TILE["glu_a"] + c
                tile_is_taken(dve, TILE["glu_b"] + c)
                take(dve.tensor_tensor(u[:, c + 1, TAPS - 1:], u[:, c + 1, TAPS - 1:], tile(t)[:], ALU.mult), t)

            def convolution():
                for c in range(CC):
                    dst = u[:, c, TAPS - 1:]
                    for tap in range(TAPS):
                        src, w_tap = u[:, c + 1, tap:tap + SEQ], column("conv_w_2", tap * CC + c)
                        if tap == 0:
                            link(dve.tensor_scalar(dst, src, w_tap, column("conv_b", c), ALU.mult, ALU.add))
                        elif tap < TAPS - 1:
                            link(dve.scalar_tensor_tensor(dst, src, w_tap, dst, ALU.mult, ALU.add))
                        else:
                            dve.scalar_tensor_tensor(dst, src, w_tap, dst, ALU.mult, ALU.add).then_inc(conv_done, 1)
                            dve.wait_ge(conv_done, c + 1)
                        yield

            taps = convolution()

            def two_heads(dst, h0, t):
                b = tile(t)
                dve.tensor_copy(dst[0:HD, h0, :], b[0:HD, :])
                take(dve.tensor_copy(dst[0:HD, h0 + 1, :], b[HD:P, :]), t)

            for half in range(2):
                t = TILE["w_uq"] + 3 * half
                for q in range(2):
                    two_heads(q_h, 4 * half + 2 * q, t + q)
                    advance(taps, 2)
                rotate(t + 2, P)
                for q in range(4):
                    ins = dve.tensor_tensor(q_h[HD:QK_DIM, 4 * half + q, :], turn[32 * q:32 * (q + 1), :],
                                            angle[32 * q:32 * (q + 1), :], ALU.add)
                ins.then_inc(heads_ready, 1)
                dve.wait_ge(heads_ready, 2 + half)
                advance(taps, 2)
            for q in range(4):
                two_heads(k_h, 2 * q, TILE["w_ukv"] + q)
                advance(taps, 1)
            for blk in range(NB):
                t = TILE["w_ukv"] + 4 + blk
                take(dve.tensor_copy(v_rows_2[:, blk, :], tile(t)[:]), t)
                advance(taps, 1)
            advance(taps, 60)

            def mask(blk):
                link(dve.tensor_scalar(gate[:, blk % 2, :], pos_row[:], pos_col[:, blk:blk + 1], NEG, ALU.is_gt, ALU.mult))

            attention(JOB["attn_2"], TILE["attn_2"], NB * H, True, o_hi, o_lo, before=mask,
                      between=lambda: advance(taps, 2))
            advance(taps, 200)

            def gated(k):
                for c in (2 * k, 2 * k + 1):
                    t = TILE["o_and_gate"] + 4 * k + c % 2
                    tile_is_taken(dve, t + 2)
                    take(dve.tensor_tensor(q_h[:, c, :], gate[:, c % 2, :], tile(t)[:], ALU.mult), t)

            gated(0)
            mean = prob_t2[:, 0, :]
            j = JOB["ln_mean"]
            dve.wait_ge(mean_done, 1)
            take_job(dve.tensor_scalar(mean, bank[4 + j % 4][:], 1.0 / (CC * P), None, ALU.mult), j)
            for c in range(CC):
                link(dve.tensor_tensor(u[:, c, TAPS - 1:], u[:, c, TAPS - 1:], mean, ALU.subtract))
                squares("ln_var", c, u[:, c, TAPS - 1:])
            gated(1)
            variance("ln_var", CC)
            for c in range(CC):
                dve.tensor_tensor(u[:, c, TAPS - 1:], u[:, c, TAPS - 1:], rstd[:], ALU.mult).then_inc(scaled, 1)
            gated(2)
            for c in range(CC):
                dve.wait_ge(silu_done, c + 1)
                split(u[:, c, TAPS - 1:], c_hi[:, c, :], c_lo[:, c, :])
            gated(3)
            for c in range(DC):
                t = TILE["conv_out"] + c
                tile_is_taken(dve, TILE["gate_conv"] + c)
                take(dve.tensor_tensor(tmp[:, c % 2, :], gate_conv[:, c, :], tile(t)[:], ALU.mult), t)
                link(dve.tensor_tensor(tmp[:, c % 2, :], tmp[:, c % 2, :], q_h[:, c, :], ALU.add))
                split(tmp[:, c % 2, :], h_hi[:, c, :], h_lo[:, c, :])
            for c in range(DC):
                t = TILE["w_out_2"] + c
                take(dve.scalar_tensor_tensor(x[:, c, :], tile(t)[:], ada[:, 2 * DC + c:2 * DC + c + 1], x[:, c, :],
                                              ALU.mult, ALU.add), t)
                squares("norm_4", c, x[:, c, :])
            variance("norm_4", DC)
            for c in range(DC):
                if c >= 2:
                    dve.wait_ge(routed, c - 1)
                link(normalize(x[:, c, :], mod[:, 1, c:c + 1], tmp[:, c % 2, :]))
                dve.tensor_scalar(tmp[:, c % 2, :], tmp[:, c % 2, :], ada[:, 3 * DC + c:3 * DC + c + 1], None, ALU.add) \
                    .then_inc(h4_ready, 1)
                dve.wait_ge(h4_ready, c + 1)
                split(tmp[:, c % 2, :], h_hi[:, c, :], h_lo[:, c, :])

            def small(v, n):
                return rt[:, v, :, 0:n]

            def wide(t, n):
                return t.to_broadcast([P, NB, n])

            def first_best(values, best, n, key, out_ap):
                link(dve.tensor_tensor(key, values, wide(best, n), ALU.is_equal))
                link(dve.tensor_tensor(key, key, const("ramp", n).unsqueeze(1).to_broadcast([P, NB, n]), ALU.mult))
                link(dve.tensor_reduce(small(13, 1), key, AX.X, ALU.max))
                link(dve.tensor_tensor(out_ap, key, wide(small(13, 1), n), ALU.is_equal))

            dve.wait_ge(routed, DC)
            dve.wait_ge(router_loaded, 32)
            j = JOB["router"]
            logits_g, logits_e = small(3, G), small(4, G * E)
            b = bank[4 + j % 4][:, 0:NB * 36].rearrange("p (b e) -> p b e", b=NB)
            link(dve.tensor_tensor(logits_g, b[:, :, 0:G], router_b[:, 0:G].unsqueeze(1).to_broadcast([P, NB, G]), ALU.add))
            take_job(dve.tensor_tensor(logits_e, b[:, :, G:], router_b[:, G:].unsqueeze(1).to_broadcast([P, NB, G * E]),
                                       ALU.add), j)
            best, group, key = small(5, 1), small(6, G), small(12, E)
            link(dve.tensor_reduce(best, logits_g, AX.X, ALU.max))
            dve.tensor_tensor(small(0, G), logits_g, wide(best, G), ALU.subtract).then_inc(shift_ready, 1)
            first_best(logits_g, best, G, small(12, G), group)
            four = rt[:, 2, :, :].rearrange("p b (g e) -> p b g e", g=G)
            link(dve.tensor_tensor(four, logits_e.rearrange("p b (g e) -> p b g e", g=G),
                                   group.unsqueeze(3).to_broadcast([P, NB, G, E]), ALU.mult))
            chosen, best_e = small(7, E), small(8, 1)
            link(dve.tensor_reduce(chosen, rt[:, 2, :, :].rearrange("p b (g e) -> p b e g", g=G), AX.X, ALU.add))
            link(dve.tensor_reduce(best_e, chosen, AX.X, ALU.max))
            dve.tensor_tensor(small(1, E), chosen, wide(best_e, E), ALU.subtract).then_inc(shift_ready, 1)
            top, second, rest = small(9, E), small(10, E), small(11, E)
            first_best(chosen, best_e, E, key, top)
            link(dve.scalar_tensor_tensor(rest, top, NEG, chosen, ALU.mult, ALU.add))
            link(dve.tensor_reduce(best_e, rest, AX.X, ALU.max))
            first_best(rest, best_e, E, key, second)
            link(dve.tensor_tensor(top, top, second, ALU.add))
            dve.wait_ge(exp_ready, 2)
            total, scale_w = small(5, 1), small(8, 1)
            link(dve.tensor_reduce(total, small(0, G), AX.X, ALU.add))
            link(dve.tensor_tensor(top, top, small(1, E), ALU.mult))
            link(dve.tensor_reduce(scale_w, top, AX.X, ALU.add))
            link(dve.tensor_tensor(scale_w, scale_w, total, ALU.mult))
            link(dve.reciprocal(scale_w, scale_w))
            link(dve.tensor_tensor(top, top, wide(scale_w, E), ALU.mult))
            dve.tensor_tensor(four, top.unsqueeze(2).to_broadcast([P, NB, G, E]),
                              group.unsqueeze(3).to_broadcast([P, NB, G, E]), ALU.mult).then_inc(weights_ready, 1)
            dve.wait_ge(weights_turned, 1)
            j = JOB["combine"]
            dve.tensor_copy(comb_t[:], bank[4 + j % 4][0:G * E, :]).then_inc(bank_free[4 + j % 4], 1)

            base = Steps.n
            with dve.Fori(0, G) as i:
                Steps.i, Steps.per = i, E
                for e in range(E):
                    t = TILE["moe"] + 2 * e
                    tile_is_taken(dve, t, i, 24)
                    take(dve.tensor_tensor(tmp[:, e % 2, :], gate[:, e % 2, :], tile(t + 1, i, 24)[:], ALU.mult),
                         t + 1, i, 24)
                    dve.wait_ge(comb_full[e % 2], 16 * (e // 2 + 1) + i * (E // 2 * 16))
                    dve.tensor_tensor(tmp[:, e % 2, :], tmp[:, e % 2, :], comb[:, e % 2, :], ALU.mult) \
                        .then_inc(comb_used, 1)
                    dve.wait_ge(comb_used, e + 1 + i * E)
                    split(tmp[:, e % 2, :], e_hi[:, e, :], e_lo[:, e, :])
                for c in range(DC):
                    t = TILE["moe"] + 2 * E + c
                    take(dve.scalar_tensor_tensor(x[:, c, :], tile(t, i, 24)[:], ada[:, 5 * DC + c:5 * DC + c + 1],
                                                  x[:, c, :], ALU.mult, ALU.add), t, i, 24)
            assert Steps.n - base == E
            Steps.n, Steps.i, Steps.per = base + G * E, 0, 0
            for c in range(DC):
                squares("norm_out", c, x[:, c, :])
            variance("norm_out", DC)
            for c in range(DC):
                normalize(x[:, c, :], column("final_norm_g", c), x[:, c, :]).then_inc(out_ready, 1)


def bucket_of(distance):
    n = np.maximum(distance, 0)
    large = MAX_EXACT + (np.log(np.maximum(n, 1) / MAX_EXACT) / np.log(MAX_DISTANCE / MAX_EXACT)
                         * (N_BUCKETS - MAX_EXACT)).astype(np.int64)
    return np.where(n < MAX_EXACT, n, np.minimum(large, N_BUCKETS - 1))


def constants():
    c = np.zeros((P, CONST["end"]), np.float32)
    i = np.arange(P)
    c[:, CONST["ident"]:][:, :P] = i[:, None] == i[None, :]
    c[:, CONST["flip"]:][:, :P] = i[:, None] == P - 1 - i[None, :]
    c[:, CONST["ones"]:][:, :P] = 1.0
    c[:, CONST["after"]:][:, :P] = i[None, :] > i[:, None]
    c[:, CONST["ramp"]:][:, :E] = E - np.arange(E)
    c[:, CONST["inv_freq"]] = np.float32(10000.0) ** (-(np.arange(P) % (ROPE // 2) * 2).astype(np.float32) / np.float32(ROPE))
    c[:, CONST["rope_sign"]] = np.where(i % ROPE < ROPE // 2, -1.0, 1.0)
    onehot = bucket_of(SEQ - 1 - np.arange(GELEM))[None, :] == np.arange(N_BUCKETS)[:, None]
    return c, onehot.astype(np.float32)


def lay_out_slabs(v):
    w_in, w_in_2 = v["w_in"][0], v["w_in_2"][0]
    gate_up = [v["w_ffn_gate"][0], v["w_ffn_up"][0]]
    w_uq, w_ukv = v["w_uq_2"][0], v["w_ukv_2"][0]
    at_in = np.cumsum([0, 512, 512, 512, 512, 64, 64, 512, 64, 8, D, D])
    at_in2 = np.cumsum([0, Q_RANK, KV_RANK, ROPE, 512, 512, D, D])
    pack = np.zeros((NS, P, SLAB), np.float32)

    def put(n, blocks):
        kc, c = SLABS[n][1:]
        dst = pack[n, :, :kc * c].reshape(P, kc, c)
        c0 = 0
        for b in blocks:
            dst[:, :, c0:c0 + b.shape[1]] = b.reshape(kc, P, b.shape[1]).transpose(1, 0, 2)
            c0 += b.shape[1] if b.shape[1] % HD == 0 else P - c0 % P
    count = {}
    for n, (name, kc, c) in enumerate(SLABS):
        k = count[name] = count.get(name, -1) + 1
        cols = slice(k * c, (k + 1) * c)
        if name == "kv_ikw":
            put(n, [w_in[:, at_in[4]:at_in[6]], w_in[:, at_in[7]:at_in[8]], w_in[:, at_in[8]:at_in[9]]])
        elif name in ("iq", "q", "conv_c", "conv_x", "conv_b", "gate_a", "gate_b"):
            first = at_in[{"conv_b": 0, "conv_c": 1, "conv_x": 2, "q": 3, "iq": 6, "gate_a": 9, "gate_b": 10}[name]]
            put(n, [w_in[:, first + k * c:first + (k + 1) * c]])
        elif name in ("branch_a", "branch_b", "w_out"):
            put(n, [v[{"branch_a": "w_branch_a", "branch_b": "w_branch_b", "w_out": "w_out"}[name]][0][:, cols]])
        elif name == "ffn_up":
            put(n, [w[:, k * P:(k + 1) * P] for w in gate_up])
        elif name == "ffn_down":
            half, q = divmod(k, DC)
            put(n, [v["w_ffn_down"][0][half * FH * P:(half + 1) * FH * P, q * P:(q + 1) * P]])
        elif name == "latents":
            first = [w_in_2[:, :256], w_in_2[:, 256:512], w_in_2[:, 512:at_in2[3]]][k]
            put(n, [first[:, :P], first[:, P:]])
        elif name in ("glu_a", "glu_b", "gate_attn", "gate_conv"):
            first = at_in2[{"glu_a": 3, "glu_b": 4, "gate_attn": 5, "gate_conv": 6}[name]]
            put(n, [w_in_2[:, first + k * c:first + (k + 1) * c]])
        elif name == "w_uq":
            heads = w_uq.reshape(Q_RANK, H, QK_DIM)[:, 4 * k:4 * k + 4]
            put(n, [heads[:, :, :HD].reshape(Q_RANK, -1), heads[:, :, HD:].reshape(Q_RANK, -1)])
        elif name == "w_ukv":
            heads = w_ukv.reshape(KV_RANK, H, 2 * HD)
            put(n, [heads[:, :, :HD].reshape(KV_RANK, -1), heads[:, :, HD:].reshape(KV_RANK, -1)])
        elif name in ("conv_out", "o_attn", "w_out_2"):
            put(n, [v[{"conv_out": "w_conv_out_2", "o_attn": "w_o_attn_2", "w_out_2": "w_out_2"}[name]][0][:, cols]])
        elif name == "moe_up":
            g, e = divmod(k, E)
            put(n, [v["expert_w_gate_2"][0, g, e], v["expert_w_up_2"][0, g, e]])
        elif name == "moe_down":
            g, q = divmod(k, 4)
            put(n, [v["expert_w_down_2"][0, g].reshape(E * P, D)[:, q * 256:(q + 1) * 256]])
    ada = v["ada_w_2"][0].reshape(DC, P, ADA_SLABS, 256).transpose(2, 1, 0, 3).reshape(ADA_SLABS, P, SLAB)
    return pack, np.ascontiguousarray(ada)


def kernel(**inputs):
    import concourse.bacc as _bacc
    from concourse.bass_utils import run_bass_kernel_spmd as _run

    v = {k: np.asarray(x) for k, x in inputs.items()}
    pack, ada = lay_out_slabs(v)

    def columns(x):
        return x.reshape(-1, P).T

    order = ["g_mix", "b_gate", "conv_w", "g_ffn", "g_final", "c_2", "ada_b_2", "norm1_g_2", "norm2_g_2",
             "q_norm_g_2", "kv_norm_g_2", "conv_w_2", "conv_b_2", "conv_ln_g_2", "conv_ln_b_2", "final_norm_g_2"]
    const, onehot = constants()
    router_w = np.concatenate([v["router_group_w_2"][0], v["router_expert_w_2"][0]], axis=1)
    arrays = {
        "x_t": v["x"][0].T,
        "wpack": pack,
        "ada_pack": ada,
        "columns": np.concatenate([columns(v[n]) for n in order], axis=1),
        "const": const,
        "onehot": onehot,
        "rel_bias": v["rel_bias"],
        "positions_2": v["positions_2"],
        "router_w": router_w.reshape(DC, P, G + G * E).transpose(1, 0, 2),
        "router_b": np.concatenate([v["router_group_b_2"], v["router_expert_b_2"]], axis=1),
    }
    nc = _bacc.Bacc("TRN2", target_bir_lowering=False, num_devices=1)
    fed, aps = {}, {}
    for name, x in arrays.items():
        x = np.ascontiguousarray(x)
        fed[f"in_{name}"] = x
        aps[name] = nc.dram_tensor(f"in_{name}", x.shape, mybir.dt.from_np(x.dtype), kind="ExternalInput").ap()
    out = nc.dram_tensor("out_t", (D, SEQ), F32, kind="ExternalOutput").ap()
    build(nc, aps, out)
    r = _run(nc, [fed], core_ids=[0])
    return np.ascontiguousarray(r.results[0]["out_t"].T)[None]
```

```python
from contextlib import ExitStack

import numpy as np

import concourse.bass as bass
from concourse import mybir

F32 = mybir.dt.float32
F32R = mybir.dt.float32r
I32 = mybir.dt.int32
ALU = mybir.AluOpType
ACT = mybir.ActivationFunctionType
AX = mybir.AxisListType

P = 128
D = 1024
SEQ = 512
NB = SEQ // P
DC = D // P
H = 8
HD = 64
K_TOP = min(256, SEQ // 4)
D_FF = 2816
FC = D_FF // P
FH = FC // 2
EPS = 1e-6
N_BUCKETS, MAX_EXACT, MAX_DISTANCE = 32, 16, 128
Q_RANK, KV_RANK, ROPE = 384, 256, 32
QC, KC = Q_RANK // P, KV_RANK // P
QK_DIM = HD + ROPE
TAPS = 31
CC = 512 // P
G, E = 4, 8
NEG = -1e30
FILL = -3.0e38
TAKEN = -3.3e38
SLAB = 2048
W = 2
GELEM = 640

SLABS = (
    [("kv_ikw", DC, 256)] + [("iq", DC, 256)] * 2 + [("q", DC, 256)] * 2
    + [("conv_c", DC, 256)] * 2 + [("conv_x", DC, 256)] * 2 + [("conv_b", DC, 256)] * 2
    + [("gate_a", DC, 256)] * 4 + [("branch_a", CC, 512)] * 2 + [("gate_b", DC, 256)] * 4
    + [("branch_b", CC, 512)] * 2 + [("w_out", DC, 256)] * 4
    + ([("ffn_up", DC, 256)] * FH + [("ffn_down", FH, 128)] * DC) * 2
    + [("latents", DC, 256)] * 3 + [("glu_b", DC, 256)] * 2 + [("glu_a", DC, 256)] * 2
    + [("w_uq", QC, 384)] * 2 + [("w_ukv", KC, 512)] * 2 + [("gate_conv", DC, 256)] * 4
    + [("o_attn", CC, 256), ("gate_attn", DC, 256)] * 4 + [("conv_out", CC, 512)] * 2
    + [("w_out_2", DC, 256)] * 4 + ([("moe_up", DC, 256)] * E + [("moe_down", E, 256)] * 4) * G
)
FIRST = {}
for _n, (_name, _, _) in enumerate(SLABS):
    FIRST.setdefault(_name, _n)
NS = len(SLABS)
ADA_SLABS = 6 * D // 256
FFN2 = FIRST["ffn_up"] + FH + DC

TILE, JOB = {}, {}


def _number(table, names):
    n = 0
    for name, count in names:
        table[name] = n
        n += count


_number(TILE, [
    ("kv_ikw", 2), ("iq", 4), ("q", 4), ("conv_c", 4), ("conv_x", 4), ("conv_b", 4), ("gate_a", 8),
    ("branch_a", 8), ("gate_b", 8), ("attn_1", 2 * NB), ("branch_b", 8), ("w_out", 8),
    ("ffn_up_0", 2 * FH), ("ffn_down_0", DC), ("ffn_up_1", 2 * FH), ("ffn_down_1", DC),
    ("latents", 6), ("glu_b", 4), ("glu_a", 4), ("w_uq", 6), ("w_ukv", 8), ("gate_conv", 8),
    ("attn_2", 2 * NB), ("o_and_gate", 16), ("conv_out", 8), ("w_out_2", 8), ("moe", 24 * G)])
_number(JOB, [
    ("norm_1", 1), ("strip", 2), ("v_rows", 1), ("iw_rows", 1), ("dots", (NB - 1) * H), ("bias", H),
    ("attn_1", 2 * NB * H), ("norm_2", 1), ("ada", 1), ("norm_3", 1), ("norm_x", 1), ("norm_q", 1), ("norm_kv", 1),
    ("attn_2", 2 * NB * H), ("ln_mean", 1), ("ln_var", 1), ("norm_4", 1), ("router", 1),
    ("combine", 1), ("norm_out", 1)])
SPLIT = {}
_number(SPLIT, [
    ("h1", DC), ("conv_1", CC), ("merged_1", DC), ("h2", DC), ("ffn_0", FH), ("ffn_1", FH),
    ("h3", DC), ("q_lat", QC), ("kv_lat", KC), ("conv_2", CC), ("merged_2", DC),
    ("h4", DC), ("moe", G * E)])
COLUMNS = {}
_number(COLUMNS, [
    ("g_mix", DC), ("b_gate", 2 * DC), ("conv_w", 3 * CC), ("g_ffn", DC), ("g_final", DC), ("c", DC),
    ("ada_b", 6 * DC), ("norm1_g", DC), ("norm2_g", DC), ("q_norm_g", QC), ("kv_norm_g", KC),
    ("conv_w_2", TAPS * CC), ("conv_b", CC), ("conv_ln_g", CC), ("conv_ln_b", CC), ("final_norm_g", DC),
    ("end", 0)])
CONST = {}
_number(CONST, [("ident", P), ("flip", P), ("ones", P), ("after", P), ("ramp", E), ("inv_freq", 1),
                ("rope_sign", 1), ("end", 0)])


def attn_jobs(r, kind):
    if kind == "logits":
        return r if r < 2 else 2 * r - 1
    return 2 * r + 2 if r < NB * H - 2 else r + NB * H


NORMS = {name: n for n, name in enumerate(
    ["norm_1", "norm_2", "norm_3", "norm_x", "norm_q", "norm_kv", "ln_var", "norm_4", "norm_out"])}


def squares_done(name, part):
    k = NORMS[name]
    side_by_side = {("norm_3", 1): 1, ("norm_x", 0): -1}
    return 2 * k + part + 1 + side_by_side.get((name, part), 0)


TILES_OF = {"kv_ikw": 2, "branch_a": 4, "branch_b": 4, "conv_out": 4, "ffn_down": 1, "w_uq": 3, "w_ukv": 4}
TILE_END = []
_t = 0
for _n, (_name, _, _) in enumerate(SLABS):
    if _n in (FIRST["branch_b"], FIRST["o_attn"]):
        _t += 2 * NB
    _t += TILES_OF.get(_name, 2)
    TILE_END.append(_t)


def build(nc, a, out):
    ctx = ExitStack()
    with ctx:
        def sem(name):
            return ctx.enter_context(nc.semaphore(name))

        def sbuf(name, shape, dt=F32, stack=ctx):
            return stack.enter_context(nc.sbuf_tensor(name, shape, dt))

        raw = sbuf("raw", [P, W, SLAB])
        whi = sbuf("whi", [P, W, SLAB], F32R)
        wlo = sbuf("wlo", [P, W, SLAB], F32R)
        x = sbuf("x", [P, DC, SEQ])
        tmp = sbuf("tmp", [P, 2, SEQ])
        square = sbuf("square", [P, 2, SEQ])
        rstd = sbuf("rstd", [P, 2, SEQ])
        pos_row = sbuf("pos_row", [P, SEQ])
        gate = sbuf("gate", [P, 2, SEQ])
        cst = sbuf("cst", [P, CONST["end"]])
        col = sbuf("col", [P, COLUMNS["end"]])
        c_act = sbuf("c_act", [P, DC])
        ada = sbuf("ada", [P, 6 * DC])
        mod = sbuf("mod", [P, 2, DC])
        g_final_2 = sbuf("g_final_2", [P, DC])
        h_hi = sbuf("h_hi", [P, DC, SEQ], F32R)
        h_lo = sbuf("h_lo", [P, DC, SEQ], F32R)
        stats = sbuf("stats", [P, 160])
        sums = stats[:, 0:NB * H].rearrange("p (b h) -> p b h", h=H)
        inv_sums = stats[:, 32:32 + NB * H].rearrange("p (b h) -> p b h", h=H)
        neg_max = stats[:, 64:66]
        top8 = stats[:, 72:80]
        iw_rows = stats[:, 80:80 + NB * H].rearrange("p (b h) -> p b h", h=H)
        pos_col = stats[:, 112:112 + NB]
        pos_col_raw = stats[:, 120:120 + NB].bitcast(I32)

        def overlay(*views):
            made, size = {}, 0
            for view in views:
                with ExitStack() as s:
                    n = 0
                    for name, shape, dt in view:
                        made[name] = sbuf(name, shape, dt, s)
                        n += 4 * int(np.prod(shape[1:])) + 32
                    size = max(size, n)
            return made, size

        memory = {}

        def place(name, *views):
            made, size = overlay(*views)
            memory.update(made)
            ctx.enter_context(nc.sbuf_tensor(name, [P, size // 4], F32))

        place("place_a",
              [("onehot", [N_BUCKETS, GELEM], F32), ("rel", [N_BUCKETS, H], F32), ("strip", [H, GELEM], F32)],
              [("conv_in", [P, CC, SEQ + 2], F32), ("conv_mid", [P, 2, SEQ], F32)],
              [("strip_t", [P, H, SEQ], F32)],
              [("ada_raw", [P, 2, SLAB], F32)],
              [("rope", [P, 5, SEQ], F32)],
              [("gate_conv", [P, DC, SEQ], F32)])
        stages = []

        def stage(*views):
            stages.append(overlay(*views))
            memory.update(stages[-1][0])

        base_1 = ExitStack()
        made, size = overlay([("iq_t", [P, CC, SEQ], F32), ("score", [P, 1152], F32), ("work", [P, 1152], F32)],
                             [("bias", [P, H, SEQ], F32)])
        memory.update(made)
        base_1.enter_context(nc.sbuf_tensor("place_1", [P, size // 4], F32))
        stage([("ik_t", [P, SEQ], F32), ("q_t", [P, CC, SEQ], F32), ("k_t", [P, SEQ], F32), ("v_t", [P, SEQ], F32),
               ("v_rows_1", [P, NB, HD], F32), ("mask_1", [P, 1280], F32), ("y1", [P, DC, SEQ], F32),
               ("prob_t1", [P, 2, SEQ], F32), ("a_hi1", [P, CC, SEQ], F32R), ("a_lo1", [P, CC, SEQ], F32R)])
        base_1.close()
        stage([("f_hi", [P, FH, SEQ], F32R), ("f_lo", [P, FH, SEQ], F32R), ("ada_sum", [P, ADA_SLABS, 256], F32)])
        base_3 = ExitStack()
        memory["q_h"] = sbuf("q_h", [P, H, SEQ], F32, base_3)
        made, size = overlay([("k_h", [P, H, SEQ], F32)],
                             [("c_hi", [P, CC, SEQ], F32R), ("c_lo", [P, CC, SEQ], F32R)])
        memory.update(made)
        base_3.enter_context(nc.sbuf_tensor("place_3", [P, size // 4], F32))
        made, size = overlay([("l_hi", [P, QC + KC, SEQ], F32R), ("l_lo", [P, QC + KC, SEQ], F32R)],
                             [("o_hi", [P, CC, SEQ], F32R), ("o_lo", [P, CC, SEQ], F32R),
                              ("prob_t2", [P, 2, SEQ], F32)])
        memory.update(made)
        base_3.enter_context(nc.sbuf_tensor("place_3b", [P, size // 4], F32))
        stage([("v_rows_2", [P, NB, H * HD], F32),
               ("u", [P, CC + 1, SEQ + TAPS - 1], F32)])
        base_3.close()
        stage([("e_hi", [P, E, SEQ], F32R), ("e_lo", [P, E, SEQ], F32R), ("comb", [P, 2, SEQ], F32),
               ("comb_t", [G * E, SEQ], F32), ("router_w", [P, DC, G + G * E], F32),
               ("router_hi", [P, DC, G + G * E], F32R), ("router_lo", [P, DC, G + G * E], F32R),
               ("router_b", [P, G + G * E], F32), ("rt", [P, 14, NB, G * E], F32)])
        m = memory
        iq_t, score, work, bias = m["iq_t"], m["score"], m["work"], m["bias"]
        ik_t, q_t, k_t, v_t, v_rows_1 = m["ik_t"], m["q_t"], m["k_t"], m["v_t"], m["v_rows_1"]
        mask_1, y1, prob_t1, a_hi1, a_lo1 = m["mask_1"], m["y1"], m["prob_t1"], m["a_hi1"], m["a_lo1"]
        conv_in, conv_mid, strip_t = m["conv_in"], m["conv_mid"], m["strip_t"]
        ada_raw, gate_conv, f_hi, f_lo, ada_sum = m["ada_raw"], m["gate_conv"], m["f_hi"], m["f_lo"], m["ada_sum"]
        q_h, k_h, c_hi, c_lo = m["q_h"], m["k_h"], m["c_hi"], m["c_lo"]
        l_hi, l_lo, o_hi, o_lo, prob_t2 = m["l_hi"], m["l_lo"], m["o_hi"], m["o_lo"], m["prob_t2"]
        v_rows_2, u = m["v_rows_2"], m["u"]
        e_hi, e_lo, comb, comb_t = m["e_hi"], m["e_lo"], m["comb"], m["comb_t"]
        router_w, router_b, rt = m["router_w"], m["router_b"], m["rt"]
        router_hi, router_lo = m["router_hi"], m["router_lo"]
        rope_cos, rope_sin, pos_raw, turn, angle = (m["rope"][:, n, :] for n in range(5))

        bank = [ctx.enter_context(nc.psum_tensor(f"bank{b}", [P, 512], F32)) for b in range(8)]
        strip_dram = nc.dram_tensor("strip_dram", [H, GELEM], F32)
        comb_dram = nc.dram_tensor("comb_dram", [G * E, SEQ], F32)

        def const(name, width=1):
            return cst[:, CONST[name]:CONST[name] + width]

        def column(name, n=0, width=1):
            return col[:, COLUMNS[name] + n:COLUMNS[name] + n + width]

        ident, flip, ones = const("ident", P), const("flip", P), const("ones", P)

        cst_loaded, col_loaded, rel_loaded = sem("cst_loaded"), sem("col_loaded"), sem("rel_loaded")
        x_loaded = [sem(f"x_loaded{n}") for n in range(2)]
        x_again = [sem(f"x_again{n}") for n in range(2)]
        slab_full = [sem(f"slab_full{w}") for w in range(W)]
        hi_done, lo_done = sem("hi_done"), sem("lo_done")
        tile_done = sem("tile_done")
        bank_free = [sem(f"bank_free{b}") for b in range(8)]
        ada_full = [sem(f"ada_full{w}") for w in range(2)]
        ada_summed, ada_done = sem("ada_summed"), sem("ada_done")
        c_ready = sem("c_ready")
        squared, summed = sem("squared"), sem("summed")
        normed, high = sem("normed"), sem("high")
        var_ready, rstd_ready = sem("var_ready"), sem("rstd_ready")
        split_done = sem("split_done")
        strip_sum, strip_stored, strip_turned = sem("strip_sum"), sem("strip_stored"), sem("strip_turned")
        bias_sum = sem("bias_sum")
        turned = sem("turned")
        dots_done, dots_used = sem("dots_done"), sem("dots_used")
        logits_done, probs_ready, probs_turned, pv_done = (
            sem("logits_done"), sem("probs_ready"), sem("probs_turned"), sem("pv_done"))
        pos_loaded, angles_ready, rope_ready = sem("pos_loaded"), sem("angles_ready"), sem("rope_ready")
        heads_ready = sem("heads_ready")
        pads_ready = sem("pads_ready")
        conv_done, mean_done, scaled, silu_done = (
            sem("conv_done"), sem("mean_done"), sem("scaled"), sem("silu_done"))
        router_loaded, router_split, routed, shift_ready, exp_ready = (
            sem("router_loaded"), sem("router_split"), sem("routed"), sem("shift_ready"), sem("exp_ready"))
        weights_ready, weights_turned, comb_stored = (
            sem("weights_ready"), sem("weights_turned"), sem("comb_stored"))
        comb_full, comb_used = [sem(f"comb_full{w}") for w in range(2)], sem("comb_used")
        out_ready, stored = sem("out_ready"), sem("stored")
        step = sem("step")

        def width(n):
            return SLABS[n][1] * SLABS[n][2]

        def parts(n):
            kc, c = SLABS[n][1:]
            return [t[:, n % W, 0:kc * c].rearrange("p (k c) -> p k c", c=c) for t in (whi, wlo)]

        def runs(eng, n0, count, body, size=2):
            whole = count // size
            if whole >= 2:
                with eng.Fori(0, whole) as i:
                    for k in range(size):
                        body(n0 + k, i, size)
            else:
                whole = 0
            for n in range(n0 + whole * size, n0 + count):
                body(n, 0, 0)

        def tile_is_done(eng, t, i=0, per=0):
            eng.wait_ge(tile_done, t + 1 + i * per)

        def tile_is_taken(eng, t, i=0, per=0):
            eng.wait_ge(bank_free[t % 4], t // 4 + 1 + i * (per // 4))

        def job_is_taken(eng, j):
            eng.wait_ge(bank_free[4 + j % 4], j // 4 + 1)

        def head_is_multiplied(eng, base_t, first, r):
            if r % H == H - 1:
                tile_is_done(eng, base_t + 2 * (r // H))
            else:
                eng.wait_ge(pv_done, first * (H - 1) // H + (H - 1) * (r // H) + r % H + 1)

        block = ctx.enter_context(nc.Block())

        @block.sync
        def _(sp):
            def load_slab(n, i=0, per=0):
                if n >= W:
                    sp.wait_ge(lo_done, n - W + 1 + i * per)
                sp.dma_start(raw[:, n % W, 0:width(n)], a["wpack"][n + i * per][:, 0:width(n)]) \
                    .then_inc(slab_full[n % W], 16)

            def load_ada(s, i=0, per=0):
                if s >= 2:
                    sp.wait_ge(ada_summed, s - 1 + i * per)
                sp.dma_start(ada_raw[:, s % 2, :], a["ada_pack"][s + i * per]).then_inc(ada_full[s % 2], 16)

            x_dram = a["x_t"].rearrange("(c p) t -> p c t", p=P)
            out_dram = out.rearrange("(c p) t -> p c t", p=P)
            sp.dma_start(x[:, 0:DC // 2, :], x_dram[:, 0:DC // 2, :]).then_inc(x_loaded[0], 16)
            sp.dma_start(cst[:], a["const"]).then_inc(cst_loaded, 16)
            sp.dma_start(x[:, DC // 2:, :], x_dram[:, DC // 2:, :]).then_inc(x_loaded[1], 16)
            sp.dma_start(col[:], a["columns"]).then_inc(col_loaded, 16)
            load_slab(0)
            load_slab(1)
            sp.dma_start(m["onehot"][:], a["onehot"]).then_inc(rel_loaded, 16)
            sp.dma_start(m["rel"][:], a["rel_bias"]).then_inc(rel_loaded, 16)
            for j in range(2):
                job_is_taken(sp, JOB["strip"] + j)
            sp.dma_start(strip_dram.ap(), m["strip"][:]).then_inc(strip_stored, 16)
            first_a = FIRST["branch_a"]
            runs(sp, 2, first_a - 2, load_slab)
            sp.wait_ge(strip_stored, 16)
            sp.wait_ge(split_done, SPLIT["conv_1"] + CC)
            sp.dma_start(strip_t[:], bass.AP(tensor=strip_dram, offset=0, ap=[[1, P], [GELEM, H], [1, SEQ]])) \
                .then_inc(strip_turned, 16)
            runs(sp, first_a, FIRST["w_out"] - first_a, load_slab)
            for half in range(2):
                for c in range(half * DC // 2, (half + 1) * DC // 2):
                    tile_is_taken(sp, TILE["branch_b"] + c)
                cs = slice(half * DC // 2, (half + 1) * DC // 2)
                sp.dma_start(x[:, cs, :], x_dram[:, cs, :]).then_inc(x_again[half], 16)
                load_slab(FIRST["w_out"] + 2 * half)
                load_slab(FIRST["w_out"] + 2 * half + 1)

            for half in range(2):
                n0, s0 = FIRST["ffn_up"] + half * (FH + DC), half * (FH + 2)
                down = n0 + FH

                def up(n, i=0, per=0, n0=n0, s0=s0):
                    load_slab(n, i, per)
                    load_ada(s0 + n - n0 - 2, i, per)

                if half == 0:
                    sp.wait_ge(bias_sum, H)
                for k in range(4):
                    load_slab(n0 + k)
                    if k < 2:
                        load_ada(s0 + k)
                runs(sp, n0 + 4, FH - 4, up)
                up(down)
                up(down + 1)
                for k in range(2, DC):
                    load_slab(down + k)
                    if half == 0 and k < 4:
                        load_ada(FH + k - 2)
                    if half == 1 and k == 3:
                        sp.wait_ge(ada_summed, ADA_SLABS)
                        sp.dma_start(pos_raw.bitcast(I32), a["positions_2"].to_broadcast([P, SEQ])) \
                            .then_inc(pos_loaded, 16)
                        sp.dma_start(pos_col_raw, a["positions_2"].rearrange("o (b p) -> p (o b)", p=P),
                                     allow_slow_non_contiguous=True).then_inc(pos_loaded, 16)
            for n in range(FIRST["latents"], FIRST["moe_up"]):
                load_slab(n)
            tile_is_done(sp, TILE["conv_out"] + DC - 1)
            sp.dma_start(router_w[:], a["router_w"]).then_inc(router_loaded, 16)
            sp.dma_start(router_b[:], a["router_b"].to_broadcast([P, G + G * E])).then_inc(router_loaded, 16)
            n0 = FIRST["moe_up"]
            load_slab(n0)
            load_slab(n0 + 1)
            job_is_taken(sp, JOB["combine"])
            sp.dma_start(comb_dram.ap(), comb_t[:]).then_inc(comb_stored, 16)
            sp.wait_ge(comb_stored, 16)

            def moe_group(i, first):
                for e in range(E):
                    if not (first and e < 2):
                        load_slab(n0 + e, i, E + 4)
                        sp.wait_ge(comb_used, e - 1 + i * E)
                    row = comb_dram.ap()[e:e + 1, :] if first else comb_dram.ap()[bass.ds(e + i * E, 1), :]
                    sp.dma_start(comb[:, e % 2, :], row.to_broadcast([P, SEQ])).then_inc(comb_full[e % 2], 16)
                for d in range(4):
                    load_slab(n0 + E + d, i, E + 4)

            moe_group(0, True)
            with sp.Fori(1, G) as i:
                moe_group(i, False)
            for c in range(DC):
                sp.wait_ge(out_ready, c + 1)
                sp.dma_start(out_dram[:, c, :], x[:, c, :]).then_inc(stored, 16)
            sp.wait_ge(stored, 16 * DC)

        @block.gpsimd
        def _(pool):
            def low_part(n, i=0, per=0):
                pool.wait_ge(hi_done, n + 1 + i * per)
                pool.tensor_tensor(wlo[:, n % W, 0:width(n)], raw[:, n % W, 0:width(n)],
                                   whi[:, n % W, 0:width(n)].bitcast(F32), ALU.subtract).then_inc(lo_done, 1)

            n = 0
            while n < NS:
                count = 1
                while n + count < NS and width(n + count) == width(n):
                    count += 1
                runs(pool, n, count, low_part)
                n += count

        @block.scalar
        def _(act):
            def high_part(n, i=0, per=0, tiles=0):
                act.wait_ge(slab_full[n % W], 16 * (n // W + 1) + i * (per // W * 16))
                if n >= W:
                    act.wait_ge(tile_done, TILE_END[n - W] + i * tiles)
                act.copy(whi[:, n % W, 0:width(n)], raw[:, n % W, 0:width(n)]).then_inc(hi_done, 1)

            def root(name):
                k = NORMS[name]
                act.wait_ge(var_ready, k + 1)
                act.activation(rstd[:, k % 2, :], rstd[:, k % 2, :], ACT.Sqrt).then_inc(rstd_ready, 1)

            made = [0]

            def highs(count, hi, shift=None):
                for c in range(count):
                    made[0] += 1
                    act.wait_ge(normed, made[0])
                    if shift is None:
                        act.copy(hi[:, c, :], tmp[:, c % 2, :]).then_inc(high, 1)
                    else:
                        act.activation(hi[:, c, :], tmp[:, c % 2, :], ACT.Identity,
                                       bias=ada[:, shift + c:shift + c + 1]).then_inc(high, 1)

            def take(out_ap, t, func, bias=0.0, i=0, per=0):
                tile_is_done(act, t, i, per)
                act.activation(out_ap, bank[t % 4][:], func, bias=bias).then_inc(bank_free[t % 4], 1)

            def attention(base_j, base_t, prob_t, first, full):
                for r in range(NB * H + 1):
                    if r < NB * H:
                        blk, h = r // H, r % H
                        w = SEQ if full else P * (blk + 1)
                        job_is_taken(act, base_j + attn_jobs(r, "logits"))
                        act.activation(square[:, r % 2, 0:w], square[:, r % 2, 0:w], ACT.Exp,
                                       bias=neg_max[:, r % 2:r % 2 + 1], scale=-1.0,
                                       accum_out=sums[:, blk, h:h + 1]).then_inc(probs_ready, 1)
                    if r >= 1:
                        s = r - 1
                        w = SEQ if full else P * (s // H + 1)
                        act.wait_ge(probs_turned, first + s + 1)
                        if s >= 2:
                            head_is_multiplied(act, base_t, first, s - 2)
                        j = base_j + attn_jobs(s, "turn")
                        act.copy(prob_t[:, s % 2, 0:w], bank[4 + j % 4][:, 0:w]).then_inc(bank_free[4 + j % 4], 1)

            def after(n, i=0, per=0, tiles=0):
                name, k = SLABS[n][0], n - FIRST[SLABS[n][0]]
                if name == "iq" and k == 1:
                    for d in range((NB - 1) * H):
                        w, j = P * (d // H + 2), JOB["dots"] + d
                        act.wait_ge(dots_done, d + 1)
                        if d >= 2:
                            act.wait_ge(dots_used, d - 1)
                        act.activation(gate[:, d % 2, 0:w], bank[4 + j % 4][:, 0:w], ACT.Relu) \
                            .then_inc(bank_free[4 + j % 4], 1)
                elif name == "gate_a":
                    for c in (2 * k, 2 * k + 1):
                        take(y1[:, c, :], TILE["gate_a"] + c, ACT.Sigmoid, column("b_gate", c))
                elif name == "gate_b":
                    for c in (2 * k, 2 * k + 1):
                        take(x[:, c, :], TILE["gate_b"] + c, ACT.Sigmoid, column("b_gate", DC + c))
                    if k == 3:
                        attention(JOB["attn_1"], TILE["attn_1"], prob_t1, 0, False)
                elif name == "w_out" and k == 3:
                    root("norm_2")
                    highs(DC, h_hi)
                    act.activation(c_act[:], column("c", 0, DC), ACT.Silu).then_inc(c_ready, 1)
                elif name == "ffn_up":
                    n0 = n - k if k < FH else FFN2
                    t = TILE["ffn_up_0" if k < FH else "ffn_up_1"] + 2 * (n - n0)
                    if n - n0 >= 2:
                        tile_is_taken(act, t - 3, i, tiles)
                    elif k < FH:
                        act.wait_ge(dots_used, (NB - 1) * H)
                    else:
                        tile_is_taken(act, TILE["ffn_up_0"] + 2 * (FH - 1 - (n - n0 + FH - 1) % 2) + 1)
                    take(gate[:, (n - n0) % 2, :], t, ACT.Silu, i=i, per=tiles)
                elif n == FFN2 + FH + DC - 1:
                    act.wait_ge(angles_ready, 1)
                    act.activation(rope_sin, angle, ACT.Sin).then_inc(rope_ready, 1)
                    act.activation(rope_cos, turn, ACT.Sin).then_inc(rope_ready, 1)
                    root("norm_3")
                    highs(DC, h_hi, shift=0)
                    root("norm_x")
                elif name == "latents" and k == 2:
                    root("norm_q")
                    highs(QC, l_hi)
                    root("norm_kv")
                    highs(KC, l_hi[:, QC:, :])
                elif name == "glu_b":
                    act.wait_ge(pads_ready, 1)
                    for c in (2 * k, 2 * k + 1):
                        take(u[:, c + 1, TAPS - 1:], TILE["glu_b"] + c, ACT.Sigmoid)
                elif name == "w_ukv":
                    for q in range(4 - 4 * k):
                        t = TILE["w_ukv"] + q
                        tile_is_done(act, t)
                        act.copy(k_h[0:HD, 2 * q, :], bank[t % 4][0:HD, :])
                        act.copy(k_h[0:HD, 2 * q + 1, :], bank[t % 4][HD:P, :]).then_inc(bank_free[t % 4], 1)
                    for blk in range(NB * k):
                        take(v_rows_2[:, blk, :], TILE["w_ukv"] + 4 + blk, ACT.Copy)
                elif name == "gate_conv":
                    if k == 0:
                        act.wait_ge(heads_ready, 3)
                    for c in (2 * k, 2 * k + 1):
                        take(gate_conv[:, c, :], TILE["gate_conv"] + c, ACT.Sigmoid)
                    if k == 3:
                        attention(JOB["attn_2"], TILE["attn_2"], prob_t2, NB * H, True)
                elif name == "gate_attn":
                    k //= 2
                    for c in (2 * k, 2 * k + 1):
                        t = TILE["o_and_gate"] + 4 * k + c % 2
                        if k:
                            tile_is_taken(act, t - 4)
                        else:
                            act.wait_ge(probs_ready, 2 * NB * H)
                            tile_is_taken(act, TILE["attn_2"] + 2 * NB - 1)
                        take(gate[:, c % 2, :], t + 2, ACT.Sigmoid)
                    if k == 1:
                        root("ln_var")
                        for c in range(CC):
                            act.wait_ge(scaled, c + 1)
                            act.activation(u[:, c, TAPS - 1:], u[:, c, TAPS - 1:], ACT.Silu,
                                           bias=column("conv_ln_b", c), scale=column("conv_ln_g", c)) \
                                .then_inc(silu_done, 1)
                elif name == "w_out_2" and k == 3:
                    root("norm_4")
                    highs(DC, h_hi, shift=3 * DC)
                    for v, n_v in ((0, G), (1, E)):
                        act.wait_ge(shift_ready, v + 1)
                        act.activation(rt[:, v, :, 0:n_v], rt[:, v, :, 0:n_v], ACT.Exp).then_inc(exp_ready, 1)
                elif name == "moe_up":
                    e = k
                    t = TILE["moe"] + 2 * e
                    tile_is_taken(act, t - 3 if e >= 2 else t - 3 - 8, i, tiles)
                    take(gate[:, e % 2, :], t, ACT.Silu, i=i, per=tiles)

            high_part(0)
            high_part(1)
            act.wait_ge(col_loaded, 16)
            root("norm_1")
            highs(DC, h_hi)
            up, moe = FIRST["ffn_up"], FIRST["moe_up"]
            for n in range(W, up + W):
                high_part(n)
                after(n - W)
            for n0 in (up, FFN2):
                for k in (0, 1):
                    high_part(n0 + W + k)
                    after(n0 + k)
                with act.Fori(0, (FH - 1 - W - 2) // 2) as i:
                    for k in (2, 3):
                        high_part(n0 + W + k, i, 2, 4)
                        after(n0 + k, i, 2, 4)
                for k in range(2 + (FH - 1 - W - 2) // 2 * 2, FH + DC):
                    high_part(n0 + W + k)
                    after(n0 + k)
            for n in range(FIRST["latents"], moe):
                high_part(n + W)
                after(n)

            def moe_group(i, per, tiles, count):
                for k in range(E + 4):
                    if k < count:
                        high_part(moe + W + k, i, per, tiles)
                    if k < E:
                        after(moe + k, i, per, tiles)

            with act.Fori(0, G - 1) as i:
                moe_group(i, E + 4, 24, E + 4)
            moe_group(G - 1, E + 4, 24, E + 4 - W)
            root("norm_out")

        @block.tensor
        def _(pe):
            def tile_bank(t, i=0, per=0):
                if t >= 4:
                    pe.wait_ge(bank_free[t % 4], t // 4 + i * (per // 4))
                return bank[t % 4]

            def job_bank(j):
                if j >= 4:
                    pe.wait_ge(bank_free[4 + j % 4], j // 4)
                return bank[4 + j % 4]

            def product(t, n, c0, rhs, i=0, per=0, tiles=0, ready=None):
                ps = tile_bank(t, i, tiles)
                hi, lo = parts(n)
                kc = SLABS[n][1]
                for k in range(kc):
                    if ready is not None:
                        pe.wait_ge(split_done, ready + k + 1 + i * per)
                    x_hi, x_lo = rhs(k)
                    wh, wl = hi[:, k, c0:c0 + P], lo[:, k, c0:c0 + P]
                    pe.matmul(ps[:], wh, x_hi, start=(k == 0), stop=False)
                    pe.matmul(ps[:], wl, x_hi, start=False, stop=False)
                    mm = pe.matmul(ps[:], wh, x_lo, start=False, stop=(k == kc - 1))
                mm.then_inc(tile_done, 1)

            def products(t, n, count, rhs, ready):
                banks = [tile_bank(t + q) for q in range(count)]
                hi, lo = parts(n)
                kc = SLABS[n][1]
                for k in range(kc):
                    pe.wait_ge(split_done, ready + k + 1)
                    x_hi, x_lo = rhs(k)
                    for q in range(count):
                        wh, wl = hi[:, k, q * P:(q + 1) * P], lo[:, k, q * P:(q + 1) * P]
                        pe.matmul(banks[q][:], wh, x_hi, start=(k == 0), stop=False)
                        pe.matmul(banks[q][:], wl, x_hi, start=False, stop=False)
                        mm = pe.matmul(banks[q][:], wh, x_lo, start=False, stop=(k == kc - 1))
                        if k == kc - 1:
                            mm.then_inc(tile_done, 1)

            def slab(n, i=0, per=0):
                pe.wait_ge(lo_done, n + 1 + i * per)

            def chunks(hi, lo):
                return lambda k: (hi[:, k, :], lo[:, k, :])

            h = chunks(h_hi, h_lo)

            def dense(name, t_name, rhs, ready=None, after_slab=None):
                n0 = FIRST[name]
                count = sum(s[0] == name for s in SLABS)
                per_slab = SLABS[n0][2] // P
                for k in range(count):
                    slab(n0 + k)
                    if k == 0 and ready is not None:
                        products(TILE[t_name], n0, per_slab, rhs, ready)
                    else:
                        for q in range(per_slab):
                            product(TILE[t_name] + k * per_slab + q, n0 + k, q * P, rhs)
                    if after_slab:
                        after_slab(k)

            def sum_squares(name, parts=square):
                b = job_bank(JOB[name])
                for part in range(2):
                    pe.wait_ge(squared, squares_done(name, part))
                    pe.matmul(b[:], ones, parts[:, part, :], start=(part == 0), stop=(part == 1)).then_inc(summed, 1)

            def attention(base_j, base_t, prob_t, first, full, q, k, v):
                def w(r):
                    return SEQ if full else P * (r // H + 1)

                def logits(r):
                    b = job_bank(base_j + attn_jobs(r, "logits"))
                    pe.matmul(b[:, 0:w(r)], q(r % H, r // H), k(r % H, w(r)), start=True, stop=True) \
                        .then_inc(logits_done, 1)

                def turn_probs(r):
                    pe.wait_ge(probs_ready, first + r + 1)
                    b = job_bank(base_j + attn_jobs(r, "turn"))
                    for s in range(w(r) // P):
                        mm = pe.transpose(b[:, s * P:(s + 1) * P], square[:, r % 2, s * P:(s + 1) * P], ident)
                    mm.then_inc(probs_turned, 1)

                def values(r):
                    hh, t = r % H, base_t + 2 * (r // H)
                    b = tile_bank(t) if hh == 0 else bank[t % 4]
                    job_is_taken(pe, base_j + attn_jobs(r, "turn"))
                    ns = w(r) // P
                    for s in range(ns):
                        mm = pe.matmul(b[:, hh * HD:(hh + 1) * HD], prob_t[:, r % 2, s * P:(s + 1) * P], v(hh, s),
                                       start=(s == 0), stop=(s == ns - 1))
                    mm.then_inc(tile_done if hh == H - 1 else pv_done, 1)

                def turn_rows(blk):
                    t = base_t + 2 * blk + 1
                    tile_is_taken(pe, t - 1)
                    b = tile_bank(t)
                    for c in range(CC):
                        mm = pe.transpose(b[:, c * P:(c + 1) * P], tmp[:, blk % 2, c * P:(c + 1) * P], ident)
                    mm.then_inc(tile_done, 1)

                logits(0)
                logits(1)
                for r in range(NB * H):
                    turn_probs(r)
                    if r + 2 < NB * H:
                        logits(r + 2)
                    if r >= 1:
                        values(r - 1)
                    if r % H == 4 and r > H:
                        turn_rows(r // H - 1)
                values(NB * H - 1)
                turn_rows(NB - 1)

            def half_rows(hh):
                return slice(HD * (hh % 2), HD * (hh % 2 + 1))

            pe.wait_ge(cst_loaded, 16)
            sum_squares("norm_1")
            pe.wait_ge(rel_loaded, 32)
            for j, (d0, d1) in enumerate(((0, SEQ), (SEQ, GELEM))):
                pe.matmul(job_bank(JOB["strip"] + j)[0:H, 0:d1 - d0], m["rel"][:], m["onehot"][:, d0:d1],
                          start=True, stop=True).then_inc(strip_sum, 1)
            dense("kv_ikw", "kv_ikw", h, ready=SPLIT["h1"])
            dense("iq", "iq", h)
            tile_is_taken(pe, TILE["kv_ikw"])
            b = job_bank(JOB["v_rows"])
            for s in range(NB):
                mm = pe.transpose(b[:, s * HD:(s + 1) * HD], v_t[HD:P, s * P:(s + 1) * P], ident[HD:P, HD:P])
            mm.then_inc(turned, 1)
            tile_is_taken(pe, TILE["kv_ikw"] + 1)
            b = job_bank(JOB["iw_rows"])
            for s in range(NB):
                mm = pe.transpose(b[:, s * H:(s + 1) * H], square[HD:HD + H, 0, s * P:(s + 1) * P],
                                  ident[HD:HD + H, HD:HD + H])
            mm.then_inc(turned, 1)
            for d in range((NB - 1) * H):
                blk, hh = d // H + 1, d % H
                if d < H and hh % 2 == 0:
                    tile_is_taken(pe, TILE["iq"] + hh // 2)
                w = P * (blk + 1)
                pe.matmul(job_bank(JOB["dots"] + d)[:, 0:w], iq_t[half_rows(hh), hh // 2, blk * P:(blk + 1) * P],
                          ik_t[half_rows(hh), 0:w], start=True, stop=True).then_inc(dots_done, 1)
            for name in ("q", "conv_c", "conv_x", "conv_b", "gate_a"):
                dense(name, name, h)
            dense("branch_a", "branch_a", chunks(a_hi1, a_lo1), ready=SPLIT["conv_1"])
            pe.wait_ge(strip_turned, 16)
            for hh in range(H):
                pe.matmul(job_bank(JOB["bias"] + hh)[:], flip, strip_t[:, hh, :], start=True, stop=True) \
                    .then_inc(bias_sum, 1)
            dense("gate_b", "gate_b", h)
            for c in range(CC):
                tile_is_taken(pe, TILE["q"] + c)
            attention(JOB["attn_1"], TILE["attn_1"], prob_t1, 0, False,
                      lambda hh, blk: q_t[half_rows(hh), hh // 2, blk * P:(blk + 1) * P],
                      lambda hh, w: k_t[half_rows(hh), 0:w],
                      lambda hh, s: v_rows_1[:, s, :])
            for blk in range(NB):
                tile_is_taken(pe, TILE["attn_1"] + 2 * blk + 1)
            dense("branch_b", "branch_b", chunks(a_hi1, a_lo1))
            dense("w_out", "w_out", h, ready=SPLIT["merged_1"])
            sum_squares("norm_2")

            for half in range(2):
                n0, t0 = (FIRST["ffn_up"], FFN2)[half], TILE[f"ffn_up_{half}"]

                def up(n, i=0, per=0, n0=n0, t0=t0):
                    slab(n, i, per)
                    for q in range(2):
                        product(t0 + 2 * (n - n0) + q, n, q * P, h, i, per, 2 * per)

                if half == 0:
                    slab(n0)
                    products(t0, n0, 2, h, SPLIT["h2"])
                runs(pe, n0 + 1 - half, FH - 1 + half, up)
                down, t0 = n0 + FH, TILE[f"ffn_down_{half}"]
                for k in range(FH):
                    pe.wait_ge(split_done, SPLIT[f"ffn_{half}"] + k + 1)

                def down_slab(n, i=0, per=0, down=down, t0=t0):
                    slab(n, i, per)
                    product(t0 + n - down, n, 0, chunks(f_hi, f_lo), i, per, per)

                if half == 0:
                    runs(pe, down, DC, down_slab, 4)
                else:
                    for c in range(DC):
                        down_slab(down + c)
                        if c == 3:
                            b = job_bank(JOB["ada"])
                            pe.wait_ge(ada_summed, ADA_SLABS)
                            for n in range(6 * DC):
                                mm = pe.matmul(b[:, n:n + 1], ada_sum[:, n // 2, n % 2 * P:(n % 2 + 1) * P], ones[:, 0:1],
                                               start=True, stop=True)
                            mm.then_inc(ada_done, 1)
            sum_squares("norm_3")
            sum_squares("norm_x", gate)

            dense("latents", "latents", h, ready=SPLIT["h3"])
            sum_squares("norm_q")
            sum_squares("norm_kv", gate)
            dense("glu_b", "glu_b", h)
            dense("glu_a", "glu_a", h)
            dense("w_uq", "w_uq", chunks(l_hi, l_lo), ready=SPLIT["q_lat"])
            n = FIRST["w_ukv"]
            slab(n)
            lat = lambda k: (l_hi[:, QC + k, :], l_lo[:, QC + k, :])
            products(TILE["w_ukv"], n, 4, lat, SPLIT["kv_lat"])
            slab(n + 1)
            for blk in range(NB):
                t = TILE["w_ukv"] + 4 + blk
                ps = tile_bank(t)
                hi, lo = parts(n + 1)
                for k in range(KC):
                    x_hi = l_hi[:, QC + k, blk * P:(blk + 1) * P]
                    x_lo = l_lo[:, QC + k, blk * P:(blk + 1) * P]
                    pe.matmul(ps[:], x_hi, hi[:, k, :], start=(k == 0), stop=False)
                    pe.matmul(ps[:], x_hi, lo[:, k, :], start=False, stop=False)
                    mm = pe.matmul(ps[:], x_lo, hi[:, k, :], start=False, stop=(k == KC - 1))
                mm.then_inc(tile_done, 1)
            dense("gate_conv", "gate_conv", h)
            pe.wait_ge(heads_ready, 3)
            for t in (4, 5, 6, 7):
                tile_is_taken(pe, TILE["w_ukv"] + t)
            attention(JOB["attn_2"], TILE["attn_2"], prob_t2, NB * H, True,
                      lambda hh, blk: q_h[0:QK_DIM, hh, blk * P:(blk + 1) * P],
                      lambda hh, w: k_h[0:QK_DIM, hh, 0:w],
                      lambda hh, s: v_rows_2[:, s, hh * HD:(hh + 1) * HD])
            for blk in range(NB):
                tile_is_taken(pe, TILE["attn_2"] + 2 * blk + 1)
            for k in range(4):
                n = FIRST["o_attn"] + 2 * k
                t = TILE["o_and_gate"] + 4 * k
                slab(n)
                for q in range(2):
                    product(t + q, n, q * P, chunks(o_hi, o_lo))
                slab(n + 1)
                for q in range(2):
                    product(t + 2 + q, n + 1, q * P, h)
                if k == 0:
                    b = job_bank(JOB["ln_mean"])
                    for c in range(CC):
                        pe.wait_ge(conv_done, c + 1)
                        mm = pe.matmul(b[:], ones, u[:, c, TAPS - 1:], start=(c == 0), stop=(c == CC - 1))
                    mm.then_inc(mean_done, 1)
                if k == 1:
                    sum_squares("ln_var")
            dense("conv_out", "conv_out", chunks(c_hi, c_lo), ready=SPLIT["conv_2"])
            dense("w_out_2", "w_out_2", h, ready=SPLIT["merged_2"])
            sum_squares("norm_4")
            def router():
                pe.wait_ge(router_split, 1)
                b = job_bank(JOB["router"])
                w = G + G * E
                for blk in range(NB):
                    cols = slice(blk * P, (blk + 1) * P)
                    for k in range(DC):
                        ps = b[:, blk * w:(blk + 1) * w]
                        pe.matmul(ps, h_hi[:, k, cols], router_hi[:, k, :], start=(k == 0), stop=False)
                        pe.matmul(ps, h_hi[:, k, cols], router_lo[:, k, :], start=False, stop=False)
                        mm = pe.matmul(ps, h_lo[:, k, cols], router_hi[:, k, :], start=False, stop=(k == DC - 1))
                mm.then_inc(routed, 1)

            n0 = FIRST["moe_up"]

            def moe_group(i, first):
                per, tiles = (0, 0) if first else (E + 4, 24)
                for e in range(E):
                    slab(n0 + e, i, per)
                    if first and e == 0:
                        products(TILE["moe"], n0, 2, h, SPLIT["h4"])
                        router()
                    else:
                        for q in range(2):
                            product(TILE["moe"] + 2 * e + q, n0 + e, q * P, h, i, 0, tiles)
                    if first and e == 1:
                        pe.wait_ge(weights_ready, 1)
                        b = job_bank(JOB["combine"])
                        for blk in range(NB):
                            mm = pe.transpose(b[0:G * E, blk * P:(blk + 1) * P],
                                              rt[:, 2, blk, :], ident)
                        mm.then_inc(weights_turned, 1)
                for d in range(4):
                    n = n0 + E + d
                    slab(n, i, per)
                    for q in range(2):
                        product(TILE["moe"] + 2 * (E + d) + q, n, q * P, chunks(e_hi, e_lo), i,
                                E if not first else 0, tiles,
                                ready=SPLIT["moe"] if d == 0 and q == 0 else None)

            moe_group(0, True)
            with pe.Fori(1, G) as i:
                moe_group(i, False)
            sum_squares("norm_out")

        @block.vector
        def _(dve):
            class Steps:
                n, i, per = 0, 0, 0

            def link(ins):
                Steps.n += 1
                ins.then_inc(step, 1)
                dve.wait_ge(step, Steps.n + Steps.i * Steps.per)

            def loop_runs(n0, count, body, size, steps):
                whole = count // size
                base = Steps.n
                with dve.Fori(0, whole) as i:
                    Steps.i, Steps.per = i, size * steps
                    for k in range(size):
                        body(n0 + k, i, size)
                assert Steps.n - base == size * steps
                Steps.n, Steps.i, Steps.per = base + whole * size * steps, 0, 0
                for n in range(n0 + whole * size, n0 + count):
                    body(n, 0, 0)

            def take(ins, t, i=0, per=0):
                ins.then_inc(bank_free[t % 4], 1)
                tile_is_taken(dve, t, i, per)

            def take_job(ins, j):
                ins.then_inc(bank_free[4 + j % 4], 1)
                job_is_taken(dve, j)

            def split(src, hi, lo):
                link(dve.tensor_copy(hi, src))
                dve.tensor_tensor(lo, src, hi.bitcast(F32), ALU.subtract).then_inc(split_done, 1)

            def squares(name, c, count, src, gain=None, parts=square):
                if c == 0 and parts is square and NORMS[name]:
                    dve.wait_ge(summed, 2 * NORMS[name])
                part = parts[:, 0 if c == 0 else 1, :]
                ins = (dve.tensor_tensor(part, src, src, ALU.mult) if gain is None else
                       dve.scalar_tensor_tensor(part, src, gain, src, ALU.mult, ALU.mult))
                if c == count - 1:
                    ins.then_inc(squared, 1)
                    return
                if c:
                    link(ins)
                    ins = dve.tensor_tensor(parts[:, 0, :], parts[:, 0, :], part, ALU.add)
                if c == count - 2:
                    ins.then_inc(squared, 1)
                    dve.wait_ge(squared, squares_done(name, 0))
                else:
                    link(ins)

            def root_of(name, wait=True):
                k = NORMS[name]
                dve.reciprocal(rstd[:, k % 2, :], rstd[:, k % 2, :]).then_inc(var_ready, 1)
                if wait:
                    dve.wait_ge(rstd_ready, k + 1)

            def variance(name, count):
                k = NORMS[name]
                dve.wait_ge(summed, 2 * k + 2)
                j = JOB[name]
                take_job(dve.tensor_scalar(rstd[:, k % 2, :], bank[4 + j % 4][:], 1.0 / (count * P), EPS,
                                           ALU.mult, ALU.add), j)
                root_of(name)

            made = [0]

            def normalized(name, first, count, src, gain, hi, lo, shift=None):
                def low(c):
                    dve.wait_ge(high, made[0] + c + 1)
                    t, t_hi = tmp[:, c % 2, :], hi[:, c, :].bitcast(F32)
                    ins = (dve.tensor_tensor(lo[:, c, :], t, t_hi, ALU.subtract) if shift is None else
                           dve.scalar_tensor_tensor(lo[:, c, :], t, ada[:, shift + c:shift + c + 1], t_hi,
                                                    ALU.add, ALU.subtract))
                    ins.then_inc(split_done, 1)

                for c in range(count):
                    if c >= 2:
                        low(c - 2)
                        dve.wait_ge(split_done, first + c - 1)
                    normalize(name, src(c), gain(c), tmp[:, c % 2, :]).then_inc(normed, 1)
                low(count - 2)
                low(count - 1)
                dve.wait_ge(split_done, first + count)
                made[0] += count

            def normalize(name, src, gain, out_ap):
                return dve.scalar_tensor_tensor(out_ap, src, gain, rstd[:, NORMS[name] % 2, :], ALU.mult, ALU.mult)

            def tile(t, i=0, per=0):
                tile_is_done(dve, t, i, per)
                return bank[t % 4]

            def attention_logits(r, base_j, first, full):
                blk, hh = r // H, r % H
                w = SEQ if full else P * (blk + 1)
                j = base_j + attn_jobs(r, "logits")
                b = bank[4 + j % 4]
                dve.wait_ge(logits_done, first + r + 1)
                if r >= 2:
                    dve.wait_ge(probs_turned, first + r - 1)
                p = square[:, r % 2, 0:w]
                if full:
                    dve.tensor_tensor_reduce(p, b[:, 0:w], gate[:, blk % 2, :], -float(QK_DIM) ** -0.5, 3e38,
                                             ALU.add, ALU.min, neg_max[:, r % 2:r % 2 + 1]) \
                        .then_inc(bank_free[4 + j % 4], 1)
                else:
                    off = P * blk * (blk + 1) // 2
                    link(dve.tensor_tensor(p, b[:, 0:w], bias[:, hh, SEQ - w:], ALU.add))
                    dve.tensor_tensor_reduce(p, p, mask_1[:, off:off + w], -1.0, 3e38,
                                             ALU.add, ALU.min, neg_max[:, r % 2:r % 2 + 1]) \
                        .then_inc(bank_free[4 + j % 4], 1)

            def attention_rows(blk, base_t, first):
                dve.wait_ge(probs_ready, first + H * (blk + 1))
                link(dve.reciprocal(inv_sums[:, blk, :], sums[:, blk, :]))
                t = base_t + 2 * blk
                take(dve.tensor_tensor(tmp[:, blk % 2, :].rearrange("p (h d) -> p h d", d=HD),
                                       tile(t)[:].rearrange("p (h d) -> p h d", d=HD),
                                       inv_sums[:, blk, :].unsqueeze(2).to_broadcast([P, H, HD]), ALU.mult), t)

            def attention_split(blk, base_t, hi, lo):
                t = base_t + 2 * blk + 1
                b = tile(t)[:].rearrange("p (c t) -> p c t", t=P)
                cols = slice(blk * P, (blk + 1) * P)
                link(dve.tensor_copy(hi[:, :, cols], b))
                take(dve.tensor_tensor(lo[:, :, cols], b, hi[:, :, cols].bitcast(F32), ALU.subtract), t)

            def attention(base_j, base_t, first, full, hi, lo, before=None, between=None):
                for r in range(NB * H):
                    if before and r % H == 0:
                        before(r // H)
                    attention_logits(r, base_j, first, full)
                    if r % H == 2 and r > H:
                        attention_rows(r // H - 1, base_t, first)
                    if r % H == 6 and r > H:
                        attention_split(r // H - 1, base_t, hi, lo)
                    if between:
                        between()
                attention_rows(NB - 1, base_t, first)
                attention_split(NB - 1, base_t, hi, lo)

            for c in range(DC):
                if c % (DC // 2) == 0:
                    dve.wait_ge(x_loaded[c // (DC // 2)], 16)
                squares("norm_1", c, DC, x[:, c, :])
            dve.wait_ge(col_loaded, 16)
            variance("norm_1", DC)
            normalized("norm_1", SPLIT["h1"], DC, lambda c: x[:, c, :], lambda c: column("g_mix", c), h_hi, h_lo)
            dve.wait_ge(strip_sum, 2)
            for j, (d0, d1) in enumerate(((0, SEQ), (SEQ, GELEM))):
                jj = JOB["strip"] + j
                take_job(dve.tensor_copy(m["strip"][:, d0:d1], bank[4 + jj % 4][0:H, 0:d1 - d0]), jj)
            t = TILE["kv_ikw"]
            b = tile(t)
            dve.tensor_copy(k_t[0:HD, :], b[0:HD, :])
            dve.tensor_copy(k_t[HD:P, :], b[0:HD, :])
            take(dve.tensor_copy(v_t[HD:P, :], b[HD:P, :]), t)
            b = tile(t + 1)
            dve.tensor_copy(ik_t[0:HD, :], b[0:HD, :])
            dve.tensor_copy(ik_t[HD:P, :], b[0:HD, :])
            take(dve.tensor_scalar(square[HD:HD + H, 0, :], b[HD:HD + H, :], H ** -0.5 * HD ** -0.5, None, ALU.mult), t + 1)
            for c in range(CC):
                t = TILE["iq"] + c
                take(dve.tensor_copy(iq_t[:, c, :], tile(t)[:]), t)
            for n, (dst, name) in enumerate(((v_rows_1[:], "v_rows"), (iw_rows, "iw_rows"))):
                j = JOB[name]
                dve.wait_ge(turned, n + 1)
                w = dst.shape[2] * NB
                take_job(dve.tensor_copy(dst, bank[4 + j % 4][:, 0:w].rearrange("p (b d) -> p b d", b=NB)), j)
            score_at = {blk: (P * (blk * (blk + 1) // 2 - 1), P * (blk + 1)) for blk in range(1, NB)}
            for d in range((NB - 1) * H):
                blk, hh = d // H + 1, d % H
                off, w = score_at[blk]
                sc = score[:, off:off + w]
                job_is_taken(dve, JOB["dots"] + d)
                iw = iw_rows[:, blk, hh:hh + 1]
                if hh == 0:
                    dve.tensor_scalar(sc, gate[:, d % 2, 0:w], iw, None, ALU.mult).then_inc(dots_used, 1)
                else:
                    dve.scalar_tensor_tensor(sc, gate[:, d % 2, 0:w], iw, sc, ALU.mult, ALU.add).then_inc(dots_used, 1)
                dve.wait_ge(dots_used, d + 1)
                if hh == H - 1:
                    link(dve.scalar_tensor_tensor(sc[:, w - P:w], const("after", P), FILL, sc[:, w - P:w],
                                                  ALU.mult, ALU.add))
            link(dve.tensor_scalar(mask_1[:, 0:P], const("after", P), NEG, None, ALU.mult))

            def top_k():
                for blk in range(1, NB):
                    off, w = score_at[blk]
                    src, dst = score[:, off:off + w], work[:, off:off + w]
                    for n in range(K_TOP // 8):
                        link(dve.max(top8, src if n == 0 else dst))
                        link(dve.match_replace(dst, top8, src if n == 0 else dst, TAKEN))
                        yield
                    mk = mask_1[:, off + P:off + P + w]
                    link(dve.tensor_tensor(mk, dst, src, ALU.is_equal))
                    link(dve.tensor_scalar(mk, mk, NEG, None, ALU.mult))
                    yield

            def advance(work_left, n):
                for _ in range(n):
                    next(work_left, None)

            selection = top_k()
            for c in range(CC):
                t = TILE["q"] + c
                take(dve.tensor_scalar(q_t[:, c, :], tile(t)[:], HD ** -0.5, None, ALU.mult), t)
                advance(selection, 3)
            dve.wait_ge(strip_stored, 16)
            link(dve.memset(conv_in[:, :, 0:2], 0.0))
            for c in range(CC):
                t = TILE["conv_c"] + c
                take(dve.tensor_copy(conv_in[:, c, 2:], tile(t)[:]), t)
                advance(selection, 4)
            for c in range(CC):
                t = TILE["conv_x"] + c
                take(dve.tensor_tensor(conv_in[:, c, 2:], conv_in[:, c, 2:], tile(t)[:], ALU.mult), t)
                advance(selection, 4)
            for c in range(CC):
                mid = conv_mid[:, c % 2, :]
                for tap in range(3):
                    src, w_tap = conv_in[:, c, tap:tap + SEQ], column("conv_w", tap * CC + c)
                    link(dve.tensor_scalar(mid, src, w_tap, None, ALU.mult) if tap == 0 else
                         dve.scalar_tensor_tensor(mid, src, w_tap, mid, ALU.mult, ALU.add))
                t = TILE["conv_b"] + c
                take(dve.tensor_tensor(tmp[:, c % 2, :], mid, tile(t)[:], ALU.mult), t)
                split(tmp[:, c % 2, :], a_hi1[:, c, :], a_lo1[:, c, :])
                advance(selection, 1)
            advance(selection, 100)
            for c in range(DC):
                t = TILE["branch_a"] + c
                tile_is_taken(dve, TILE["gate_a"] + c)
                take(dve.tensor_tensor(y1[:, c, :], y1[:, c, :], tile(t)[:], ALU.mult), t)
            for hh in range(H):
                j = JOB["bias"] + hh
                dve.wait_ge(bias_sum, hh + 1)
                take_job(dve.tensor_copy(bias[:, hh, :], bank[4 + j % 4][:]), j)
            attention(JOB["attn_1"], TILE["attn_1"], 0, False, a_hi1, a_lo1)
            for c in range(DC):
                t = TILE["branch_b"] + c
                tile_is_taken(dve, TILE["gate_b"] + c)
                take(dve.tensor_tensor(tmp[:, c % 2, :], x[:, c, :], tile(t)[:], ALU.mult), t)
                link(dve.tensor_tensor(tmp[:, c % 2, :], tmp[:, c % 2, :], y1[:, c, :], ALU.add))
                split(tmp[:, c % 2, :], h_hi[:, c, :], h_lo[:, c, :])
            for c in range(DC):
                t = TILE["w_out"] + c
                if c % (DC // 2) == 0:
                    dve.wait_ge(x_again[c // (DC // 2)], 16)
                take(dve.tensor_tensor(x[:, c, :], x[:, c, :], tile(t)[:], ALU.add), t)
                squares("norm_2", c, DC, x[:, c, :])
            variance("norm_2", DC)
            normalized("norm_2", SPLIT["h2"], DC, lambda c: x[:, c, :], lambda c: column("g_ffn", c), h_hi, h_lo)
            link(dve.tensor_tensor(g_final_2[:], column("g_final", 0, DC), column("g_final", 0, DC), ALU.mult))
            dve.wait_ge(c_ready, 1)

            def modulation(s, i=0, per=0, slot=0):
                dve.wait_ge(ada_full[slot], 16 * (s // 2 + 1) + i * (per // 2 * 16))
                w_ada = ada_raw[:, slot, :].rearrange("p (k c) -> p k c", c=256)
                total = ada_sum[:, bass.ds(s + i * per, 1), :].rearrange("p a c -> p (a c)")
                for k in range(DC):
                    if k == 0:
                        ins = dve.tensor_scalar(total, w_ada[:, k, :], c_act[:, k:k + 1], None, ALU.mult)
                    else:
                        ins = dve.scalar_tensor_tensor(total, w_ada[:, k, :], c_act[:, k:k + 1], total, ALU.mult, ALU.add)
                    if k < DC - 1:
                        link(ins)
                    else:
                        ins.then_inc(ada_summed, 1)

            def rotary_angles():
                dve.wait_ge(pos_loaded, 32)
                link(dve.tensor_copy(pos_row[:], pos_raw.bitcast(I32)))
                link(dve.tensor_copy(pos_col, pos_col_raw))
                link(dve.tensor_scalar(angle, pos_row[:], const("inv_freq"), None, ALU.mult))
                link(dve.tensor_scalar(turn, angle, 1.0 / (2.0 * np.pi), 12582912.0, ALU.mult, ALU.add))
                link(dve.tensor_scalar(turn, turn, -12582912.0, None, ALU.add))
                for part in (6.28125, 0.0019359588623046875, 2.0 * np.pi - 6.28125 - 0.0019359588623046875):
                    link(dve.scalar_tensor_tensor(angle, turn, -part, angle, ALU.mult, ALU.add))
                link(dve.tensor_scalar(turn, angle, np.pi / 2, None, ALU.add))
                link(dve.tensor_scalar(pos_raw, turn, np.pi, -2.0 * np.pi, ALU.is_gt, ALU.mult))
                link(dve.tensor_tensor(turn, turn, pos_raw, ALU.add))
                link(dve.tensor_scalar(turn, turn, 3.1415925, -3.1415925, ALU.min, ALU.max))
                dve.tensor_scalar(angle, angle, 3.1415925, -3.1415925, ALU.min, ALU.max).then_inc(angles_ready, 1)

            for half in range(2):
                n0, t0, s0 = (FIRST["ffn_up"], FFN2)[half], TILE[f"ffn_up_{half}"], half * (FH + 2)

                def up(n, i=0, per=0, n0=n0, t0=t0, s0=s0):
                    k, t = n - n0, t0 + 2 * (n - n0)
                    tile_is_taken(dve, t, i, 2 * per)
                    take(dve.tensor_tensor(tmp[:, k % 2, :], gate[:, k % 2, :], tile(t + 1, i, 2 * per)[:], ALU.mult),
                         t + 1, i, 2 * per)
                    chunk = bass.ds(k + i * per, 1)
                    split(tmp[:, k % 2, :], f_hi[:, chunk, :].rearrange("p a t -> p (a t)"),
                          f_lo[:, chunk, :].rearrange("p a t -> p (a t)"))
                    modulation(s0 + k, i, per, (s0 + k) % 2)

                loop_runs(n0, FH, up, 2, DC)
                down, t0 = n0 + FH, TILE[f"ffn_down_{half}"]

                def add_down(n, i=0, per=0, down=down, t0=t0):
                    t, chunk = t0 + n - down, bass.ds(n - down + i * per, 1)
                    xc = x[:, chunk, :].rearrange("p a t -> p (a t)")
                    take(dve.tensor_tensor(xc, xc, tile(t, i, per)[:], ALU.add), t, i, per)

                if half == 0:
                    for c in range(DC):
                        add_down(down + c)
                        if c in (4, 5):
                            modulation(FH + c - 4, slot=(FH + c - 4) % 2)
                else:
                    for c in range(DC):
                        add_down(down + c)
                        squares("norm_3", c, DC, x[:, c, :], gain=g_final_2[:, c:c + 1])
                        squares("norm_x", c, DC, x[:, c, :], parts=gate)
                        if c == 4:
                            rotary_angles()
                        if c == 5:
                            dve.wait_ge(ada_done, 1)
                            j = JOB["ada"]
                            take_job(dve.tensor_tensor(ada[:], bank[4 + j % 4][:, 0:6 * DC], column("ada_b", 0, 6 * DC),
                                                       ALU.add), j)
                            for n, (at, gain) in enumerate(((DC, "norm1_g"), (4 * DC, "norm2_g"))):
                                link(dve.tensor_scalar(mod[:, n, :], ada[:, at:at + DC], 1.0, None, ALU.add))
                                link(dve.tensor_tensor(mod[:, n, :], mod[:, n, :], column(gain, 0, DC), ALU.mult))
                            link(dve.tensor_tensor(mod[:, 0, :], mod[:, 0, :], column("g_final", 0, DC), ALU.mult))

            r_3, r_x = rstd[:, NORMS["norm_3"] % 2, :], rstd[:, NORMS["norm_x"] % 2, :]
            bank_b, bank_a = bank[4 + JOB["norm_3"] % 4], bank[4 + JOB["norm_x"] % 4]
            dve.wait_ge(summed, 2 * NORMS["norm_x"] + 2)
            link(dve.tensor_scalar(r_3, bank_a[:], EPS / D, EPS * EPS, ALU.mult, ALU.add))
            take_job(dve.scalar_tensor_tensor(r_3, bank_b[:], 1.0 / D, r_3, ALU.mult, ALU.add), JOB["norm_3"])
            root_of("norm_3")
            normalized("norm_3", SPLIT["h3"], DC, lambda c: x[:, c, :], lambda c: mod[:, 0, c:c + 1], h_hi, h_lo, shift=0)
            take_job(dve.tensor_scalar(r_x, bank_a[:], 1.0 / D, EPS, ALU.mult, ALU.add), JOB["norm_x"])
            root_of("norm_x")
            for c in range(DC):
                normalize("norm_x", x[:, c, :], column("g_final", c), x[:, c, :])
            dve.memset(u[:, :, 0:TAPS - 1], 0.0).then_inc(pads_ready, 1)
            dve.wait_ge(pads_ready, 1)
            for c in range(QC + KC):
                t = TILE["latents"] + c
                take(dve.tensor_copy(q_h[:, c, :], tile(t)[:]), t)
                if c < QC:
                    squares("norm_q", c, QC, q_h[:, c, :])
                else:
                    squares("norm_kv", c - QC, KC, q_h[:, c, :], parts=gate)
            dve.wait_ge(rope_ready, 2)
            link(dve.tensor_scalar(rope_sin, rope_sin, const("rope_sign"), None, ALU.mult))

            def rotate(t, rows):
                take(dve.tensor_copy(turn[0:rows, :], tile(t)[0:rows, :]), t)
                link(dve.stream_shuffle(angle[0:rows, :], turn[0:rows, :],
                                        [(r + ROPE // 2) % ROPE for r in range(ROPE)]))
                link(dve.tensor_tensor(turn[0:rows, :], turn[0:rows, :], rope_cos[0:rows, :], ALU.mult))
                link(dve.tensor_tensor(angle[0:rows, :], angle[0:rows, :], rope_sin[0:rows, :], ALU.mult))

            rotate(TILE["latents"] + QC + KC, ROPE)
            link(dve.tensor_tensor(k_h[HD:QK_DIM, 0, :], turn[0:ROPE, :], angle[0:ROPE, :], ALU.add))
            dve.tensor_copy(k_h[HD:QK_DIM, 1:, :], k_h[HD:QK_DIM, 0:1, :].to_broadcast([ROPE, H - 1, SEQ])) \
                .then_inc(heads_ready, 1)
            for name, c0, count in (("q", 0, QC), ("kv", QC, KC)):
                variance("norm_" + name, count)
                normalized("norm_" + name, SPLIT[name + "_lat"], count, lambda c: q_h[:, c0 + c, :], lambda c: column(name + "_norm_g", c),
                           l_hi[:, c0:, :], l_lo[:, c0:, :])
            for c in range(CC):
                t = TILE["glu_a"] + c
                tile_is_taken(dve, TILE["glu_b"] + c)
                take(dve.tensor_tensor(u[:, c + 1, TAPS - 1:], u[:, c + 1, TAPS - 1:], tile(t)[:], ALU.mult), t)

            def convolution():
                for c in range(CC):
                    dst = u[:, c, TAPS - 1:]
                    for tap in range(TAPS):
                        src, w_tap = u[:, c + 1, tap:tap + SEQ], column("conv_w_2", tap * CC + c)
                        if tap == 0:
                            link(dve.tensor_scalar(dst, src, w_tap, column("conv_b", c), ALU.mult, ALU.add))
                        elif tap < TAPS - 1:
                            link(dve.scalar_tensor_tensor(dst, src, w_tap, dst, ALU.mult, ALU.add))
                        else:
                            dve.scalar_tensor_tensor(dst, src, w_tap, dst, ALU.mult, ALU.add).then_inc(conv_done, 1)
                            dve.wait_ge(conv_done, c + 1)
                        yield

            taps = convolution()

            def two_heads(dst, h0, t):
                b = tile(t)
                dve.tensor_copy(dst[0:HD, h0, :], b[0:HD, :])
                take(dve.tensor_copy(dst[0:HD, h0 + 1, :], b[HD:P, :]), t)

            for half in range(2):
                t = TILE["w_uq"] + 3 * half
                for q in range(2):
                    two_heads(q_h, 4 * half + 2 * q, t + q)
                rotate(t + 2, P)
                for q in range(4):
                    ins = dve.tensor_tensor(q_h[HD:QK_DIM, 4 * half + q, :], turn[32 * q:32 * (q + 1), :],
                                            angle[32 * q:32 * (q + 1), :], ALU.add)
                ins.then_inc(heads_ready, 1)
                dve.wait_ge(heads_ready, 2 + half)
            advance(taps, 60)

            def mask(blk):
                link(dve.tensor_scalar(gate[:, blk % 2, :], pos_row[:], pos_col[:, blk:blk + 1], NEG, ALU.is_gt, ALU.mult))

            attention(JOB["attn_2"], TILE["attn_2"], NB * H, True, o_hi, o_lo, before=mask,
                      between=lambda: advance(taps, 2))
            advance(taps, 200)

            def gated(k):
                for c in (2 * k, 2 * k + 1):
                    t = TILE["o_and_gate"] + 4 * k + c % 2
                    tile_is_taken(dve, t + 2)
                    take(dve.tensor_tensor(q_h[:, c, :], gate[:, c % 2, :], tile(t)[:], ALU.mult), t)

            gated(0)
            mean = prob_t2[:, 0, :]
            j = JOB["ln_mean"]
            dve.wait_ge(mean_done, 1)
            take_job(dve.tensor_scalar(mean, bank[4 + j % 4][:], 1.0 / (CC * P), None, ALU.mult), j)
            for c in range(CC):
                link(dve.tensor_tensor(u[:, c, TAPS - 1:], u[:, c, TAPS - 1:], mean, ALU.subtract))
                squares("ln_var", c, CC, u[:, c, TAPS - 1:])
            gated(1)
            variance("ln_var", CC)
            for c in range(CC):
                dve.tensor_tensor(u[:, c, TAPS - 1:], u[:, c, TAPS - 1:], rstd[:, NORMS["ln_var"] % 2, :],
                                  ALU.mult).then_inc(scaled, 1)
            gated(2)
            for c in range(CC):
                dve.wait_ge(silu_done, c + 1)
                split(u[:, c, TAPS - 1:], c_hi[:, c, :], c_lo[:, c, :])
            gated(3)
            for c in range(DC):
                t = TILE["conv_out"] + c
                tile_is_taken(dve, TILE["gate_conv"] + c)
                take(dve.tensor_tensor(tmp[:, c % 2, :], gate_conv[:, c, :], tile(t)[:], ALU.mult), t)
                link(dve.tensor_tensor(tmp[:, c % 2, :], tmp[:, c % 2, :], q_h[:, c, :], ALU.add))
                split(tmp[:, c % 2, :], h_hi[:, c, :], h_lo[:, c, :])
            for c in range(DC):
                t = TILE["w_out_2"] + c
                take(dve.scalar_tensor_tensor(x[:, c, :], tile(t)[:], ada[:, 2 * DC + c:2 * DC + c + 1], x[:, c, :],
                                              ALU.mult, ALU.add), t)
                squares("norm_4", c, DC, x[:, c, :])
            dve.wait_ge(router_loaded, 32)
            link(dve.tensor_copy(router_hi[:], router_w[:]))
            dve.tensor_tensor(router_lo[:], router_w[:], router_hi[:].bitcast(F32), ALU.subtract).then_inc(router_split, 1)
            variance("norm_4", DC)
            normalized("norm_4", SPLIT["h4"], DC, lambda c: x[:, c, :], lambda c: mod[:, 1, c:c + 1], h_hi, h_lo, shift=3 * DC)

            def small(v, n):
                return rt[:, v, :, 0:n]

            def wide(t, n):
                return t.to_broadcast([P, NB, n])

            def first_best(values, best, n, key, out_ap):
                link(dve.tensor_tensor(key, values, wide(best, n), ALU.is_equal))
                link(dve.tensor_tensor(key, key, const("ramp", n).unsqueeze(1).to_broadcast([P, NB, n]), ALU.mult))
                link(dve.tensor_reduce(small(13, 1), key, AX.X, ALU.max))
                link(dve.tensor_tensor(out_ap, key, wide(small(13, 1), n), ALU.is_equal))

            dve.wait_ge(routed, 1)
            j = JOB["router"]
            logits_g, logits_e = small(3, G), small(4, G * E)
            b = bank[4 + j % 4][:, 0:NB * 36].rearrange("p (b e) -> p b e", b=NB)
            link(dve.tensor_tensor(logits_g, b[:, :, 0:G], router_b[:, 0:G].unsqueeze(1).to_broadcast([P, NB, G]), ALU.add))
            take_job(dve.tensor_tensor(logits_e, b[:, :, G:], router_b[:, G:].unsqueeze(1).to_broadcast([P, NB, G * E]),
                                       ALU.add), j)
            best, group, key = small(5, 1), small(6, G), small(12, E)
            link(dve.tensor_reduce(best, logits_g, AX.X, ALU.max))
            dve.tensor_tensor(small(0, G), logits_g, wide(best, G), ALU.subtract).then_inc(shift_ready, 1)
            first_best(logits_g, best, G, small(12, G), group)
            four = rt[:, 2, :, :].rearrange("p b (g e) -> p b g e", g=G)
            link(dve.tensor_tensor(four, logits_e.rearrange("p b (g e) -> p b g e", g=G),
                                   group.unsqueeze(3).to_broadcast([P, NB, G, E]), ALU.mult))
            chosen, best_e = small(7, E), small(8, 1)
            link(dve.tensor_reduce(chosen, rt[:, 2, :, :].rearrange("p b (g e) -> p b e g", g=G), AX.X, ALU.add))
            link(dve.tensor_reduce(best_e, chosen, AX.X, ALU.max))
            dve.tensor_tensor(small(1, E), chosen, wide(best_e, E), ALU.subtract).then_inc(shift_ready, 1)
            top, second, rest = small(9, E), small(10, E), small(11, E)
            first_best(chosen, best_e, E, key, top)
            link(dve.scalar_tensor_tensor(rest, top, NEG, chosen, ALU.mult, ALU.add))
            link(dve.tensor_reduce(best_e, rest, AX.X, ALU.max))
            first_best(rest, best_e, E, key, second)
            link(dve.tensor_tensor(top, top, second, ALU.add))
            dve.wait_ge(exp_ready, 2)
            total, scale_w = small(5, 1), small(8, 1)
            link(dve.tensor_reduce(total, small(0, G), AX.X, ALU.add))
            link(dve.tensor_tensor(top, top, small(1, E), ALU.mult))
            link(dve.tensor_reduce(scale_w, top, AX.X, ALU.add))
            link(dve.tensor_tensor(scale_w, scale_w, total, ALU.mult))
            link(dve.reciprocal(scale_w, scale_w))
            link(dve.tensor_tensor(top, top, wide(scale_w, E), ALU.mult))
            dve.tensor_tensor(four, top.unsqueeze(2).to_broadcast([P, NB, G, E]),
                              group.unsqueeze(3).to_broadcast([P, NB, G, E]), ALU.mult).then_inc(weights_ready, 1)
            dve.wait_ge(weights_turned, 1)
            j = JOB["combine"]
            dve.tensor_copy(comb_t[:], bank[4 + j % 4][0:G * E, :]).then_inc(bank_free[4 + j % 4], 1)

            def moe_group(i, last):
                for e in range(E):
                    t = TILE["moe"] + 2 * e
                    tile_is_taken(dve, t, i, 24)
                    take(dve.tensor_tensor(tmp[:, e % 2, :], gate[:, e % 2, :], tile(t + 1, i, 24)[:], ALU.mult),
                         t + 1, i, 24)
                    dve.wait_ge(comb_full[e % 2], 16 * (e // 2 + 1) + i * (E // 2 * 16))
                    dve.tensor_tensor(tmp[:, e % 2, :], tmp[:, e % 2, :], comb[:, e % 2, :], ALU.mult) \
                        .then_inc(comb_used, 1)
                    dve.wait_ge(comb_used, e + 1 + i * E)
                    split(tmp[:, e % 2, :], e_hi[:, e, :], e_lo[:, e, :])
                for c in range(DC):
                    t = TILE["moe"] + 2 * E + c
                    take(dve.scalar_tensor_tensor(x[:, c, :], tile(t, i, 24)[:], ada[:, 5 * DC + c:5 * DC + c + 1],
                                                  x[:, c, :], ALU.mult, ALU.add), t, i, 24)
                    if last:
                        squares("norm_out", c, DC, x[:, c, :])

            base = Steps.n
            with dve.Fori(0, G - 1) as i:
                Steps.i, Steps.per = i, E
                moe_group(i, False)
            assert Steps.n - base == E
            Steps.n, Steps.i, Steps.per = base + (G - 1) * E, 0, 0
            moe_group(G - 1, True)
            variance("norm_out", DC)
            for c in range(DC):
                normalize("norm_out", x[:, c, :], column("final_norm_g", c), x[:, c, :]).then_inc(out_ready, 1)


def bucket_of(distance):
    n = np.maximum(distance, 0)
    large = MAX_EXACT + (np.log(np.maximum(n, 1) / MAX_EXACT) / np.log(MAX_DISTANCE / MAX_EXACT)
                         * (N_BUCKETS - MAX_EXACT)).astype(np.int64)
    return np.where(n < MAX_EXACT, n, np.minimum(large, N_BUCKETS - 1))


def constants():
    c = np.zeros((P, CONST["end"]), np.float32)
    i = np.arange(P)
    c[:, CONST["ident"]:][:, :P] = i[:, None] == i[None, :]
    c[:, CONST["flip"]:][:, :P] = i[:, None] == P - 1 - i[None, :]
    c[:, CONST["ones"]:][:, :P] = 1.0
    c[:, CONST["after"]:][:, :P] = i[None, :] > i[:, None]
    c[:, CONST["ramp"]:][:, :E] = E - np.arange(E)
    c[:, CONST["inv_freq"]] = np.float32(10000.0) ** (-(np.arange(P) % (ROPE // 2) * 2).astype(np.float32) / np.float32(ROPE))
    c[:, CONST["rope_sign"]] = np.where(i % ROPE < ROPE // 2, -1.0, 1.0)
    onehot = bucket_of(SEQ - 1 - np.arange(GELEM))[None, :] == np.arange(N_BUCKETS)[:, None]
    return c, onehot.astype(np.float32)


def lay_out_slabs(v):
    w_in, w_in_2 = v["w_in"][0], v["w_in_2"][0]
    gate_up = [v["w_ffn_gate"][0], v["w_ffn_up"][0]]
    w_uq, w_ukv = v["w_uq_2"][0], v["w_ukv_2"][0]
    at_in = np.cumsum([0, 512, 512, 512, 512, 64, 64, 512, 64, 8, D, D])
    at_in2 = np.cumsum([0, Q_RANK, KV_RANK, ROPE, 512, 512, D, D])
    pack = np.zeros((NS, P, SLAB), np.float32)

    def put(n, blocks):
        kc, c = SLABS[n][1:]
        dst = pack[n, :, :kc * c].reshape(P, kc, c)
        c0 = 0
        for b in blocks:
            dst[:, :, c0:c0 + b.shape[1]] = b.reshape(kc, P, b.shape[1]).transpose(1, 0, 2)
            c0 += b.shape[1] if b.shape[1] % HD == 0 else P - c0 % P
    count = {}
    for n, (name, kc, c) in enumerate(SLABS):
        k = count[name] = count.get(name, -1) + 1
        cols = slice(k * c, (k + 1) * c)
        if name == "kv_ikw":
            put(n, [w_in[:, at_in[4]:at_in[6]], w_in[:, at_in[7]:at_in[8]], w_in[:, at_in[8]:at_in[9]]])
        elif name in ("iq", "q", "conv_c", "conv_x", "conv_b", "gate_a", "gate_b"):
            first = at_in[{"conv_b": 0, "conv_c": 1, "conv_x": 2, "q": 3, "iq": 6, "gate_a": 9, "gate_b": 10}[name]]
            put(n, [w_in[:, first + k * c:first + (k + 1) * c]])
        elif name in ("branch_a", "branch_b", "w_out"):
            put(n, [v[{"branch_a": "w_branch_a", "branch_b": "w_branch_b", "w_out": "w_out"}[name]][0][:, cols]])
        elif name == "ffn_up":
            put(n, [w[:, k * P:(k + 1) * P] for w in gate_up])
        elif name == "ffn_down":
            half, q = divmod(k, DC)
            put(n, [v["w_ffn_down"][0][half * FH * P:(half + 1) * FH * P, q * P:(q + 1) * P]])
        elif name == "latents":
            first = [w_in_2[:, :256], w_in_2[:, 256:512], w_in_2[:, 512:at_in2[3]]][k]
            put(n, [first[:, :P], first[:, P:]])
        elif name in ("glu_a", "glu_b", "gate_attn", "gate_conv"):
            first = at_in2[{"glu_a": 3, "glu_b": 4, "gate_attn": 5, "gate_conv": 6}[name]]
            put(n, [w_in_2[:, first + k * c:first + (k + 1) * c]])
        elif name == "w_uq":
            heads = w_uq.reshape(Q_RANK, H, QK_DIM)[:, 4 * k:4 * k + 4]
            put(n, [heads[:, :, :HD].reshape(Q_RANK, -1), heads[:, :, HD:].reshape(Q_RANK, -1)])
        elif name == "w_ukv":
            heads = w_ukv.reshape(KV_RANK, H, 2 * HD)
            put(n, [heads[:, :, k * HD:(k + 1) * HD].reshape(KV_RANK, -1)])
        elif name in ("conv_out", "o_attn", "w_out_2"):
            put(n, [v[{"conv_out": "w_conv_out_2", "o_attn": "w_o_attn_2", "w_out_2": "w_out_2"}[name]][0][:, cols]])
        elif name == "moe_up":
            g, e = divmod(k, E)
            put(n, [v["expert_w_gate_2"][0, g, e], v["expert_w_up_2"][0, g, e]])
        elif name == "moe_down":
            g, q = divmod(k, 4)
            put(n, [v["expert_w_down_2"][0, g].reshape(E * P, D)[:, q * 256:(q + 1) * 256]])
    ada = v["ada_w_2"][0].reshape(DC, P, ADA_SLABS, 256).transpose(2, 1, 0, 3).reshape(ADA_SLABS, P, SLAB)
    return pack, np.ascontiguousarray(ada)


def kernel(**inputs):
    import concourse.bacc as _bacc
    from concourse.bass_utils import run_bass_kernel_spmd as _run

    v = {k: np.asarray(x) for k, x in inputs.items()}
    pack, ada = lay_out_slabs(v)

    def columns(x):
        return x.reshape(-1, P).T

    order = ["g_mix", "b_gate", "conv_w", "g_ffn", "g_final", "c_2", "ada_b_2", "norm1_g_2", "norm2_g_2",
             "q_norm_g_2", "kv_norm_g_2", "conv_w_2", "conv_b_2", "conv_ln_g_2", "conv_ln_b_2", "final_norm_g_2"]
    const, onehot = constants()
    router_w = np.concatenate([v["router_group_w_2"][0], v["router_expert_w_2"][0]], axis=1)
    arrays = {
        "x_t": v["x"][0].T,
        "wpack": pack,
        "ada_pack": ada,
        "columns": np.concatenate([columns(v[n]) for n in order], axis=1),
        "const": const,
        "onehot": onehot,
        "rel_bias": v["rel_bias"],
        "positions_2": v["positions_2"],
        "router_w": router_w.reshape(DC, P, G + G * E).transpose(1, 0, 2),
        "router_b": np.concatenate([v["router_group_b_2"], v["router_expert_b_2"]], axis=1),
    }
    nc = _bacc.Bacc("TRN2", target_bir_lowering=False, num_devices=1)
    fed, aps = {}, {}
    for name, x in arrays.items():
        x = np.ascontiguousarray(x)
        fed[f"in_{name}"] = x
        aps[name] = nc.dram_tensor(f"in_{name}", x.shape, mybir.dt.from_np(x.dtype), kind="ExternalInput").ap()
    out = nc.dram_tensor("out_t", (D, SEQ), F32, kind="ExternalOutput").ap()
    build(nc, aps, out)
    r = _run(nc, [fed], core_ids=[0])
    return np.ascontiguousarray(r.results[0]["out_t"].T)[None]
```

```python
from contextlib import ExitStack

import numpy as np

import concourse.bass as bass
from concourse import mybir

F32 = mybir.dt.float32
F32R = mybir.dt.float32r
I32 = mybir.dt.int32
ALU = mybir.AluOpType
ACT = mybir.ActivationFunctionType
AX = mybir.AxisListType

P = 128
D = 1024
SEQ = 512
NB = SEQ // P
DC = D // P
H = 8
HD = 64
K_TOP = min(256, SEQ // 4)
D_FF = 2816
FC = D_FF // P
FH = FC // 2
EPS = 1e-6
N_BUCKETS, MAX_EXACT, MAX_DISTANCE = 32, 16, 128
Q_RANK, KV_RANK, ROPE = 384, 256, 32
QC, KC = Q_RANK // P, KV_RANK // P
QK_DIM = HD + ROPE
TAPS = 31
CC = 512 // P
G, E = 4, 8
NEG = -1e30
FILL = -3.0e38
TAKEN = -3.3e38
SLAB = 2048
W = 2
GELEM = 640

SLABS = (
    [("kv_ikw", DC, 256)] + [("iq", DC, 256)] * 2 + [("q", DC, 256)] * 2
    + [("conv_c", DC, 256)] * 2 + [("conv_x", DC, 256)] * 2 + [("conv_b", DC, 256)] * 2
    + [("gate_a", DC, 256)] * 4 + [("branch_a", CC, 512)] * 2 + [("gate_b", DC, 256)] * 4
    + [("branch_b", CC, 512)] * 2 + [("w_out", DC, 256)] * 4
    + ([("ffn_up", DC, 256)] * FH + [("ffn_down", FH, 128)] * DC) * 2
    + [("latents", DC, 256)] * 3 + [("glu_b", DC, 256)] * 2
    + [("w_uq", QC, 384), ("glu_a", DC, 256), ("w_uq", QC, 384), ("w_ukv", KC, 512), ("glu_a", DC, 256)]
    + [("w_ukv", KC, 512)] + [("gate_conv", DC, 256)] * 4
    + [("gate_attn", DC, 256), ("o_attn", CC, 256)] * 4 + [("conv_out", CC, 512)] * 2
    + [("w_out_2", DC, 256)] * 4 + ([("moe_up", DC, 256)] * E + [("moe_down", E, 256)] * 4) * G
)
FIRST = {}
for _n, (_name, _, _) in enumerate(SLABS):
    FIRST.setdefault(_name, _n)
NS = len(SLABS)
AT = {name: [n for n, slab in enumerate(SLABS) if slab[0] == name] for name in ("w_uq", "w_ukv", "glu_a")}
ADA_SLABS = 6 * D // 256
FFN2 = FIRST["ffn_up"] + FH + DC

TILE, JOB = {}, {}


def _number(table, names):
    n = 0
    for name, count in names:
        table[name] = n
        n += count


_number(TILE, [
    ("kv_ikw", 2), ("iq", 4), ("q", 4), ("conv_c", 4), ("conv_x", 4), ("conv_b", 4), ("gate_a", 8),
    ("branch_a", 8), ("attn_1", DC + 2 * NB), ("branch_b", 8), ("w_out", 8),
    ("ffn_up_0", 2 * FH), ("ffn_down_0", DC), ("ffn_up_1", 2 * FH), ("ffn_down_1", DC),
    ("latents", 6), ("glu_b", 4), ("w_uq_0", 3), ("glu_a_0", 2), ("w_uq_1", 3), ("w_ukv_0", 4), ("glu_a_1", 2),
    ("w_ukv_1", 4), ("attn_2", DC + 2 * NB),
    ("gate_and_o", 16), ("conv_out", 8), ("w_out_2", 8), ("moe", 24 * G)])
_number(JOB, [
    ("norm_1", 1), ("norm_1_all", 1), ("strip", 2), ("v_rows", 1), ("iw_rows", 1), ("dots", (NB - 1) * H), ("bias", H),
    ("attn_1", 2 * NB * H), ("norm_2", 1), ("norm_2_all", 1), ("ada_a", 1), ("norm_3", 1), ("norm_x", 1),
    ("ada_b", 1), ("norm_q", 1), ("norm_kv", 1), ("norm_q_all", 1), ("norm_kv_all", 1),
    ("attn_2", 2 * NB * H), ("ln_mean", 1), ("ln_var", 1), ("norm_4", 1), ("norm_4_all", 1), ("router", 1),
    ("router_rows", 1), ("combine", 1), ("norm_out", 1), ("norm_out_all", 1)])
SPLIT = {}
_number(SPLIT, [
    ("h1", DC), ("conv_1", CC), ("merged_1", DC), ("h2", DC), ("ffn_0", FH), ("ffn_1", FH),
    ("h3", DC), ("q_lat", QC), ("kv_lat", KC), ("conv_2", CC), ("merged_2", DC),
    ("h4", DC), ("moe", G * E)])
COLUMNS = {}
_number(COLUMNS, [
    ("g_mix", DC), ("b_gate", 2 * DC), ("conv_w", 3 * CC), ("g_ffn", DC), ("g_final", DC), ("c", DC),
    ("ada_b", 6 * DC), ("norm1_g", DC), ("norm2_g", DC), ("q_norm_g", QC), ("kv_norm_g", KC),
    ("conv_w_2", TAPS * CC), ("conv_b", CC), ("conv_ln_g", CC), ("conv_ln_b", CC), ("final_norm_g", DC),
    ("end", 0)])
CONST = {}
_number(CONST, [("ident", P), ("flip", P), ("ones", P), ("after", P), ("ramp", E), ("inv_freq", 1),
                ("rope_sign", 1), ("eps", 1), ("end", 0)])


def attn_jobs(r, kind):
    if kind == "logits":
        return r if r < 2 else 2 * r - 1
    return 2 * r + 2 if r < NB * H - 2 else r + NB * H


NORMS = {name: n for n, name in enumerate(
    ["norm_1", "norm_2", "norm_3", "norm_x", "norm_q", "norm_kv", "ln_var", "norm_4", "norm_out"])}

SPREAD = {name: n for n, name in enumerate(["norm_1", "norm_2", "norm_q", "norm_kv", "norm_4", "norm_out"])}


def squares_done(name, part):
    k = NORMS[name]
    side_by_side = {("norm_3", 1): 1, ("norm_x", 0): -1}
    return 2 * k - 1 + part + side_by_side.get((name, part), 0)


TILES_OF = {"kv_ikw": 2, "branch_a": 4, "branch_b": 4, "conv_out": 4, "ffn_down": 1, "w_uq": 3, "w_ukv": 4}


PER_STEP = [1 if r >= (NB - 1) * H and r % 2 == 0 else 2 for r in range(NB * H)]
GATE_LEFT = DC * DC - sum(PER_STEP)


def attention_tiles():
    order, done_in, unit = [], [[] for _ in range(NB * H)], 0
    for r in range(NB * H):
        for _ in range(PER_STEP[r]):
            unit += 1
            if unit % DC == 0:
                order.append(("gate", unit // DC - 1))
                done_in[r].append(unit // DC - 1)
        if r and r % H == 0:
            order.append(("values", r // H - 1))
        if r % H == 4 and r > H:
            order.append(("turned", r // H - 1))
    order += [("values", NB - 1), ("turned", NB - 1), ("gate", DC - 1)]
    assert unit + GATE_LEFT == DC * DC and unit // DC == DC - 1
    done_in[NB * H - 1].append(DC - 1)
    return {key: n for n, key in enumerate(order)}, done_in


IN_ATTN, GATE_DONE = attention_tiles()
TILE_END = []
_t = 0
for _n, (_name, _, _) in enumerate(SLABS):
    if _name in ("gate_b", "gate_conv"):
        _k = _n - FIRST[_name]
        TILE_END.append(TILE["attn_1" if _name == "gate_b" else "attn_2"] + IN_ATTN["gate", 2 * _k + 1] + 1)
        _t = TILE["attn_1" if _name == "gate_b" else "attn_2"] + len(IN_ATTN)
    else:
        _t += TILES_OF.get(_name, 2)
        TILE_END.append(_t)


def build(nc, a, out):
    ctx = ExitStack()
    with ctx:
        def sem(name):
            return ctx.enter_context(nc.semaphore(name))

        def sbuf(name, shape, dt=F32, stack=ctx):
            return stack.enter_context(nc.sbuf_tensor(name, shape, dt))

        raw = sbuf("raw", [P, W, SLAB])
        whi = sbuf("whi", [P, W, SLAB], F32R)
        wlo = sbuf("wlo", [P, W, SLAB], F32R)
        x = sbuf("x", [P, DC, SEQ])
        tmp = sbuf("tmp", [P, 2, SEQ])
        square = sbuf("square", [P, 2, SEQ])
        rstd = sbuf("rstd", [P, 2, SEQ])
        pos_row = sbuf("pos_row", [P, SEQ])
        gate = sbuf("gate", [P, 2, SEQ])
        cst = sbuf("cst", [P, CONST["end"]])
        col = sbuf("col", [P, COLUMNS["end"]])
        c_act = sbuf("c_act", [P, DC])
        ada = sbuf("ada", [P, 6 * DC])
        mod = sbuf("mod", [P, 2, DC])
        g_final_2 = sbuf("g_final_2", [P, DC])
        h_hi = sbuf("h_hi", [P, DC, SEQ], F32R)
        h_lo = sbuf("h_lo", [P, DC, SEQ], F32R)
        stats = sbuf("stats", [P, 160])
        sums = stats[:, 0:NB * H].rearrange("p (b h) -> p b h", h=H)
        inv_sums = stats[:, 32:32 + NB * H].rearrange("p (b h) -> p b h", h=H)
        neg_max = stats[:, 64:66]
        top8 = stats[:, 72:80]
        iw_rows = stats[:, 80:80 + NB * H].rearrange("p (b h) -> p b h", h=H)
        pos_col = stats[:, 112:112 + NB]
        inv_mean = [stats[:, 128 + NB * n:128 + NB * (n + 1)] for n in range(2)]
        pos_col_raw = stats[:, 120:120 + NB].bitcast(I32)

        def overlay(*views):
            made, size = {}, 0
            for view in views:
                with ExitStack() as s:
                    n = 0
                    for name, shape, dt in view:
                        made[name] = sbuf(name, shape, dt, s)
                        n += 4 * int(np.prod(shape[1:])) + 32
                    size = max(size, n)
            return made, size

        memory = {}

        def place(name, *views):
            made, size = overlay(*views)
            memory.update(made)
            ctx.enter_context(nc.sbuf_tensor(name, [P, size // 4], F32))

        place("place_a",
              [("onehot", [N_BUCKETS, GELEM], F32), ("rel", [N_BUCKETS, H], F32), ("strip", [H, GELEM], F32)],
              [("conv_in", [P, CC, SEQ + 2], F32), ("conv_mid", [P, 2, SEQ], F32)],
              [("strip_t", [P, H, SEQ], F32)],
              [("ada_raw", [P, 2, SLAB], F32)],
              [("rope", [P, 5, SEQ], F32)],
              [("gate_conv", [P, DC, SEQ], F32)])
        stages = []

        def stage(*views):
            stages.append(overlay(*views))
            memory.update(stages[-1][0])

        base_1 = ExitStack()
        made, size = overlay([("iq_t", [P, CC, SEQ], F32), ("score", [P, 1152], F32), ("work", [P, 1152], F32)],
                             [("bias", [P, H, SEQ], F32)])
        memory.update(made)
        base_1.enter_context(nc.sbuf_tensor("place_1", [P, size // 4], F32))
        stage([("ik_t", [P, SEQ], F32), ("q_t", [P, CC, SEQ], F32), ("k_t", [P, SEQ], F32), ("v_t", [P, SEQ], F32),
               ("v_rows_1", [P, NB, HD], F32), ("mask_1", [P, 1280], F32), ("y1", [P, DC, SEQ], F32),
               ("prob_t1", [P, 2, SEQ], F32), ("a_hi1", [P, CC, SEQ], F32R), ("a_lo1", [P, CC, SEQ], F32R)])
        base_1.close()
        stage([("f_hi", [P, FH, SEQ], F32R), ("f_lo", [P, FH, SEQ], F32R), ("ada_sum", [P, ADA_SLABS, 256], F32)])
        base_3 = ExitStack()
        memory["q_h"] = sbuf("q_h", [P, H, SEQ], F32, base_3)
        made, size = overlay([("k_h", [P, H, SEQ], F32)],
                             [("c_hi", [P, CC, SEQ], F32R), ("c_lo", [P, CC, SEQ], F32R)])
        memory.update(made)
        base_3.enter_context(nc.sbuf_tensor("place_3", [P, size // 4], F32))
        made, size = overlay([("l_hi", [P, QC + KC, SEQ], F32R), ("l_lo", [P, QC + KC, SEQ], F32R)],
                             [("o_hi", [P, CC, SEQ], F32R), ("o_lo", [P, CC, SEQ], F32R),
                              ("prob_t2", [P, 2, SEQ], F32)])
        memory.update(made)
        base_3.enter_context(nc.sbuf_tensor("place_3b", [P, size // 4], F32))
        stage([("v_rows_2", [P, NB, H * HD], F32),
               ("u", [P, CC + 2, SEQ + TAPS - 1], F32)])
        base_3.close()
        stage([("e_hi", [P, E, SEQ], F32R), ("e_lo", [P, E, SEQ], F32R), ("comb", [P, 2, SEQ], F32),
               ("comb_t", [G * E, SEQ], F32), ("router_w", [P, DC, P], F32),
               ("router_hi", [P, DC, P], F32R), ("router_lo", [P, DC, P], F32R), ("logits_t", [G + G * E, SEQ], F32),
               ("router_b", [P, G + G * E], F32), ("rt", [P, 14, NB, G * E], F32)])
        m = memory
        iq_t, score, work, bias = m["iq_t"], m["score"], m["work"], m["bias"]
        ik_t, q_t, k_t, v_t, v_rows_1 = m["ik_t"], m["q_t"], m["k_t"], m["v_t"], m["v_rows_1"]
        mask_1, y1, prob_t1, a_hi1, a_lo1 = m["mask_1"], m["y1"], m["prob_t1"], m["a_hi1"], m["a_lo1"]
        conv_in, conv_mid, strip_t = m["conv_in"], m["conv_mid"], m["strip_t"]
        ada_raw, gate_conv, f_hi, f_lo, ada_sum = m["ada_raw"], m["gate_conv"], m["f_hi"], m["f_lo"], m["ada_sum"]
        q_h, k_h, c_hi, c_lo = m["q_h"], m["k_h"], m["c_hi"], m["c_lo"]
        l_hi, l_lo, o_hi, o_lo, prob_t2 = m["l_hi"], m["l_lo"], m["o_hi"], m["o_lo"], m["prob_t2"]
        v_rows_2, u = m["v_rows_2"], m["u"]
        e_hi, e_lo, comb, comb_t = m["e_hi"], m["e_lo"], m["comb"], m["comb_t"]
        router_w, router_b, rt = m["router_w"], m["router_b"], m["rt"]
        router_hi, router_lo, logits_t = m["router_hi"], m["router_lo"], m["logits_t"]
        rope_cos, rope_sin, pos_raw, turn, angle = (m["rope"][:, n, :] for n in range(5))

        bank = [ctx.enter_context(nc.psum_tensor(f"bank{b}", [P, 512], F32)) for b in range(8)]
        strip_dram = nc.dram_tensor("strip_dram", [H, GELEM], F32)
        comb_dram = nc.dram_tensor("comb_dram", [G * E, SEQ], F32)

        conv_place = [0, 1, 2, CC + 1]

        def convolved(c):
            return u[:, conv_place[c], TAPS - 1:]

        def const(name, width=1):
            return cst[:, CONST[name]:CONST[name] + width]

        def column(name, n=0, width=1):
            return col[:, COLUMNS[name] + n:COLUMNS[name] + n + width]

        ident, flip, ones = const("ident", P), const("flip", P), const("ones", P)

        cst_loaded, col_loaded, rel_loaded = sem("cst_loaded"), sem("col_loaded"), sem("rel_loaded")
        x_loaded = [sem(f"x_loaded{n}") for n in range(4)]
        x_again = [sem(f"x_again{n}") for n in range(2)]
        slab_full = [sem(f"slab_full{w}") for w in range(W)]
        hi_done, lo_done = sem("hi_done"), sem("lo_done")
        tile_done = sem("tile_done")
        bank_free = [sem(f"bank_free{b}") for b in range(8)]
        ada_full = [sem(f"ada_full{w}") for w in range(2)]
        inverted, spread = sem("inverted"), sem("spread")
        ada_summed, ada_done = sem("ada_summed"), sem("ada_done")
        c_ready = sem("c_ready")
        x_squared, pair_squared = sem("x_squared"), sem("pair_squared")
        gate_ready = sem("gate_ready")
        squared, summed = sem("squared"), sem("summed")
        normed, high = sem("normed"), sem("high")
        var_ready, rstd_ready = sem("var_ready"), sem("rstd_ready")
        split_done = sem("split_done")
        strip_sum, strip_stored, strip_turned = sem("strip_sum"), sem("strip_stored"), sem("strip_turned")
        bias_sum = sem("bias_sum")
        turned = sem("turned")
        dots_done, dots_used = sem("dots_done"), sem("dots_used")
        logits_done, probs_ready, probs_turned, pv_done = (
            sem("logits_done"), sem("probs_ready"), sem("probs_turned"), sem("pv_done"))
        pos_loaded, angles_ready, rope_ready = sem("pos_loaded"), sem("angles_ready"), sem("rope_ready")
        heads_ready = sem("heads_ready")
        y_done = sem("y_done")
        pads_ready = sem("pads_ready")
        tap_scaled, tap_added = sem("tap_scaled"), sem("tap_added")
        conv_done, mean_done, scaled, silu_done = (
            sem("conv_done"), sem("mean_done"), sem("scaled"), sem("silu_done"))
        router_loaded, router_split, routed, shift_ready, exp_ready = (
            sem("router_loaded"), sem("router_split"), sem("routed"), sem("shift_ready"), sem("exp_ready"))
        logits_turned = sem("logits_turned")
        weights_ready, weights_turned, comb_stored = (
            sem("weights_ready"), sem("weights_turned"), sem("comb_stored"))
        comb_full, comb_used = [sem(f"comb_full{w}") for w in range(2)], sem("comb_used")
        out_ready, stored = sem("out_ready"), sem("stored")
        step = sem("step")

        def width(n):
            return SLABS[n][1] * SLABS[n][2]

        def halves(n):
            kc, c = SLABS[n][1:]
            return slice(0, kc // 2 * c), slice(kc // 2 * c, kc * c)

        def parts(n):
            kc, c = SLABS[n][1:]
            return [t[:, n % W, 0:kc * c].rearrange("p (k c) -> p k c", c=c) for t in (whi, wlo)]

        def runs(eng, n0, count, body, size=2):
            whole = count // size
            if whole >= 2:
                with eng.Fori(0, whole) as i:
                    for k in range(size):
                        body(n0 + k, i, size)
            else:
                whole = 0
            for n in range(n0 + whole * size, n0 + count):
                body(n, 0, 0)

        def tile_is_done(eng, t, i=0, per=0):
            eng.wait_ge(tile_done, t + 1 + i * per)

        def tile_is_taken(eng, t, i=0, per=0):
            eng.wait_ge(bank_free[t % 4], t // 4 + 1 + i * (per // 4))

        def job_is_taken(eng, j):
            eng.wait_ge(bank_free[4 + j % 4], j // 4 + 1)

        def head_is_multiplied(eng, base_t, first, r):
            if r % H == H - 1:
                tile_is_done(eng, base_t + IN_ATTN["values", r // H])
            else:
                eng.wait_ge(pv_done, first * (H - 1) // H + (H - 1) * (r // H) + r % H + 1)

        block = ctx.enter_context(nc.Block())

        @block.sync
        def _(sp):
            def load_slab(n, i=0, per=0):
                if n >= W:
                    sp.wait_ge(lo_done, 2 * (n - W + 1) + i * (2 * per))
                sp.dma_start(raw[:, n % W, 0:width(n)], a["wpack"][n + i * per][:, 0:width(n)]) \
                    .then_inc(slab_full[n % W], 16)

            def load_ada(s, i=0, per=0):
                if s >= 2:
                    sp.wait_ge(ada_summed, s - 1 + i * per)
                sp.dma_start(ada_raw[:, s % 2, :], a["ada_pack"][s + i * per]).then_inc(ada_full[s % 2], 16)

            x_dram = a["x_t"].rearrange("(c p) t -> p c t", p=P)
            out_dram = out.rearrange("(c p) t -> p c t", p=P)
            for n in range(4):
                sp.dma_start(x[:, 2 * n:2 * n + 2, :], x_dram[:, 2 * n:2 * n + 2, :]).then_inc(x_loaded[n], 16)
                if n == 0:
                    sp.dma_start(cst[:], a["const"]).then_inc(cst_loaded, 16)
            sp.dma_start(col[:], a["columns"]).then_inc(col_loaded, 16)
            load_slab(0)
            load_slab(1)
            sp.dma_start(m["onehot"][:], a["onehot"]).then_inc(rel_loaded, 16)
            sp.dma_start(m["rel"][:], a["rel_bias"]).then_inc(rel_loaded, 16)
            for j in range(2):
                job_is_taken(sp, JOB["strip"] + j)
            sp.dma_start(strip_dram.ap(), m["strip"][:]).then_inc(strip_stored, 16)
            runs(sp, 2, FIRST["w_out"] - 2, load_slab)
            load_slab(FIRST["w_out"])
            load_slab(FIRST["w_out"] + 1)
            for half in range(2):
                for c in range(half * DC // 2, (half + 1) * DC // 2):
                    tile_is_taken(sp, TILE["branch_b"] + c)
                cs = slice(half * DC // 2, (half + 1) * DC // 2)
                sp.dma_start(x[:, cs, :], x_dram[:, cs, :]).then_inc(x_again[half], 16)
                load_slab(FIRST["w_out"] + 2 + half)

            for half in range(2):
                n0, s0 = FIRST["ffn_up"] + half * (FH + DC), half * (FH + 2)
                down = n0 + FH

                def up(n, i=0, per=0, n0=n0, s0=s0):
                    load_slab(n, i, per)
                    load_ada(s0 + n - n0 - 2, i, per)

                if half == 0:
                    sp.wait_ge(bias_sum, H)
                for k in range(4):
                    load_slab(n0 + k)
                    if k < 2:
                        load_ada(s0 + k)
                runs(sp, n0 + 4, FH - 4, up)
                up(down)
                up(down + 1)
                for k in range(2, DC):
                    load_slab(down + k)
                    if half == 0 and k < 4:
                        load_ada(FH + k - 2)
                    if half == 1 and k == 3:
                        sp.wait_ge(ada_summed, ADA_SLABS)
                        sp.dma_start(pos_raw.bitcast(I32), a["positions_2"].to_broadcast([P, SEQ])) \
                            .then_inc(pos_loaded, 16)
                        sp.dma_start(pos_col_raw, a["positions_2"].rearrange("o (b p) -> p (o b)", p=P),
                                     allow_slow_non_contiguous=True).then_inc(pos_loaded, 16)
            for n in range(FIRST["latents"], FIRST["moe_up"]):
                load_slab(n)
            tile_is_done(sp, TILE["conv_out"] + DC - 1)
            sp.dma_start(router_w[:], a["router_w"]).then_inc(router_loaded, 16)
            sp.dma_start(router_b[:], a["router_b"].to_broadcast([P, G + G * E])).then_inc(router_loaded, 16)
            n0 = FIRST["moe_up"]
            for e in range(4):
                load_slab(n0 + e)
            job_is_taken(sp, JOB["combine"])
            sp.dma_start(comb_dram.ap(), comb_t[:]).then_inc(comb_stored, 16)
            sp.wait_ge(comb_stored, 16)

            def moe_group(i, first):
                for e in range(E):
                    if not (first and e < 4):
                        load_slab(n0 + e, i, E + 4)
                    if not (first and e < 2):
                        sp.wait_ge(comb_used, e - 1 + i * E)
                    row = comb_dram.ap()[e:e + 1, :] if first else comb_dram.ap()[bass.ds(e + i * E, 1), :]
                    sp.dma_start(comb[:, e % 2, :], row.to_broadcast([P, SEQ])).then_inc(comb_full[e % 2], 16)
                for d in range(4):
                    load_slab(n0 + E + d, i, E + 4)

            moe_group(0, True)
            with sp.Fori(1, G) as i:
                moe_group(i, False)
            for c in range(DC):
                sp.wait_ge(out_ready, c + 1)
                sp.dma_start(out_dram[:, c, :], x[:, c, :]).then_inc(stored, 16)
            sp.wait_ge(stored, 16 * DC)

        @block.gpsimd
        def _(pool):
            def low_part(n, i=0, per=0):
                for half, cols in enumerate(halves(n)):
                    pool.wait_ge(hi_done, 2 * n + half + 1 + i * (2 * per))
                    pool.tensor_tensor(wlo[:, n % W, cols], raw[:, n % W, cols], whi[:, n % W, cols].bitcast(F32),
                                       ALU.subtract).then_inc(lo_done, 1)

            def add_taps(first, count):
                for tap in range(first, first + count):
                    pool.wait_ge(tap_scaled, tap + 1)
                    if tap > 1:
                        pool.wait_ge(tap_added, tap - 1)
                    pool.tensor_tensor(convolved(CC - 1), convolved(CC - 1), rstd[:, tap % 2, :], ALU.add) \
                        .then_inc(tap_added, 1)

            gate_conv_0 = FIRST["gate_conv"]
            n = 0
            while n < NS:
                if gate_conv_0 < n <= gate_conv_0 + 4:
                    low_part(n)
                    k = n - gate_conv_0 - 1
                    add_taps(1 + 8 * k, min(8, TAPS - 1 - 8 * k))
                    n += 1
                    continue
                count = 1
                while n + count < NS and width(n + count) == width(n) and n + count != gate_conv_0 + 1:
                    count += 1
                runs(pool, n, count, low_part)
                n += count

        @block.scalar
        def _(act):
            def high_part(n, i=0, per=0, tiles=0):
                act.wait_ge(slab_full[n % W], 16 * (n // W + 1) + i * (per // W * 16))
                if n >= W:
                    act.wait_ge(tile_done, TILE_END[n - W] + i * tiles)
                for cols in halves(n):
                    act.copy(whi[:, n % W, cols], raw[:, n % W, cols]).then_inc(hi_done, 1)

            def root(name, count, out_ap=None):
                if name in SPREAD:
                    act.wait_ge(spread, SPREAD[name] + 1)
                    b = 4 + JOB[name + "_all"] % 4
                    act.activation(rstd[:, NORMS[name] % 2, :], bank[b][:], ACT.Sqrt).then_inc(bank_free[b], 1)
                    return
                k, b = NORMS[name], 4 + JOB[name] % 4
                act.wait_ge(summed, 2 * k + 2)
                act.activation(rstd[:, k % 2, :] if out_ap is None else out_ap, bank[b][:], ACT.Sqrt,
                               scale=1.0 / (count * P), bias=const("eps")).then_inc(bank_free[b], 1)

            made = [0]

            def highs(count, hi, shift=None, start=0):
                for c in range(start, start + count):
                    made[0] += 1
                    act.wait_ge(normed, made[0])
                    if shift is None:
                        act.copy(hi[:, c, :], tmp[:, c % 2, :]).then_inc(high, 1)
                    else:
                        act.activation(hi[:, c, :], tmp[:, c % 2, :], ACT.Identity,
                                       bias=ada[:, shift + c:shift + c + 1]).then_inc(high, 1)

            def take(out_ap, t, func, bias=0.0, i=0, per=0):
                tile_is_done(act, t, i, per)
                act.activation(out_ap, bank[t % 4][:], func, bias=bias).then_inc(bank_free[t % 4], 1)

            def scale_tap(tap):
                src = u[:, CC, tap:tap + SEQ]
                w_tap = column("conv_w_2", tap * CC + CC - 1)
                if tap == 0:
                    tile_is_taken(act, TILE["glu_a_1"] + 1)
                    act.activation(convolved(CC - 1), src, ACT.Identity, scale=w_tap, bias=column("conv_b", CC - 1)) \
                        .then_inc(tap_scaled, 1)
                    return
                if tap > 2:
                    act.wait_ge(tap_added, tap - 2)
                act.activation(rstd[:, tap % 2, :], src, ACT.Copy, scale=w_tap).then_inc(tap_scaled, 1)

            def attention(base_j, base_t, prob_t, first, full, gate_slab, take_gate):
                for r in range(NB * H + 1):
                    if r < NB * H:
                        blk, h = r // H, r % H
                        w = SEQ if full else P * (blk + 1)
                        job_is_taken(act, base_j + attn_jobs(r, "logits"))
                        act.activation(square[:, r % 2, 0:w], square[:, r % 2, 0:w], ACT.Exp,
                                       bias=neg_max[:, r % 2:r % 2 + 1], scale=-1.0,
                                       accum_out=sums[:, blk, h:h + 1]).then_inc(probs_ready, 1)
                    if full and r < TAPS:
                        scale_tap(r)
                    if r >= 1:
                        s = r - 1
                        w = SEQ if full else P * (s // H + 1)
                        act.wait_ge(probs_turned, first + s + 1)
                        if s >= 2:
                            head_is_multiplied(act, base_t, first, s - 2)
                        j = base_j + attn_jobs(s, "turn")
                        act.copy(prob_t[:, s % 2, 0:w], bank[4 + j % 4][:, 0:w]).then_inc(bank_free[4 + j % 4], 1)
                        for c in GATE_DONE[s]:
                            take_gate(c, base_t + IN_ATTN["gate", c])
                            if c % 2 == 1:
                                high_part(gate_slab + c // 2 + W)

            def after(n, i=0, per=0, tiles=0):
                name = SLABS[n][0]
                k = AT[name].index(n) if name in AT else n - FIRST[name]
                if name == "iq" and k == 1:
                    for d in range((NB - 1) * H):
                        w, j = P * (d // H + 2), JOB["dots"] + d
                        act.wait_ge(dots_done, d + 1)
                        if d >= 2:
                            act.wait_ge(dots_used, d - 1)
                        act.activation(gate[:, d % 2, 0:w], bank[4 + j % 4][:, 0:w], ACT.Relu) \
                            .then_inc(bank_free[4 + j % 4], 1)
                elif name == "gate_a":
                    if k == 2:
                        act.wait_ge(strip_stored, 16)
                        act.wait_ge(split_done, SPLIT["conv_1"] + CC)
                        act.dma_start(strip_t[:], bass.AP(tensor=strip_dram, offset=0, ap=[[1, P], [GELEM, H], [1, SEQ]])) \
                            .then_inc(strip_turned, 16)
                    for c in (2 * k, 2 * k + 1):
                        take(y1[:, c, :], TILE["gate_a"] + c, ACT.Sigmoid, column("b_gate", c))
                elif name == "gate_b" and k == 0:
                    attention(JOB["attn_1"], TILE["attn_1"], prob_t1, 0, False, n,
                              lambda c, t: take(x[:, c, :], t, ACT.Copy))
                    for c in range(DC):
                        tile_is_taken(act, TILE["attn_1"] + IN_ATTN["gate", c])
                        act.activation(x[:, c, :], x[:, c, :], ACT.Sigmoid, bias=column("b_gate", DC + c)) \
                            .then_inc(gate_ready, 1)
                elif name == "branch_b":
                    highs(CC, h_hi, start=CC * k)
                elif name == "conv_out":
                    highs(CC, h_hi, start=CC * k)
                elif name == "w_out" and k == 3:
                    root("norm_2", DC)
                    highs(DC, h_hi)
                    act.activation(c_act[:], column("c", 0, DC), ACT.Silu).then_inc(c_ready, 1)
                elif name == "ffn_up":
                    n0 = n - k if k < FH else FFN2
                    t = TILE["ffn_up_0" if k < FH else "ffn_up_1"] + 2 * (n - n0)
                    if n - n0 >= 2:
                        tile_is_taken(act, t - 3, i, tiles)
                    elif k < FH:
                        act.wait_ge(dots_used, (NB - 1) * H)
                    else:
                        tile_is_taken(act, TILE["ffn_up_0"] + 2 * (FH - 1 - (n - n0 + FH - 1) % 2) + 1)
                    take(gate[:, (n - n0) % 2, :], t, ACT.Silu, i=i, per=tiles)
                elif n == FFN2 + FH + DC - 1:
                    act.wait_ge(angles_ready, 1)
                    act.activation(rope_sin, angle, ACT.Sin).then_inc(rope_ready, 1)
                    act.activation(rope_cos, turn, ACT.Sin).then_inc(rope_ready, 1)
                    act.wait_ge(var_ready, 1)
                    r_3 = rstd[:, NORMS["norm_3"] % 2, :]
                    act.activation(r_3, r_3, ACT.Sqrt).then_inc(rstd_ready, 1)
                    highs(DC, h_hi, shift=0)
                    act.wait_ge(ada_done, 2)
                    root("norm_x", DC, v_rows_2[:, NB - 1, :])
                elif name == "glu_b":
                    act.wait_ge(pads_ready, 1)
                    for c in (2 * k, 2 * k + 1):
                        take(u[:, c + 1, TAPS - 1:], TILE["glu_b"] + c, ACT.Sigmoid)
                    if k == 0:
                        root("norm_q", QC)
                        highs(QC, l_hi)
                elif name == "w_uq":
                    for q in range(2):
                        t, head = TILE[f"w_uq_{k}"] + q, 4 * k + 2 * q
                        tile_is_done(act, t)
                        act.copy(q_h[0:HD, head, :], bank[t % 4][0:HD, :])
                        act.copy(q_h[0:HD, head + 1, :], bank[t % 4][HD:P, :]).then_inc(bank_free[t % 4], 1)
                    if k == 0:
                        root("norm_kv", KC)
                        highs(KC, l_hi[:, QC:, :])
                elif name == "w_ukv":
                    if k == 1:
                        act.wait_ge(y_done, 1)
                    for q in range(4 - 4 * k):
                        t = TILE["w_ukv_0"] + q
                        tile_is_done(act, t)
                        act.copy(k_h[0:HD, 2 * q, :], bank[t % 4][0:HD, :])
                        act.copy(k_h[0:HD, 2 * q + 1, :], bank[t % 4][HD:P, :]).then_inc(bank_free[t % 4], 1)
                    for blk in range(NB * k):
                        take(v_rows_2[:, blk, :], TILE["w_ukv_1"] + blk, ACT.Copy)
                elif name == "gate_conv" and k == 0:
                    act.wait_ge(heads_ready, 3)
                    attention(JOB["attn_2"], TILE["attn_2"], prob_t2, NB * H, True, n,
                              lambda c, t: take(gate_conv[:, c, :], t, ACT.Copy))
                elif name == "gate_attn":
                    k //= 2
                    for c in (2 * k, 2 * k + 1):
                        t = TILE["gate_and_o"] + 4 * k + c % 2
                        if k:
                            tile_is_taken(act, t - 2)
                        take(gate[:, c % 2, :], t, ACT.Sigmoid)
                    if k == 0:
                        for c in range(DC):
                            tile_is_taken(act, TILE["attn_2"] + IN_ATTN["gate", c])
                            act.activation(gate_conv[:, c, :], gate_conv[:, c, :], ACT.Sigmoid).then_inc(gate_ready, 1)
                    if k == 1:
                        root("ln_var", CC)
                        for c in range(CC):
                            act.wait_ge(scaled, c + 1)
                            act.activation(convolved(c), convolved(c), ACT.Silu,
                                           bias=column("conv_ln_b", c), scale=column("conv_ln_g", c)) \
                                .then_inc(silu_done, 1)
                elif name == "w_out_2" and k == 3:
                    root("norm_4", DC)
                    highs(DC, h_hi, shift=3 * DC)
                elif name == "moe_up":
                    e = k
                    t = TILE["moe"] + 2 * e
                    tile_is_taken(act, t - 3 if e >= 2 else t - 3 - 8, i, tiles)
                    take(gate[:, e % 2, :], t, ACT.Silu, i=i, per=tiles)

            for c in range(1, DC, 2):
                act.wait_ge(x_loaded[c // 2], 16)
                act.activation(y1[:, c, :], x[:, c, :], ACT.Square).then_inc(x_squared, 1)
            high_part(0)
            act.wait_ge(cst_loaded, 16)
            act.wait_ge(col_loaded, 16)
            root("norm_1", DC)
            highs(DC, h_hi)
            high_part(1)
            up, moe = FIRST["ffn_up"], FIRST["moe_up"]
            for n in range(up):
                if SLABS[n][0] == "gate_a":
                    after(n)
                    high_part(n + W)
                    continue
                if SLABS[n][0] != "gate_b":
                    high_part(n + W)
                after(n)
            for n0 in (up, FFN2):
                for k in (0, 1):
                    high_part(n0 + W + k)
                    after(n0 + k)
                with act.Fori(0, (FH - 1 - W - 2) // 2) as i:
                    for k in (2, 3):
                        high_part(n0 + W + k, i, 2, 4)
                        after(n0 + k, i, 2, 4)
                for k in range(2 + (FH - 1 - W - 2) // 2 * 2, FH + DC):
                    high_part(n0 + W + k)
                    after(n0 + k)
            for n in range(FIRST["latents"], moe):
                if SLABS[n][0] == "w_ukv":
                    after(n)
                    high_part(n + W)
                    continue
                if SLABS[n][0] != "gate_conv":
                    high_part(n + W)
                after(n)

            def moe_group(i, per, tiles, count, first=False):
                for k in range(E + 4):
                    if k < count:
                        high_part(moe + W + k, i, per, tiles)
                    if k < E:
                        after(moe + k, i, per, tiles)
                    if first and k == 0:
                        for v, n_v in ((0, G), (1, E)):
                            act.wait_ge(shift_ready, v + 1)
                            act.activation(rt[:, v, :, 0:n_v], rt[:, v, :, 0:n_v], ACT.Exp).then_inc(exp_ready, 1)

            moe_group(0, 0, 0, E + 4, True)
            with act.Fori(1, G - 1) as i:
                moe_group(i, E + 4, 24, E + 4)
            moe_group(G - 1, E + 4, 24, E + 4 - W)
            root("norm_out", DC)

        @block.tensor
        def _(pe):
            def tile_bank(t, i=0, per=0):
                if t >= 4:
                    pe.wait_ge(bank_free[t % 4], t // 4 + i * (per // 4))
                return bank[t % 4]

            def job_bank(j):
                if j >= 4:
                    pe.wait_ge(bank_free[4 + j % 4], j // 4)
                return bank[4 + j % 4]

            def product(t, n, c0, rhs, i=0, per=0, tiles=0, ready=None):
                ps = tile_bank(t, i, tiles)
                hi, lo = parts(n)
                kc = SLABS[n][1]
                for k in range(kc):
                    if k == kc // 2:
                        second_half()
                    if ready is not None:
                        pe.wait_ge(split_done, ready + k + 1 + i * per)
                    x_hi, x_lo = rhs(k)
                    wh, wl = hi[:, k, c0:c0 + P], lo[:, k, c0:c0 + P]
                    pe.matmul(ps[:], wh, x_hi, start=(k == 0), stop=False)
                    pe.matmul(ps[:], wl, x_hi, start=False, stop=False)
                    mm = pe.matmul(ps[:], wh, x_lo, start=False, stop=(k == kc - 1))
                mm.then_inc(tile_done, 1)

            def products(t, n, count, rhs, ready):
                banks = [tile_bank(t + q) for q in range(count)]
                hi, lo = parts(n)
                kc = SLABS[n][1]
                for k in range(kc):
                    if k == kc // 2:
                        second_half()
                    pe.wait_ge(split_done, ready + k + 1)
                    x_hi, x_lo = rhs(k)
                    for q in range(count):
                        wh, wl = hi[:, k, q * P:(q + 1) * P], lo[:, k, q * P:(q + 1) * P]
                        pe.matmul(banks[q][:], wh, x_hi, start=(k == 0), stop=False)
                        pe.matmul(banks[q][:], wl, x_hi, start=False, stop=False)
                        mm = pe.matmul(banks[q][:], wh, x_lo, start=False, stop=(k == kc - 1))
                        if k == kc - 1:
                            mm.then_inc(tile_done, 1)

            second = []

            def slab(n, i=0, per=0):
                pe.wait_ge(lo_done, 2 * n + 1 + i * (2 * per))
                second[:] = [(2 * n + 2, i, 2 * per)]

            def second_half():
                for n, i, per in second:
                    pe.wait_ge(lo_done, n + i * per)
                second.clear()

            def chunks(hi, lo):
                return lambda k: (hi[:, k, :], lo[:, k, :])

            h = chunks(h_hi, h_lo)

            def dense(name, t_name, rhs, ready=None, after_slab=None):
                n0 = FIRST[name]
                count = sum(s[0] == name for s in SLABS)
                per_slab = SLABS[n0][2] // P
                for k in range(count):
                    slab(n0 + k)
                    if k == 0 and ready is not None and per_slab == 2:
                        products(TILE[t_name], n0, per_slab, rhs, ready)
                    else:
                        for q in range(per_slab):
                            product(TILE[t_name] + k * per_slab + q, n0 + k, q * P, rhs,
                                    ready=ready if k == 0 and q == 0 else None)
                    if after_slab:
                        after_slab(k)

            def sum_tokens(b, part, first, last):
                for blk in range(NB):
                    mm = pe.matmul(b[:, blk:blk + 1], part[:, blk * P:(blk + 1) * P], ones[:, 0:1],
                                   start=first and blk == 0, stop=last and blk == NB - 1)
                return mm

            def spread_inverse(name):
                b, slot = job_bank(JOB[name + "_all"]), inv_mean[SPREAD[name] % 2]
                pe.wait_ge(inverted, SPREAD[name] + 1)
                for blk in range(NB):
                    mm = pe.matmul(b[:, blk * P:(blk + 1) * P], slot[:, blk:blk + 1].to_broadcast([P, P]), ident,
                                   start=True, stop=True)
                mm.then_inc(spread, 1)

            def sum_squares(name, parts=square):
                b = job_bank(JOB[name])
                for part in range(2):
                    pe.wait_ge(squared, squares_done(name, part))
                    if name in SPREAD:
                        sum_tokens(b, parts[:, part, :], part == 0, part == 1).then_inc(summed, 1)
                        continue
                    pe.matmul(b[:], ones, parts[:, part, :], start=(part == 0), stop=(part == 1)).then_inc(summed, 1)

            def gate_products(n0, base_t):
                for c in range(DC):
                    if c % 2 == 0:
                        slab(n0 + c // 2)
                    ps = tile_bank(base_t + IN_ATTN["gate", c])
                    hi, lo = parts(n0 + c // 2)
                    cols = slice(c % 2 * P, (c % 2 + 1) * P)
                    for k in range(DC):
                        if k == DC // 2:
                            second_half()
                        x_hi, x_lo = h(k)
                        pe.matmul(ps[:], hi[:, k, cols], x_hi, start=(k == 0), stop=False)
                        pe.matmul(ps[:], lo[:, k, cols], x_hi, start=False, stop=False)
                        mm = pe.matmul(ps[:], hi[:, k, cols], x_lo, start=False, stop=(k == DC - 1))
                        if k == DC - 1:
                            mm.then_inc(tile_done, 1)
                        yield

            def attention(base_j, base_t, prob_t, first, full, gate_slab, q, k, v):
                gate_work = gate_products(gate_slab, base_t)

                def w(r):
                    return SEQ if full else P * (r // H + 1)

                def logits(r):
                    b = job_bank(base_j + attn_jobs(r, "logits"))
                    pe.matmul(b[:, 0:w(r)], q(r % H, r // H), k(r % H, w(r)), start=True, stop=True) \
                        .then_inc(logits_done, 1)

                def turn_probs(r):
                    pe.wait_ge(probs_ready, first + r + 1)
                    b = job_bank(base_j + attn_jobs(r, "turn"))
                    for s in range(w(r) // P):
                        mm = pe.transpose(b[:, s * P:(s + 1) * P], square[:, r % 2, s * P:(s + 1) * P], ident)
                    mm.then_inc(probs_turned, 1)

                def values(r):
                    hh, t = r % H, base_t + IN_ATTN["values", r // H]
                    b = tile_bank(t) if hh == 0 else bank[t % 4]
                    job_is_taken(pe, base_j + attn_jobs(r, "turn"))
                    if full and r == 0:
                        for blk in range(NB):
                            tile_is_taken(pe, TILE["w_ukv_1"] + blk)
                    ns = w(r) // P
                    for s in range(ns):
                        mm = pe.matmul(b[:, hh * HD:(hh + 1) * HD], prob_t[:, r % 2, s * P:(s + 1) * P], v(hh, s),
                                       start=(s == 0), stop=(s == ns - 1))
                    mm.then_inc(tile_done if hh == H - 1 else pv_done, 1)

                def turn_rows(blk):
                    t = base_t + IN_ATTN["turned", blk]
                    tile_is_taken(pe, base_t + IN_ATTN["values", blk])
                    b = tile_bank(t)
                    for c in range(CC):
                        mm = pe.transpose(b[:, c * P:(c + 1) * P], tmp[:, blk % 2, c * P:(c + 1) * P], ident)
                    mm.then_inc(tile_done, 1)

                logits(0)
                logits(1)
                for r in range(NB * H):
                    if r == 0:
                        for _ in range(PER_STEP[r]):
                            next(gate_work)
                    turn_probs(r)
                    if r + 2 < NB * H:
                        logits(r + 2)
                    if r:
                        for _ in range(PER_STEP[r]):
                            next(gate_work)
                    if r >= 1:
                        values(r - 1)
                    if r % H == 4 and r > H:
                        turn_rows(r // H - 1)
                values(NB * H - 1)
                for _ in range(GATE_LEFT // 2):
                    next(gate_work)
                turn_rows(NB - 1)
                for _ in gate_work:
                    pass

            def half_rows(hh):
                return slice(HD * (hh % 2), HD * (hh % 2 + 1))

            pe.wait_ge(cst_loaded, 16)
            b = job_bank(JOB["norm_1"])
            for c in range(0, DC, 2):
                pe.wait_ge(pair_squared, c // 2 + 1)
                mm = sum_tokens(b, y1[:, c, :], c == 0, c == DC - 2)
                if c >= DC - 4:
                    mm.then_inc(summed, 1)
            spread_inverse("norm_1")
            pe.wait_ge(rel_loaded, 32)
            for j, (d0, d1) in enumerate(((0, SEQ), (SEQ, GELEM))):
                pe.matmul(job_bank(JOB["strip"] + j)[0:H, 0:d1 - d0], m["rel"][:], m["onehot"][:, d0:d1],
                          start=True, stop=True).then_inc(strip_sum, 1)
            dense("kv_ikw", "kv_ikw", h, ready=SPLIT["h1"])
            dense("iq", "iq", h)
            tile_is_taken(pe, TILE["kv_ikw"])
            b = job_bank(JOB["v_rows"])
            for s in range(NB):
                mm = pe.transpose(b[:, s * HD:(s + 1) * HD], v_t[HD:P, s * P:(s + 1) * P], ident[HD:P, HD:P])
            mm.then_inc(turned, 1)
            tile_is_taken(pe, TILE["kv_ikw"] + 1)
            b = job_bank(JOB["iw_rows"])
            for s in range(NB):
                mm = pe.transpose(b[:, s * H:(s + 1) * H], square[HD:HD + H, 0, s * P:(s + 1) * P],
                                  ident[HD:HD + H, HD:HD + H])
            mm.then_inc(turned, 1)
            for d in range((NB - 1) * H):
                blk, hh = d // H + 1, d % H
                if d < H and hh % 2 == 0:
                    tile_is_taken(pe, TILE["iq"] + hh // 2)
                w = P * (blk + 1)
                pe.matmul(job_bank(JOB["dots"] + d)[:, 0:w], iq_t[half_rows(hh), hh // 2, blk * P:(blk + 1) * P],
                          ik_t[half_rows(hh), 0:w], start=True, stop=True).then_inc(dots_done, 1)
            for name in ("q", "conv_c", "conv_x", "conv_b", "gate_a"):
                dense(name, name, h)
            dense("branch_a", "branch_a", chunks(a_hi1, a_lo1), ready=SPLIT["conv_1"])
            pe.wait_ge(strip_turned, 16)
            for hh in range(H):
                pe.matmul(job_bank(JOB["bias"] + hh)[:], flip, strip_t[:, hh, :], start=True, stop=True) \
                    .then_inc(bias_sum, 1)
            for c in range(CC):
                tile_is_taken(pe, TILE["q"] + c)
            attention(JOB["attn_1"], TILE["attn_1"], prob_t1, 0, False, FIRST["gate_b"],
                      lambda hh, blk: q_t[half_rows(hh), hh // 2, blk * P:(blk + 1) * P],
                      lambda hh, w: k_t[half_rows(hh), 0:w],
                      lambda hh, s: v_rows_1[:, s, :])
            for blk in range(NB):
                tile_is_taken(pe, TILE["attn_1"] + IN_ATTN["turned", blk])
            dense("branch_b", "branch_b", chunks(a_hi1, a_lo1))
            dense("w_out", "w_out", h, ready=SPLIT["merged_1"])
            sum_squares("norm_2")
            spread_inverse("norm_2")

            def modulation(job, c0, c1):
                b = job_bank(JOB[job])
                pe.wait_ge(ada_summed, ADA_SLABS)
                for n in range(c0, c1):
                    mm = pe.matmul(b[:, n:n + 1], ada_sum[:, n // 2, n % 2 * P:(n % 2 + 1) * P], ones[:, 0:1],
                                   start=True, stop=True)
                mm.then_inc(ada_done, 1)

            for half in range(2):
                n0, t0 = (FIRST["ffn_up"], FFN2)[half], TILE[f"ffn_up_{half}"]

                def up(n, i=0, per=0, n0=n0, t0=t0):
                    slab(n, i, per)
                    for q in range(2):
                        product(t0 + 2 * (n - n0) + q, n, q * P, h, i, per, 2 * per)

                if half == 0:
                    slab(n0)
                    products(t0, n0, 2, h, SPLIT["h2"])
                runs(pe, n0 + 1 - half, FH - 1 + half, up)
                down, t0 = n0 + FH, TILE[f"ffn_down_{half}"]
                for c in range(DC):
                    slab(down + c)
                    product(t0 + c, down + c, 0, chunks(f_hi, f_lo), ready=SPLIT[f"ffn_{half}"] if c == 0 else None)
                    if half == 1 and c == 3:
                        modulation("ada_a", 0, 2 * DC)
            sum_squares("norm_3")
            sum_squares("norm_x", gate)
            modulation("ada_b", 2 * DC, 6 * DC)

            dense("latents", "latents", h, ready=SPLIT["h3"])
            sum_squares("norm_q")
            sum_squares("norm_kv", gate)
            dense("glu_b", "glu_b", h, after_slab=lambda k: spread_inverse(("norm_q", "norm_kv")[k]))
            lat = lambda k: (l_hi[:, QC + k, :], l_lo[:, QC + k, :])
            for k in range(2):
                slab(AT["w_uq"][k])
                for q in range(3):
                    product(TILE[f"w_uq_{k}"] + q, AT["w_uq"][k], q * P, chunks(l_hi, l_lo),
                            ready=SPLIT["q_lat"] if k == 0 and q == 0 else None)
                if k == 1:
                    slab(AT["w_ukv"][0])
                    for q in range(4):
                        product(TILE["w_ukv_0"] + q, AT["w_ukv"][0], q * P, lat, ready=SPLIT["kv_lat"] if q == 0 else None)
                slab(AT["glu_a"][k])
                for q in range(2):
                    product(TILE[f"glu_a_{k}"] + q, AT["glu_a"][k], q * P, h)
            slab(AT["w_ukv"][1])
            for blk in range(NB):
                t = TILE["w_ukv_1"] + blk
                ps = tile_bank(t)
                hi, lo = parts(AT["w_ukv"][1])
                for k in range(KC):
                    if k == KC // 2:
                        second_half()
                    x_hi = l_hi[:, QC + k, blk * P:(blk + 1) * P]
                    x_lo = l_lo[:, QC + k, blk * P:(blk + 1) * P]
                    pe.matmul(ps[:], x_hi, hi[:, k, :], start=(k == 0), stop=False)
                    pe.matmul(ps[:], x_hi, lo[:, k, :], start=False, stop=False)
                    mm = pe.matmul(ps[:], x_lo, hi[:, k, :], start=False, stop=(k == KC - 1))
                mm.then_inc(tile_done, 1)
            pe.wait_ge(heads_ready, 3)
            for q in range(4):
                tile_is_taken(pe, TILE["w_ukv_0"] + q)
            attention(JOB["attn_2"], TILE["attn_2"], prob_t2, NB * H, True, FIRST["gate_conv"],
                      lambda hh, blk: q_h[0:QK_DIM, hh, blk * P:(blk + 1) * P],
                      lambda hh, w: k_h[0:QK_DIM, hh, 0:w],
                      lambda hh, s: v_rows_2[:, s, hh * HD:(hh + 1) * HD])
            for k in range(4):
                n = FIRST["gate_attn"] + 2 * k
                t = TILE["gate_and_o"] + 4 * k
                slab(n)
                for q in range(2):
                    product(t + q, n, q * P, h)
                if k == 0:
                    b = job_bank(JOB["ln_mean"])
                    pe.wait_ge(conv_done, CC - 1)
                    pe.wait_ge(tap_added, TAPS - 1)
                    for c in range(CC):
                        mm = pe.matmul(b[:], ones, convolved(c), start=(c == 0), stop=(c == CC - 1))
                    mm.then_inc(mean_done, 1)
                    tile_is_taken(pe, TILE["attn_2"] + IN_ATTN["turned", NB - 1])
                slab(n + 1)
                for q in range(2):
                    product(t + 2 + q, n + 1, q * P, chunks(o_hi, o_lo))
                if k == 0:
                    sum_squares("ln_var")
            dense("conv_out", "conv_out", chunks(c_hi, c_lo), ready=SPLIT["conv_2"])
            dense("w_out_2", "w_out_2", h, ready=SPLIT["merged_2"])
            sum_squares("norm_4")
            spread_inverse("norm_4")
            def expert_0_and_router():
                banks = [tile_bank(TILE["moe"]), tile_bank(TILE["moe"] + 1), job_bank(JOB["router"])]
                hi, lo = parts(n0)
                weights = [(hi[:, :, 0:P], lo[:, :, 0:P]), (hi[:, :, P:], lo[:, :, P:]), (router_hi[:], router_lo[:])]
                pe.wait_ge(router_split, 1)
                for k in range(DC):
                    if k == DC // 2:
                        second_half()
                    pe.wait_ge(split_done, SPLIT["h4"] + k + 1)
                    x_hi, x_lo = h(k)
                    for ps, (w_hi, w_lo), done in zip(banks, weights, (tile_done, tile_done, routed)):
                        pe.matmul(ps[:], w_hi[:, k, :], x_hi, start=(k == 0), stop=False)
                        pe.matmul(ps[:], w_lo[:, k, :], x_hi, start=False, stop=False)
                        mm = pe.matmul(ps[:], w_hi[:, k, :], x_lo, start=False, stop=(k == DC - 1))
                        if k == DC - 1:
                            mm.then_inc(done, 1)

            def turn_logits():
                job_is_taken(pe, JOB["router"])
                b, w = job_bank(JOB["router_rows"]), G + G * E
                for blk in range(NB):
                    mm = pe.transpose(b[:, blk * w:(blk + 1) * w], logits_t[:, blk * P:(blk + 1) * P], ident[0:w, 0:w])
                mm.then_inc(logits_turned, 1)

            def turn_weights():
                pe.wait_ge(weights_ready, 1)
                b = job_bank(JOB["combine"])
                for blk in range(NB):
                    mm = pe.transpose(b[0:G * E, blk * P:(blk + 1) * P], rt[:, 2, blk, :], ident)
                mm.then_inc(weights_turned, 1)

            n0 = FIRST["moe_up"]

            def moe_group(i, first):
                per, tiles = (0, 0) if first else (E + 4, 24)
                for e in range(E):
                    slab(n0 + e, i, per)
                    if first and e == 0:
                        expert_0_and_router()
                        continue
                    for q in range(2):
                        product(TILE["moe"] + 2 * e + q, n0 + e, q * P, h, i, 0, tiles)
                        if first and e == 1 and q == 0:
                            turn_logits()
                        if first and e == 2 and q == 0:
                            turn_weights()
                for d in range(4):
                    n = n0 + E + d
                    slab(n, i, per)
                    for q in range(2):
                        product(TILE["moe"] + 2 * (E + d) + q, n, q * P, chunks(e_hi, e_lo), i,
                                E if not first else 0, tiles,
                                ready=SPLIT["moe"] if d == 0 and q == 0 else None)

            moe_group(0, True)
            with pe.Fori(1, G) as i:
                moe_group(i, False)
            sum_squares("norm_out")
            spread_inverse("norm_out")

        @block.vector
        def _(dve):
            class Steps:
                n, i, per = 0, 0, 0

            def link(ins):
                Steps.n += 1
                ins.then_inc(step, 1)
                dve.wait_ge(step, Steps.n + Steps.i * Steps.per)

            def loop_runs(n0, count, body, size, steps):
                whole = count // size
                base = Steps.n
                with dve.Fori(0, whole) as i:
                    Steps.i, Steps.per = i, size * steps
                    for k in range(size):
                        body(n0 + k, i, size)
                assert Steps.n - base == size * steps
                Steps.n, Steps.i, Steps.per = base + whole * size * steps, 0, 0
                for n in range(n0 + whole * size, n0 + count):
                    body(n, 0, 0)

            def take(ins, t, i=0, per=0):
                ins.then_inc(bank_free[t % 4], 1)
                tile_is_taken(dve, t, i, per)

            def take_job(ins, j):
                ins.then_inc(bank_free[4 + j % 4], 1)
                job_is_taken(dve, j)

            def split(src, hi, lo):
                link(dve.tensor_copy(hi, src))
                dve.tensor_tensor(lo, src, hi.bitcast(F32), ALU.subtract).then_inc(split_done, 1)

            def squares(name, c, count, src, gain=None, parts=square):
                if c == 0 and parts is square:
                    dve.wait_ge(summed, 2 * NORMS[name])
                part = parts[:, 0 if c == 0 else 1, :]
                ins = (dve.tensor_tensor(part, src, src, ALU.mult) if gain is None else
                       dve.scalar_tensor_tensor(part, src, gain, src, ALU.mult, ALU.mult))
                if c == count - 1:
                    ins.then_inc(squared, 1)
                    return
                if c:
                    link(ins)
                    ins = dve.tensor_tensor(parts[:, 0, :], parts[:, 0, :], part, ALU.add)
                if c == count - 2:
                    ins.then_inc(squared, 1)
                    dve.wait_ge(squared, squares_done(name, 0))
                else:
                    link(ins)

            def inverse_mean(name, count=DC):
                j, slot = JOB[name], inv_mean[SPREAD[name] % 2]
                dve.wait_ge(summed, 2 * NORMS[name] + 2)
                take_job(dve.tensor_scalar(slot, bank[4 + j % 4][:, 0:NB], 1.0 / (count * P), EPS, ALU.mult, ALU.add), j)
                dve.reciprocal(slot, slot).then_inc(inverted, 1)

            def inverse(name):
                if name in SPREAD:
                    job_is_taken(dve, JOB[name + "_all"])
                    return
                job_is_taken(dve, JOB[name])
                r = rstd[:, NORMS[name] % 2, :]
                link(dve.reciprocal(r, r))

            made = [0]

            def two_parts(first, count, put, hi, lo, shift=None):
                def low(c):
                    dve.wait_ge(high, made[0] + c + 1)
                    t, t_hi = tmp[:, c % 2, :], hi[:, c, :].bitcast(F32)
                    ins = (dve.tensor_tensor(lo[:, c, :], t, t_hi, ALU.subtract) if shift is None else
                           dve.scalar_tensor_tensor(lo[:, c, :], t, ada[:, shift + c:shift + c + 1], t_hi,
                                                    ALU.add, ALU.subtract))
                    ins.then_inc(split_done, 1)

                for c in range(count):
                    if c >= 2:
                        low(c - 2)
                        dve.wait_ge(split_done, first + c - 1)
                    put(c, tmp[:, c % 2, :]).then_inc(normed, 1)
                low(count - 2)
                low(count - 1)
                dve.wait_ge(split_done, first + count)
                made[0] += count

            def normalized(name, first, count, src, gain, hi, lo, shift=None):
                two_parts(first, count, lambda c, slot: normalize(name, src(c), gain(c), slot), hi, lo, shift)

            def normalize(name, src, gain, out_ap):
                return dve.scalar_tensor_tensor(out_ap, src, gain, rstd[:, NORMS[name] % 2, :], ALU.mult, ALU.mult)

            def tile(t, i=0, per=0):
                tile_is_done(dve, t, i, per)
                return bank[t % 4]

            def attention_logits(r, base_j, first, full):
                blk, hh = r // H, r % H
                w = SEQ if full else P * (blk + 1)
                j = base_j + attn_jobs(r, "logits")
                b = bank[4 + j % 4]
                dve.wait_ge(logits_done, first + r + 1)
                if r >= 2:
                    dve.wait_ge(probs_turned, first + r - 1)
                p = square[:, r % 2, 0:w]
                if full:
                    dve.tensor_tensor_reduce(p, b[:, 0:w], gate[:, blk % 2, :], -float(QK_DIM) ** -0.5, 3e38,
                                             ALU.add, ALU.min, neg_max[:, r % 2:r % 2 + 1]) \
                        .then_inc(bank_free[4 + j % 4], 1)
                else:
                    off = P * blk * (blk + 1) // 2
                    link(dve.tensor_tensor(p, b[:, 0:w], bias[:, hh, SEQ - w:], ALU.add))
                    dve.tensor_tensor_reduce(p, p, mask_1[:, off:off + w], -1.0, 3e38,
                                             ALU.add, ALU.min, neg_max[:, r % 2:r % 2 + 1]) \
                        .then_inc(bank_free[4 + j % 4], 1)

            def attention_rows(blk, base_t, first):
                dve.wait_ge(probs_ready, first + H * (blk + 1))
                link(dve.reciprocal(inv_sums[:, blk, :], sums[:, blk, :]))
                t = base_t + IN_ATTN["values", blk]
                take(dve.tensor_tensor(tmp[:, blk % 2, :].rearrange("p (h d) -> p h d", d=HD),
                                       tile(t)[:].rearrange("p (h d) -> p h d", d=HD),
                                       inv_sums[:, blk, :].unsqueeze(2).to_broadcast([P, H, HD]), ALU.mult), t)

            def attention_split(blk, base_t, hi, lo):
                t = base_t + IN_ATTN["turned", blk]
                b = tile(t)[:].rearrange("p (c t) -> p c t", t=P)
                cols = slice(blk * P, (blk + 1) * P)
                link(dve.tensor_copy(hi[:, :, cols], b))
                take(dve.tensor_tensor(lo[:, :, cols], b, hi[:, :, cols].bitcast(F32), ALU.subtract), t)

            def attention(base_j, base_t, first, full, hi, lo, before=None, between=None):
                for r in range(NB * H):
                    if before and r % H == 0:
                        before(r // H)
                    attention_logits(r, base_j, first, full)
                    if r % H == 2 and r > H:
                        attention_rows(r // H - 1, base_t, first)
                    if r % H == 6 and r > H:
                        attention_split(r // H - 1, base_t, hi, lo)
                    if between:
                        between(r)
                attention_rows(NB - 1, base_t, first)
                attention_split(NB - 1, base_t, hi, lo)

            for c in range(0, DC, 2):
                dve.wait_ge(x_loaded[c // 2], 16)
                link(dve.tensor_tensor(y1[:, c, :], x[:, c, :], x[:, c, :], ALU.mult))
                dve.wait_ge(x_squared, c // 2 + 1)
                dve.tensor_tensor(y1[:, c, :], y1[:, c, :], y1[:, c + 1, :], ALU.add).then_inc(pair_squared, 1)
            dve.wait_ge(col_loaded, 16)
            inverse_mean("norm_1")
            inverse("norm_1")
            normalized("norm_1", SPLIT["h1"], DC, lambda c: x[:, c, :], lambda c: column("g_mix", c), h_hi, h_lo)
            dve.wait_ge(strip_sum, 2)
            for j, (d0, d1) in enumerate(((0, SEQ), (SEQ, GELEM))):
                jj = JOB["strip"] + j
                take_job(dve.tensor_copy(m["strip"][:, d0:d1], bank[4 + jj % 4][0:H, 0:d1 - d0]), jj)
            t = TILE["kv_ikw"]
            b = tile(t)
            dve.tensor_copy(k_t[0:HD, :], b[0:HD, :])
            dve.tensor_copy(k_t[HD:P, :], b[0:HD, :])
            take(dve.tensor_copy(v_t[HD:P, :], b[HD:P, :]), t)
            b = tile(t + 1)
            dve.tensor_copy(ik_t[0:HD, :], b[0:HD, :])
            dve.tensor_copy(ik_t[HD:P, :], b[0:HD, :])
            take(dve.tensor_scalar(square[HD:HD + H, 0, :], b[HD:HD + H, :], H ** -0.5 * HD ** -0.5, None, ALU.mult), t + 1)
            for c in range(CC):
                t = TILE["iq"] + c
                take(dve.tensor_copy(iq_t[:, c, :], tile(t)[:]), t)
            for n, (dst, name) in enumerate(((v_rows_1[:], "v_rows"), (iw_rows, "iw_rows"))):
                j = JOB[name]
                dve.wait_ge(turned, n + 1)
                w = dst.shape[2] * NB
                take_job(dve.tensor_copy(dst, bank[4 + j % 4][:, 0:w].rearrange("p (b d) -> p b d", b=NB)), j)
            score_at = {blk: (P * (blk * (blk + 1) // 2 - 1), P * (blk + 1)) for blk in range(1, NB)}
            for d in range((NB - 1) * H):
                blk, hh = d // H + 1, d % H
                off, w = score_at[blk]
                sc = score[:, off:off + w]
                job_is_taken(dve, JOB["dots"] + d)
                iw = iw_rows[:, blk, hh:hh + 1]
                if hh == 0:
                    dve.tensor_scalar(sc, gate[:, d % 2, 0:w], iw, None, ALU.mult).then_inc(dots_used, 1)
                else:
                    dve.scalar_tensor_tensor(sc, gate[:, d % 2, 0:w], iw, sc, ALU.mult, ALU.add).then_inc(dots_used, 1)
                dve.wait_ge(dots_used, d + 1)
                if hh == H - 1:
                    link(dve.scalar_tensor_tensor(sc[:, w - P:w], const("after", P), FILL, sc[:, w - P:w],
                                                  ALU.mult, ALU.add))
            link(dve.tensor_scalar(mask_1[:, 0:P], const("after", P), NEG, None, ALU.mult))

            def top_k():
                for blk in range(1, NB):
                    off, w = score_at[blk]
                    src, dst = score[:, off:off + w], work[:, off:off + w]
                    for n in range(K_TOP // 8):
                        link(dve.max(top8, src if n == 0 else dst))
                        link(dve.match_replace(dst, top8, src if n == 0 else dst, TAKEN))
                        yield
                    mk = mask_1[:, off + P:off + P + w]
                    link(dve.tensor_tensor(mk, dst, src, ALU.is_equal))
                    link(dve.tensor_scalar(mk, mk, NEG, None, ALU.mult))
                    yield

            def advance(work_left, n):
                for _ in range(n):
                    next(work_left, None)

            selection = top_k()
            for c in range(CC):
                t = TILE["q"] + c
                take(dve.tensor_scalar(q_t[:, c, :], tile(t)[:], HD ** -0.5, None, ALU.mult), t)
                advance(selection, 3)
            dve.wait_ge(strip_stored, 16)
            link(dve.memset(conv_in[:, :, 0:2], 0.0))
            for c in range(CC):
                t = TILE["conv_c"] + c
                take(dve.tensor_copy(conv_in[:, c, 2:], tile(t)[:]), t)
                advance(selection, 4)
            for c in range(CC):
                t = TILE["conv_x"] + c
                take(dve.tensor_tensor(conv_in[:, c, 2:], conv_in[:, c, 2:], tile(t)[:], ALU.mult), t)
                advance(selection, 4)
            for c in range(CC):
                mid = conv_mid[:, c % 2, :]
                for tap in range(3):
                    src, w_tap = conv_in[:, c, tap:tap + SEQ], column("conv_w", tap * CC + c)
                    link(dve.tensor_scalar(mid, src, w_tap, None, ALU.mult) if tap == 0 else
                         dve.scalar_tensor_tensor(mid, src, w_tap, mid, ALU.mult, ALU.add))
                t = TILE["conv_b"] + c
                take(dve.tensor_tensor(tmp[:, c % 2, :], mid, tile(t)[:], ALU.mult), t)
                split(tmp[:, c % 2, :], a_hi1[:, c, :], a_lo1[:, c, :])
                advance(selection, 1)
            advance(selection, 100)
            for c in range(DC):
                t = TILE["branch_a"] + c
                tile_is_taken(dve, TILE["gate_a"] + c)
                take(dve.tensor_tensor(y1[:, c, :], y1[:, c, :], tile(t)[:], ALU.mult), t)
            for hh in range(H):
                j = JOB["bias"] + hh
                dve.wait_ge(bias_sum, hh + 1)
                take_job(dve.tensor_copy(bias[:, hh, :], bank[4 + j % 4][:]), j)
            attention(JOB["attn_1"], TILE["attn_1"], 0, False, a_hi1, a_lo1)
            def merged_1(c, slot):
                t = TILE["branch_b"] + c
                dve.wait_ge(gate_ready, c + 1)
                take(dve.tensor_tensor(slot, x[:, c, :], tile(t)[:], ALU.mult), t)
                return dve.tensor_tensor(slot, slot, y1[:, c, :], ALU.add)

            two_parts(SPLIT["merged_1"], DC, merged_1, h_hi, h_lo)
            for c in range(DC):
                t = TILE["w_out"] + c
                if c % (DC // 2) == 0:
                    dve.wait_ge(x_again[c // (DC // 2)], 16)
                take(dve.tensor_tensor(x[:, c, :], x[:, c, :], tile(t)[:], ALU.add), t)
                squares("norm_2", c, DC, x[:, c, :])
            inverse_mean("norm_2")
            inverse("norm_2")
            normalized("norm_2", SPLIT["h2"], DC, lambda c: x[:, c, :], lambda c: column("g_ffn", c), h_hi, h_lo)
            link(dve.tensor_tensor(g_final_2[:], column("g_final", 0, DC), column("g_final", 0, DC), ALU.mult))
            dve.wait_ge(c_ready, 1)

            def modulation(s, i=0, per=0, slot=0):
                dve.wait_ge(ada_full[slot], 16 * (s // 2 + 1) + i * (per // 2 * 16))
                w_ada = ada_raw[:, slot, :].rearrange("p (k c) -> p k c", c=256)
                total = ada_sum[:, bass.ds(s + i * per, 1), :].rearrange("p a c -> p (a c)")
                for k in range(DC):
                    if k == 0:
                        ins = dve.tensor_scalar(total, w_ada[:, k, :], c_act[:, k:k + 1], None, ALU.mult)
                    else:
                        ins = dve.scalar_tensor_tensor(total, w_ada[:, k, :], c_act[:, k:k + 1], total, ALU.mult, ALU.add)
                    if k < DC - 1:
                        link(ins)
                    else:
                        ins.then_inc(ada_summed, 1)

            def take_modulation(job, c0, c1):
                j = JOB[job]
                take_job(dve.tensor_tensor(ada[:, c0:c1], bank[4 + j % 4][:, c0:c1], column("ada_b", c0, c1 - c0),
                                           ALU.add), j)

            def gain_of(n, at, gain):
                link(dve.tensor_scalar(mod[:, n, :], ada[:, at:at + DC], 1.0, None, ALU.add))
                link(dve.tensor_tensor(mod[:, n, :], mod[:, n, :], column(gain, 0, DC), ALU.mult))

            def rotary_angles():
                dve.wait_ge(pos_loaded, 32)
                link(dve.tensor_copy(pos_row[:], pos_raw.bitcast(I32)))
                link(dve.tensor_copy(pos_col, pos_col_raw))
                link(dve.tensor_scalar(angle, pos_row[:], const("inv_freq"), None, ALU.mult))
                link(dve.tensor_scalar(turn, angle, 1.0 / (2.0 * np.pi), 12582912.0, ALU.mult, ALU.add))
                link(dve.tensor_scalar(turn, turn, -12582912.0, None, ALU.add))
                for part in (6.28125, 0.0019359588623046875, 2.0 * np.pi - 6.28125 - 0.0019359588623046875):
                    link(dve.scalar_tensor_tensor(angle, turn, -part, angle, ALU.mult, ALU.add))
                link(dve.tensor_scalar(turn, angle, np.pi / 2, None, ALU.add))
                link(dve.tensor_scalar(pos_raw, turn, np.pi, -2.0 * np.pi, ALU.is_gt, ALU.mult))
                link(dve.tensor_tensor(turn, turn, pos_raw, ALU.add))
                link(dve.tensor_scalar(turn, turn, 3.1415925, -3.1415925, ALU.min, ALU.max))
                dve.tensor_scalar(angle, angle, 3.1415925, -3.1415925, ALU.min, ALU.max).then_inc(angles_ready, 1)

            for half in range(2):
                n0, t0, s0 = (FIRST["ffn_up"], FFN2)[half], TILE[f"ffn_up_{half}"], half * (FH + 2)

                def up(n, i=0, per=0, n0=n0, t0=t0, s0=s0):
                    k, t = n - n0, t0 + 2 * (n - n0)
                    tile_is_taken(dve, t, i, 2 * per)
                    take(dve.tensor_tensor(tmp[:, k % 2, :], gate[:, k % 2, :], tile(t + 1, i, 2 * per)[:], ALU.mult),
                         t + 1, i, 2 * per)
                    chunk = bass.ds(k + i * per, 1)
                    split(tmp[:, k % 2, :], f_hi[:, chunk, :].rearrange("p a t -> p (a t)"),
                          f_lo[:, chunk, :].rearrange("p a t -> p (a t)"))
                    modulation(s0 + k, i, per, (s0 + k) % 2)

                loop_runs(n0, FH, up, 2, DC)
                down, t0 = n0 + FH, TILE[f"ffn_down_{half}"]

                def add_down(n, i=0, per=0, down=down, t0=t0):
                    t, chunk = t0 + n - down, bass.ds(n - down + i * per, 1)
                    xc = x[:, chunk, :].rearrange("p a t -> p (a t)")
                    take(dve.tensor_tensor(xc, xc, tile(t, i, per)[:], ALU.add), t, i, per)

                if half == 0:
                    for c in range(DC):
                        add_down(down + c)
                        if c in (4, 5):
                            modulation(FH + c - 4, slot=(FH + c - 4) % 2)
                else:
                    for c in range(DC):
                        add_down(down + c)
                        squares("norm_3", c, DC, x[:, c, :], gain=g_final_2[:, c:c + 1])
                        squares("norm_x", c, DC, x[:, c, :], parts=gate)
                        if c == 4:
                            rotary_angles()
                        if c == 5:
                            dve.wait_ge(ada_done, 1)
                            take_modulation("ada_a", 0, 2 * DC)
                            gain_of(0, DC, "norm1_g")
                            link(dve.tensor_tensor(mod[:, 0, :], mod[:, 0, :], column("g_final", 0, DC), ALU.mult))

            r_3, r_x = rstd[:, NORMS["norm_3"] % 2, :], v_rows_2[:, NB - 1, :]
            bank_b, bank_a = bank[4 + JOB["norm_3"] % 4], bank[4 + JOB["norm_x"] % 4]
            dve.wait_ge(summed, 2 * NORMS["norm_x"] + 2)
            link(dve.tensor_scalar(r_3, bank_a[:], EPS / D, EPS * EPS, ALU.mult, ALU.add))
            take_job(dve.scalar_tensor_tensor(r_3, bank_b[:], 1.0 / D, r_3, ALU.mult, ALU.add), JOB["norm_3"])
            dve.reciprocal(r_3, r_3).then_inc(var_ready, 1)
            dve.wait_ge(rstd_ready, 1)
            normalized("norm_3", SPLIT["h3"], DC, lambda c: x[:, c, :], lambda c: mod[:, 0, c:c + 1], h_hi, h_lo, shift=0)
            dve.wait_ge(ada_done, 2)
            take_modulation("ada_b", 2 * DC, 6 * DC)
            gain_of(1, 4 * DC, "norm2_g")
            dve.memset(u[:, :, 0:TAPS - 1], 0.0).then_inc(pads_ready, 1)
            dve.wait_ge(pads_ready, 1)
            q_latent, kv_latent = q_h[:, 0:QC, :], q_h[:, H - KC:, :]
            for c in range(QC):
                t = TILE["latents"] + c
                take(dve.tensor_copy(q_latent[:, c, :], tile(t)[:]), t)
                squares("norm_q", c, QC, q_latent[:, c, :])
            for c in range(KC):
                t = TILE["latents"] + QC + c
                take(dve.tensor_copy(kv_latent[:, c, :], tile(t)[:]), t)
                squares("norm_kv", c, KC, kv_latent[:, c, :], parts=gate)
            inverse_mean("norm_q", QC)
            inverse_mean("norm_kv", KC)
            dve.wait_ge(rope_ready, 2)
            link(dve.tensor_scalar(rope_sin, rope_sin, const("rope_sign"), None, ALU.mult))

            def rotate(t, rows):
                take(dve.tensor_copy(turn[0:rows, :], tile(t)[0:rows, :]), t)
                link(dve.stream_shuffle(angle[0:rows, :], turn[0:rows, :],
                                        [(r + ROPE // 2) % ROPE for r in range(ROPE)]))
                link(dve.tensor_tensor(turn[0:rows, :], turn[0:rows, :], rope_cos[0:rows, :], ALU.mult))
                link(dve.tensor_tensor(angle[0:rows, :], angle[0:rows, :], rope_sin[0:rows, :], ALU.mult))

            rotate(TILE["latents"] + QC + KC, ROPE)
            link(dve.tensor_tensor(k_h[HD:QK_DIM, 0, :], turn[0:ROPE, :], angle[0:ROPE, :], ALU.add))
            dve.tensor_copy(k_h[HD:QK_DIM, 1:, :], k_h[HD:QK_DIM, 0:1, :].to_broadcast([ROPE, H - 1, SEQ])) \
                .then_inc(heads_ready, 1)

            def latent(name, source, c0, count):
                inverse("norm_" + name)
                normalized("norm_" + name, SPLIT[name + "_lat"], count, lambda c: source[:, c, :],
                           lambda c: column(name + "_norm_g", c), l_hi[:, c0:, :], l_lo[:, c0:, :])

            latent("q", q_latent, 0, QC)
            job_is_taken(dve, JOB["norm_x"])
            link(dve.reciprocal(r_x, r_x))

            def convolution():
                for c in range(CC - 1):
                    dst = convolved(c)
                    for tap in range(TAPS):
                        src, w_tap = u[:, c + 1, tap:tap + SEQ], column("conv_w_2", tap * CC + c)
                        if tap == 0:
                            link(dve.tensor_scalar(dst, src, w_tap, column("conv_b", c), ALU.mult, ALU.add))
                        elif tap < TAPS - 1:
                            link(dve.scalar_tensor_tensor(dst, src, w_tap, dst, ALU.mult, ALU.add))
                        else:
                            dve.scalar_tensor_tensor(dst, src, w_tap, dst, ALU.mult, ALU.add).then_inc(conv_done, 1)
                            dve.wait_ge(conv_done, c + 1)
                        yield

            taps = convolution()

            for half in range(2):
                rotate(TILE[f"w_uq_{half}"] + 2, P)
                for q in range(4):
                    ins = dve.tensor_tensor(q_h[HD:QK_DIM, 4 * half + q, :], turn[32 * q:32 * (q + 1), :],
                                            angle[32 * q:32 * (q + 1), :], ALU.add)
                ins.then_inc(heads_ready, 1)
                dve.wait_ge(heads_ready, 2 + half)
                if half == 0:
                    latent("kv", kv_latent, QC, KC)
                else:
                    for c in range(DC):
                        ins = dve.scalar_tensor_tensor(x[:, c, :], x[:, c, :], column("g_final", c), r_x, ALU.mult, ALU.mult)
                    ins.then_inc(y_done, 1)
                for c in (2 * half, 2 * half + 1):
                    t = TILE[f"glu_a_{half}"] + c % 2
                    tile_is_taken(dve, TILE["glu_b"] + c)
                    take(dve.tensor_tensor(u[:, c + 1, TAPS - 1:], u[:, c + 1, TAPS - 1:], tile(t)[:], ALU.mult), t)
                advance(taps, 4)

            def mask(blk):
                link(dve.tensor_scalar(gate[:, blk % 2, :], pos_row[:], pos_col[:, blk:blk + 1], NEG, ALU.is_gt, ALU.mult))

            attention(JOB["attn_2"], TILE["attn_2"], NB * H, True, o_hi, o_lo, before=mask,
                      between=lambda r: advance(taps, 2 if r % H in (0, 2, 6) else 3))
            advance(taps, TAPS * CC)

            def gated(k):
                for c in (2 * k, 2 * k + 1):
                    t = TILE["gate_and_o"] + 4 * k + 2 + c % 2
                    tile_is_taken(dve, t - 2)
                    take(dve.tensor_tensor(q_h[:, c, :], gate[:, c % 2, :], tile(t)[:], ALU.mult), t)

            mean = prob_t2[:, 0, :]
            j = JOB["ln_mean"]
            dve.wait_ge(mean_done, 1)
            take_job(dve.tensor_scalar(mean, bank[4 + j % 4][:], 1.0 / (CC * P), None, ALU.mult), j)
            for c in range(CC):
                link(dve.tensor_tensor(convolved(c), convolved(c), mean, ALU.subtract))
                squares("ln_var", c, CC, convolved(c))
            gated(0)
            inverse("ln_var")
            for c in range(CC):
                dve.tensor_tensor(convolved(c), convolved(c), rstd[:, NORMS["ln_var"] % 2, :], ALU.mult) \
                    .then_inc(scaled, 1)
            gated(1)
            for c in range(CC):
                dve.wait_ge(silu_done, c + 1)
                split(convolved(c), c_hi[:, c, :], c_lo[:, c, :])
            gated(2)
            gated(3)

            def merged_2(c, slot):
                t = TILE["conv_out"] + c
                dve.wait_ge(gate_ready, DC + c + 1)
                take(dve.tensor_tensor(slot, gate_conv[:, c, :], tile(t)[:], ALU.mult), t)
                return dve.tensor_tensor(slot, slot, q_h[:, c, :], ALU.add)

            two_parts(SPLIT["merged_2"], DC, merged_2, h_hi, h_lo)
            for c in range(DC):
                if c == DC // 2:
                    dve.wait_ge(router_loaded, 32)
                    link(dve.tensor_copy(router_hi[:], router_w[:]))
                    dve.tensor_tensor(router_lo[:], router_w[:], router_hi[:].bitcast(F32), ALU.subtract) \
                        .then_inc(router_split, 1)
                t = TILE["w_out_2"] + c
                take(dve.scalar_tensor_tensor(x[:, c, :], tile(t)[:], ada[:, 2 * DC + c:2 * DC + c + 1], x[:, c, :],
                                              ALU.mult, ALU.add), t)
                squares("norm_4", c, DC, x[:, c, :])
            inverse_mean("norm_4")
            inverse("norm_4")
            normalized("norm_4", SPLIT["h4"], DC, lambda c: x[:, c, :], lambda c: mod[:, 1, c:c + 1], h_hi, h_lo, shift=3 * DC)

            def hidden(e, i=0):
                t = TILE["moe"] + 2 * e
                tile_is_taken(dve, t, i, 24)
                take(dve.tensor_tensor(tmp[:, e % 2, :], gate[:, e % 2, :], tile(t + 1, i, 24)[:], ALU.mult),
                     t + 1, i, 24)

            def weighted(e, i=0):
                dve.wait_ge(comb_full[e % 2], 16 * (e // 2 + 1) + i * (E // 2 * 16))
                dve.tensor_tensor(tmp[:, e % 2, :], tmp[:, e % 2, :], comb[:, e % 2, :], ALU.mult) \
                    .then_inc(comb_used, 1)
                dve.wait_ge(comb_used, e + 1 + i * E)
                split(tmp[:, e % 2, :], e_hi[:, e, :], e_lo[:, e, :])

            def small(v, n):
                return rt[:, v, :, 0:n]

            def wide(t, n):
                return t.to_broadcast([P, NB, n])

            def first_best(values, best, n, key, out_ap):
                link(dve.tensor_tensor(key, values, wide(best, n), ALU.is_equal))
                link(dve.tensor_tensor(key, key, const("ramp", n).unsqueeze(1).to_broadcast([P, NB, n]), ALU.mult))
                link(dve.tensor_reduce(small(13, 1), key, AX.X, ALU.max))
                link(dve.tensor_tensor(out_ap, key, wide(small(13, 1), n), ALU.is_equal))

            dve.wait_ge(routed, 1)
            j = JOB["router"]
            dve.wait_ge(router_loaded, 32)
            take_job(dve.tensor_copy(logits_t[:], bank[4 + j % 4][0:G + G * E, :]), j)
            hidden(0)
            dve.wait_ge(logits_turned, 1)
            j = JOB["router_rows"]
            logits_g, logits_e = small(3, G), small(4, G * E)
            b = bank[4 + j % 4][:, 0:NB * 36].rearrange("p (b e) -> p b e", b=NB)
            link(dve.tensor_tensor(logits_g, b[:, :, 0:G], router_b[:, 0:G].unsqueeze(1).to_broadcast([P, NB, G]), ALU.add))
            take_job(dve.tensor_tensor(logits_e, b[:, :, G:], router_b[:, G:].unsqueeze(1).to_broadcast([P, NB, G * E]),
                                       ALU.add), j)
            best, group, key = small(5, 1), small(6, G), small(12, E)
            link(dve.tensor_reduce(best, logits_g, AX.X, ALU.max))
            dve.tensor_tensor(small(0, G), logits_g, wide(best, G), ALU.subtract).then_inc(shift_ready, 1)
            first_best(logits_g, best, G, small(12, G), group)
            four = rt[:, 2, :, :].rearrange("p b (g e) -> p b g e", g=G)
            link(dve.tensor_tensor(four, logits_e.rearrange("p b (g e) -> p b g e", g=G),
                                   group.unsqueeze(3).to_broadcast([P, NB, G, E]), ALU.mult))
            chosen, best_e = small(7, E), small(8, 1)
            link(dve.tensor_reduce(chosen, rt[:, 2, :, :].rearrange("p b (g e) -> p b e g", g=G), AX.X, ALU.add))
            link(dve.tensor_reduce(best_e, chosen, AX.X, ALU.max))
            dve.tensor_tensor(small(1, E), chosen, wide(best_e, E), ALU.subtract).then_inc(shift_ready, 1)
            top, second, rest = small(9, E), small(10, E), small(11, E)
            first_best(chosen, best_e, E, key, top)
            link(dve.scalar_tensor_tensor(rest, top, NEG, chosen, ALU.mult, ALU.add))
            link(dve.tensor_reduce(best_e, rest, AX.X, ALU.max))
            first_best(rest, best_e, E, key, second)
            link(dve.tensor_tensor(top, top, second, ALU.add))
            dve.wait_ge(exp_ready, 2)
            total, scale_w = small(5, 1), small(8, 1)
            link(dve.tensor_reduce(total, small(0, G), AX.X, ALU.add))
            link(dve.tensor_tensor(top, top, small(1, E), ALU.mult))
            link(dve.tensor_reduce(scale_w, top, AX.X, ALU.add))
            link(dve.tensor_tensor(scale_w, scale_w, total, ALU.mult))
            link(dve.reciprocal(scale_w, scale_w))
            link(dve.tensor_tensor(top, top, wide(scale_w, E), ALU.mult))
            dve.tensor_tensor(four, top.unsqueeze(2).to_broadcast([P, NB, G, E]),
                              group.unsqueeze(3).to_broadcast([P, NB, G, E]), ALU.mult).then_inc(weights_ready, 1)
            hidden(1)
            dve.wait_ge(weights_turned, 1)
            j = JOB["combine"]
            dve.tensor_copy(comb_t[:], bank[4 + j % 4][0:G * E, :]).then_inc(bank_free[4 + j % 4], 1)

            def moe_group(i, first, last):
                for e in range(E):
                    if not (first and e < 2):
                        hidden(e, i)
                        weighted(e, i)
                for c in range(DC):
                    t = TILE["moe"] + 2 * E + c
                    take(dve.scalar_tensor_tensor(x[:, c, :], tile(t, i, 24)[:], ada[:, 5 * DC + c:5 * DC + c + 1],
                                                  x[:, c, :], ALU.mult, ALU.add), t, i, 24)
                    if last:
                        squares("norm_out", c, DC, x[:, c, :])

            weighted(0)
            weighted(1)
            moe_group(0, True, False)
            base = Steps.n - E
            with dve.Fori(1, G - 1) as i:
                Steps.n, Steps.i, Steps.per = base, i, E
                moe_group(i, False, False)
            assert Steps.n - base == E
            Steps.n, Steps.i, Steps.per = base + (G - 1) * E, 0, 0
            moe_group(G - 1, False, True)
            inverse_mean("norm_out")
            inverse("norm_out")
            for c in range(DC):
                normalize("norm_out", x[:, c, :], column("final_norm_g", c), x[:, c, :]).then_inc(out_ready, 1)


def bucket_of(distance):
    n = np.maximum(distance, 0)
    large = MAX_EXACT + (np.log(np.maximum(n, 1) / MAX_EXACT) / np.log(MAX_DISTANCE / MAX_EXACT)
                         * (N_BUCKETS - MAX_EXACT)).astype(np.int64)
    return np.where(n < MAX_EXACT, n, np.minimum(large, N_BUCKETS - 1))


def constants():
    c = np.zeros((P, CONST["end"]), np.float32)
    i = np.arange(P)
    c[:, CONST["ident"]:][:, :P] = i[:, None] == i[None, :]
    c[:, CONST["flip"]:][:, :P] = i[:, None] == P - 1 - i[None, :]
    c[:, CONST["ones"]:][:, :P] = 1.0
    c[:, CONST["after"]:][:, :P] = i[None, :] > i[:, None]
    c[:, CONST["ramp"]:][:, :E] = E - np.arange(E)
    c[:, CONST["inv_freq"]] = np.float32(10000.0) ** (-(np.arange(P) % (ROPE // 2) * 2).astype(np.float32) / np.float32(ROPE))
    c[:, CONST["rope_sign"]] = np.where(i % ROPE < ROPE // 2, -1.0, 1.0)
    c[:, CONST["eps"]] = EPS
    onehot = bucket_of(SEQ - 1 - np.arange(GELEM))[None, :] == np.arange(N_BUCKETS)[:, None]
    return c, onehot.astype(np.float32)


def lay_out_slabs(v):
    w_in, w_in_2 = v["w_in"][0], v["w_in_2"][0]
    gate_up = [v["w_ffn_gate"][0], v["w_ffn_up"][0]]
    w_uq, w_ukv = v["w_uq_2"][0], v["w_ukv_2"][0]
    at_in = np.cumsum([0, 512, 512, 512, 512, 64, 64, 512, 64, 8, D, D])
    at_in2 = np.cumsum([0, Q_RANK, KV_RANK, ROPE, 512, 512, D, D])
    pack = np.zeros((NS, P, SLAB), np.float32)

    def put(n, blocks):
        kc, c = SLABS[n][1:]
        dst = pack[n, :, :kc * c].reshape(P, kc, c)
        c0 = 0
        for b in blocks:
            dst[:, :, c0:c0 + b.shape[1]] = b.reshape(kc, P, b.shape[1]).transpose(1, 0, 2)
            c0 += b.shape[1] if b.shape[1] % HD == 0 else P - c0 % P
    count = {}
    for n, (name, kc, c) in enumerate(SLABS):
        k = count[name] = count.get(name, -1) + 1
        cols = slice(k * c, (k + 1) * c)
        if name == "kv_ikw":
            put(n, [w_in[:, at_in[4]:at_in[6]], w_in[:, at_in[7]:at_in[8]], w_in[:, at_in[8]:at_in[9]]])
        elif name in ("iq", "q", "conv_c", "conv_x", "conv_b", "gate_a", "gate_b"):
            first = at_in[{"conv_b": 0, "conv_c": 1, "conv_x": 2, "q": 3, "iq": 6, "gate_a": 9, "gate_b": 10}[name]]
            put(n, [w_in[:, first + k * c:first + (k + 1) * c]])
        elif name in ("branch_a", "branch_b", "w_out"):
            put(n, [v[{"branch_a": "w_branch_a", "branch_b": "w_branch_b", "w_out": "w_out"}[name]][0][:, cols]])
        elif name == "ffn_up":
            put(n, [w[:, k * P:(k + 1) * P] for w in gate_up])
        elif name == "ffn_down":
            half, q = divmod(k, DC)
            put(n, [v["w_ffn_down"][0][half * FH * P:(half + 1) * FH * P, q * P:(q + 1) * P]])
        elif name == "latents":
            first = [w_in_2[:, :256], w_in_2[:, 256:512], w_in_2[:, 512:at_in2[3]]][k]
            put(n, [first[:, :P], first[:, P:]])
        elif name in ("glu_a", "glu_b", "gate_attn", "gate_conv"):
            first = at_in2[{"glu_a": 3, "glu_b": 4, "gate_attn": 5, "gate_conv": 6}[name]]
            put(n, [w_in_2[:, first + k * c:first + (k + 1) * c]])
        elif name == "w_uq":
            heads = w_uq.reshape(Q_RANK, H, QK_DIM)[:, 4 * k:4 * k + 4]
            put(n, [heads[:, :, :HD].reshape(Q_RANK, -1), heads[:, :, HD:].reshape(Q_RANK, -1)])
        elif name == "w_ukv":
            heads = w_ukv.reshape(KV_RANK, H, 2 * HD)
            put(n, [heads[:, :, k * HD:(k + 1) * HD].reshape(KV_RANK, -1)])
        elif name in ("conv_out", "o_attn", "w_out_2"):
            put(n, [v[{"conv_out": "w_conv_out_2", "o_attn": "w_o_attn_2", "w_out_2": "w_out_2"}[name]][0][:, cols]])
        elif name == "moe_up":
            g, e = divmod(k, E)
            put(n, [v["expert_w_gate_2"][0, g, e], v["expert_w_up_2"][0, g, e]])
        elif name == "moe_down":
            g, q = divmod(k, 4)
            put(n, [v["expert_w_down_2"][0, g].reshape(E * P, D)[:, q * 256:(q + 1) * 256]])
    ada = v["ada_w_2"][0].reshape(DC, P, ADA_SLABS, 256).transpose(2, 1, 0, 3).reshape(ADA_SLABS, P, SLAB)
    return pack, np.ascontiguousarray(ada)


def kernel(**inputs):
    import concourse.bacc as _bacc
    from concourse.bass_utils import run_bass_kernel_spmd as _run

    v = {k: np.asarray(x) for k, x in inputs.items()}
    pack, ada = lay_out_slabs(v)

    def columns(x):
        return x.reshape(-1, P).T

    order = ["g_mix", "b_gate", "conv_w", "g_ffn", "g_final", "c_2", "ada_b_2", "norm1_g_2", "norm2_g_2",
             "q_norm_g_2", "kv_norm_g_2", "conv_w_2", "conv_b_2", "conv_ln_g_2", "conv_ln_b_2", "final_norm_g_2"]
    const, onehot = constants()
    router_w = np.concatenate([v["router_group_w_2"][0], v["router_expert_w_2"][0]], axis=1)
    arrays = {
        "x_t": v["x"][0].T,
        "wpack": pack,
        "ada_pack": ada,
        "columns": np.concatenate([columns(v[n]) for n in order], axis=1),
        "const": const,
        "onehot": onehot,
        "rel_bias": v["rel_bias"],
        "positions_2": v["positions_2"],
        "router_w": np.pad(router_w.reshape(DC, P, G + G * E).transpose(1, 0, 2), ((0, 0), (0, 0), (0, P - G - G * E))),
        "router_b": np.concatenate([v["router_group_b_2"], v["router_expert_b_2"]], axis=1),
    }
    nc = _bacc.Bacc("TRN2", target_bir_lowering=False, num_devices=1)
    fed, aps = {}, {}
    for name, x in arrays.items():
        x = np.ascontiguousarray(x)
        fed[f"in_{name}"] = x
        aps[name] = nc.dram_tensor(f"in_{name}", x.shape, mybir.dt.from_np(x.dtype), kind="ExternalInput").ap()
    out = nc.dram_tensor("out_t", (D, SEQ), F32, kind="ExternalOutput").ap()
    build(nc, aps, out)
    r = _run(nc, [fed], core_ids=[0])
    return np.ascontiguousarray(r.results[0]["out_t"].T)[None]
```
